# Optimizing a Trainium2 kernel written in Bass

```python
import jax, jax.numpy as jnp
from jax import lax
import numpy as np

D_MODEL = 1024
BATCH = 1
SEQ = 256
DEPTH = 2

PLE_DIM = 256
R_HEADS = 4
R_DK = 64
R_DV = 128
R_CHUNK = 128
ROPE_BASE = 10000.0
M_HEADS = 4
M_DK = 64
M_DV = 128
M_CHUNK = 64
M_CONV = 4
AB_MIX = R_HEADS * R_DV + M_HEADS * M_DV
AB_SIZES = (R_HEADS * R_DK, R_HEADS * R_DK, R_HEADS * R_DV, R_HEADS * R_DV,
            M_HEADS * M_DK, M_HEADS * M_DK, M_HEADS * M_DV, M_HEADS * M_DV,
            M_HEADS, M_HEADS)
AB_COLS = sum(AB_SIZES)
N_HEADS = 16
N_KV_GROUPS = 2
HEAD_DIM = 64
CMP_BLOCK = 32
CMP_STRIDE = 16
CMP_HIDDEN = 256
SLC_BLOCK = 64
N_SELECT = 16
WINDOW = 512
Q_BLOCK = 128
NSA_SIZES = (N_HEADS * HEAD_DIM,) + (N_KV_GROUPS * HEAD_DIM,) * 6 + (N_HEADS * 3,)
NSA_COLS = sum(NSA_SIZES)
D_FF = 2816
FFN_CONV = 3

NEG = -1e30
BIG = 1e30
EPS = 1e-6


def rms_norm(x, g):
    xf = x.astype(jnp.float32)
    y = xf * lax.rsqrt(jnp.mean(xf * xf, axis=-1, keepdims=True) + EPS)
    return (y * g.astype(jnp.float32)).astype(x.dtype)

def split_cols(z, sizes):
    return jnp.split(z, np.cumsum(sizes)[:-1].tolist(), axis=-1)

def causal_dwconv(x, w, b):
    K = w.shape[0]
    T = x.shape[1]
    xp = jnp.pad(x, ((0, 0), (K - 1, 0), (0, 0)))
    y = b
    for j in range(K):
        y = y + xp[:, j:j + T] * w[j]
    return y

def to_chunks(x, L):
    B, T = x.shape[:2]
    x = x.reshape((B, T // L, L) + x.shape[2:])
    return jnp.moveaxis(x, (1, 2), (0, 3))

def from_chunks(y):
    y = jnp.moveaxis(y, (0, 3), (1, 2))
    return y.reshape((y.shape[0], y.shape[1] * y.shape[2]) + y.shape[3:])

def rotary(x, pos):
    half = x.shape[-1] // 2
    inv = ROPE_BASE ** (-jnp.arange(half, dtype=jnp.float32) / half)
    ang = pos[:, None] * inv[None, :]
    cos = jnp.cos(ang)[:, None, :]
    sin = jnp.sin(ang)[:, None, :]
    x1, x2 = x[..., :half], x[..., half:]
    return jnp.concatenate([x1 * cos - x2 * sin, x1 * sin + x2 * cos], axis=-1)

def retention_chunkwise(q, k, v):
    B, T, H, DK = q.shape
    DV = v.shape[-1]
    L = R_CHUNK
    log_g = jnp.log1p(-jnp.exp2(-5.0 - jnp.arange(H, dtype=jnp.float32)))
    idx = jnp.arange(L, dtype=jnp.float32)
    diff = idx[:, None] - idx[None, :]
    causal = diff >= 0
    dmask = jnp.where(causal, jnp.exp(jnp.where(causal, diff, 0.0)[None] * log_g[:, None, None]), 0.0)
    q_dec = jnp.exp((idx + 1.0)[None, :] * log_g[:, None])
    k_dec = jnp.exp((L - 1.0 - idx)[None, :] * log_g[:, None])
    c_dec = jnp.exp(L * log_g)

    def step(R, xs):
        qc, kc, vc = xs
        s = jnp.einsum('bhld,bhmd->bhlm', qc, kc) * dmask
        o = (jnp.einsum('bhlm,bhme->bhle', s, vc)
             + jnp.einsum('bhld,bhde->bhle', qc, R) * q_dec[..., None])
        R = c_dec[:, None, None] * R + jnp.einsum('bhmd,bhme->bhde', kc * k_dec[..., None], vc)
        return R, o

    R0 = jnp.zeros((B, H, DK, DV), jnp.float32)
    _, o = lax.scan(step, R0, (to_chunks(q, L), to_chunks(k, L), to_chunks(v, L)))
    return from_chunks(o)

def mlstm_chunkwise(q, k, v, ig, lf):
    B, T, H, DK = q.shape
    DV = v.shape[-1]
    L = M_CHUNK
    causal = jnp.tril(jnp.ones((L, L), dtype=bool))

    def step(carry, xs):
        C, n, m = carry
        qc, kc, vc, ic, fc = xs
        b = jnp.cumsum(fc, axis=-1)
        dlog = jnp.where(causal, b[..., :, None] - b[..., None, :] + ic[..., None, :], NEG)
        inter = b + m[..., None]
        m_t = jnp.maximum(inter, jnp.max(dlog, axis=-1))
        s = jnp.einsum('bhld,bhsd->bhls', qc, kc) * jnp.exp(dlog - m_t[..., None])
        w_inter = jnp.exp(inter - m_t)
        num = (jnp.einsum('bhls,bhse->bhle', s, vc)
               + w_inter[..., None] * jnp.einsum('bhld,bhde->bhle', qc, C))
        den = jnp.sum(s, axis=-1) + w_inter * jnp.einsum('bhld,bhd->bhl', qc, n)
        h = num / jnp.maximum(jnp.abs(den), jnp.exp(-m_t))[..., None]
        b_last = b[..., -1]
        wlog = b_last[..., None] - b + ic
        m_new = jnp.maximum(b_last + m, jnp.max(wlog, axis=-1))
        decay = jnp.exp(b_last + m - m_new)
        wk = kc * jnp.exp(wlog - m_new[..., None])[..., None]
        C = decay[..., None, None] * C + jnp.einsum('bhsd,bhse->bhde', wk, vc)
        n = decay[..., None] * n + jnp.sum(wk, axis=2)
        return (C, n, m_new), h

    init = (jnp.zeros((B, H, DK, DV), jnp.float32), jnp.zeros((B, H, DK), jnp.float32),
            jnp.zeros((B, H), jnp.float32))
    xs = (to_chunks(q, L), to_chunks(k, L), to_chunks(v, L), to_chunks(ig, L), to_chunks(lf, L))
    _, h = lax.scan(step, init, xs)
    return from_chunks(h)

def ab_mixer(h, w_in, conv_w, conv_b, ret_g, ig_b, fg_b, m_g, w_out):
    B, T, _ = h.shape
    z = (h @ w_in).astype(jnp.float32)
    rq, rk, rv, rg, mq, mk, mv, mo, mi, mf = split_cols(z, AB_SIZES)
    pos = jnp.arange(T, dtype=jnp.float32)
    rq = rotary(rq.reshape(B, T, R_HEADS, R_DK), pos)
    rk = rotary(rk.reshape(B, T, R_HEADS, R_DK), pos) * (R_DK ** -0.5)
    ret = retention_chunkwise(rq, rk, rv.reshape(B, T, R_HEADS, R_DV))
    ret = rms_norm(ret, ret_g.reshape(R_HEADS, R_DV)).reshape(B, T, -1) * jax.nn.silu(rg)
    mqk = jax.nn.silu(causal_dwconv(jnp.concatenate([mq, mk], axis=-1), conv_w, conv_b))
    mq, mk = jnp.split(mqk, 2, axis=-1)
    hm = mlstm_chunkwise(mq.reshape(B, T, M_HEADS, M_DK) * (M_DK ** -0.5),
                         mk.reshape(B, T, M_HEADS, M_DK),
                         mv.reshape(B, T, M_HEADS, M_DV),
                         mi + ig_b,
                         jax.nn.log_sigmoid(mf + fg_b))
    mlstm = jax.nn.sigmoid(mo) * rms_norm(hm, m_g.reshape(M_HEADS, M_DV)).reshape(B, T, -1)
    y = jnp.concatenate([ret, mlstm], axis=-1) @ w_out
    return y.astype(h.dtype)

def nsa_mixer(h, w_in, q_g, k_g, pos_k, pos_v, w1k, w2k, w1v, w2v, gate_b, w_out):
    B, T, _ = h.shape
    G, HG, HD = N_KV_GROUPS, N_HEADS // N_KV_GROUPS, HEAD_DIM
    z = (h @ w_in).astype(jnp.float32)
    q, kc, vc, ks, vs, kw, vw, gt = split_cols(z, NSA_SIZES)
    q = rms_norm(q.reshape(B, T, G, HG, HD), q_g).transpose(0, 2, 3, 1, 4)

    def kv(t):
        return t.reshape(B, T, G, HD)

    nc = (T - CMP_BLOCK) // CMP_STRIDE + 1
    c_start = jnp.arange(nc) * CMP_STRIDE
    cidx = c_start[:, None] + jnp.arange(CMP_BLOCK)[None, :]

    def compress(t, pos, w1, w2):
        blk = kv(t)[:, cidx] + pos[:, None, :]
        blk = blk.transpose(0, 3, 1, 2, 4).reshape(B, G, nc, CMP_BLOCK * HD)
        return jax.nn.gelu(blk @ w1) @ w2

    kc = rms_norm(compress(kc, pos_k, w1k, w2k), k_g[0])
    vc = compress(vc, pos_v, w1v, w2v)
    ks = rms_norm(kv(ks), k_g[1]).transpose(0, 2, 1, 3)
    vs = kv(vs).transpose(0, 2, 1, 3)
    kw = rms_norm(kv(kw), k_g[2]).transpose(0, 2, 1, 3)
    vw = kv(vw).transpose(0, 2, 1, 3)
    ns = T // SLC_BLOCK
    n_sel = min(N_SELECT, ns)
    ks_blk = ks.reshape(B, G, ns, SLC_BLOCK, HD)
    vs_blk = vs.reshape(B, G, ns, SLC_BLOCK, HD)
    pad = ((0, 0), (0, 0), (WINDOW, 0), (0, 0))
    kw_pad = jnp.pad(kw, pad)
    vw_pad = jnp.pad(vw, pad)
    gates = jax.nn.sigmoid(gt.reshape(B, T, G, HG, 3) + gate_b.reshape(G, HG, 3)).transpose(0, 2, 3, 1, 4)
    cmp_end = c_start + CMP_BLOCK - 1
    sj = jnp.arange(ns)
    overlap = ((c_start[:, None] < (sj[None, :] + 1) * SLC_BLOCK)
               & (c_start[:, None] + CMP_BLOCK > sj[None, :] * SLC_BLOCK)).astype(jnp.float32)
    scale = HD ** -0.5
    bi = jnp.arange(B)[:, None, None, None]
    gi = jnp.arange(G)[None, :, None, None]

    def query_block(qb):
        t0 = qb * Q_BLOCK
        tpos = t0 + jnp.arange(Q_BLOCK)
        qq = lax.dynamic_slice_in_dim(q, t0, Q_BLOCK, axis=3)
        s = jnp.einsum('bghqd,bgnd->bghqn', qq, kc) * scale
        cvalid = cmp_end[None, :] <= tpos[:, None]
        p_c = jnp.where(cvalid, jax.nn.softmax(jnp.where(cvalid, s, NEG), axis=-1), 0.0)
        o_cmp = jnp.einsum('bghqn,bgnd->bghqd', p_c, vc)
        imp = jnp.einsum('bghqn,ns->bgqs', p_c, overlap)
        cur = tpos // SLC_BLOCK
        forced = (sj[None, :] == 0) | (sj[None, :] == cur[:, None]) | (sj[None, :] == cur[:, None] - 1)
        bvalid = sj[None, :] <= cur[:, None]
        score = jnp.where(forced, BIG, jnp.where(bvalid, imp, NEG))
        _, sel = lax.top_k(score, n_sel)
        kg = ks_blk[bi, gi, sel]
        vg = vs_blk[bi, gi, sel]
        kpos = sel[..., None] * SLC_BLOCK + jnp.arange(SLC_BLOCK)
        smask = (kpos <= tpos[:, None, None])[:, :, None]
        s = jnp.einsum('bghqd,bgqnkd->bghqnk', qq, kg) * scale
        s = jnp.where(smask, s, NEG).reshape(B, G, HG, Q_BLOCK, n_sel * SLC_BLOCK)
        p_s = jax.nn.softmax(s, axis=-1).reshape(B, G, HG, Q_BLOCK, n_sel, SLC_BLOCK)
        o_slc = jnp.einsum('bghqnk,bgqnkd->bghqd', p_s, vg)
        kwb = lax.dynamic_slice_in_dim(kw_pad, t0, WINDOW + Q_BLOCK, axis=2)
        vwb = lax.dynamic_slice_in_dim(vw_pad, t0, WINDOW + Q_BLOCK, axis=2)
        wpos = t0 - WINDOW + jnp.arange(WINDOW + Q_BLOCK)
        wmask = ((wpos[None, :] <= tpos[:, None]) & (wpos[None, :] > tpos[:, None] - WINDOW)
                 & (wpos[None, :] >= 0))
        s = jnp.einsum('bghqd,bgkd->bghqk', qq, kwb) * scale
        p_w = jax.nn.softmax(jnp.where(wmask, s, NEG), axis=-1)
        o_win = jnp.einsum('bghqk,bgkd->bghqd', p_w, vwb)
        g = lax.dynamic_slice_in_dim(gates, t0, Q_BLOCK, axis=3)
        return g[..., 0:1] * o_cmp + g[..., 1:2] * o_slc + g[..., 2:3] * o_win

    o = lax.map(query_block, jnp.arange(T // Q_BLOCK))
    o = o.transpose(1, 0, 4, 2, 3, 5).reshape(B, T, N_HEADS * HD)
    return (o @ w_out).astype(h.dtype)

def conv_ffn(h, w_up, conv_w, conv_b, w_down):
    a, b = jnp.split(h @ w_up, 2, axis=-1)
    a = causal_dwconv(a, conv_w, conv_b)
    return (jax.nn.gelu(a) * b) @ w_down

def first_inputs(seed: int = 0) -> dict:
    key = jax.random.key(seed)
    keys = iter(jax.random.split(key, 64))
    f32 = jnp.float32
    NE = (DEPTH + 1) // 2
    NO = DEPTH // 2

    def nrm(shape, scale):
        return scale * jax.random.normal(next(keys), shape, f32)

    def gain(shape):
        return 1.0 + nrm(shape, 0.02)

    return {
        'x': nrm((BATCH, SEQ, D_MODEL), 1.0),
        'p': nrm((DEPTH, BATCH, SEQ, PLE_DIM), 1.0),
        'ab_norm_g': gain((NE, D_MODEL)),
        'ab_w_in': nrm((NE, D_MODEL, AB_COLS), D_MODEL ** -0.5),
        'ab_conv_w': nrm((NE, M_CONV, 2 * M_HEADS * M_DK), M_CONV ** -0.5),
        'ab_conv_b': nrm((NE, 2 * M_HEADS * M_DK), 0.02),
        'ab_ret_norm_g': gain((NE, R_HEADS * R_DV)),
        'ab_ig_b': nrm((NE, M_HEADS), 0.1),
        'ab_fg_b': jnp.linspace(3.0, 6.0, M_HEADS, dtype=f32)[None, :] + nrm((NE, M_HEADS), 0.1),
        'ab_m_norm_g': gain((NE, M_HEADS * M_DV)),
        'ab_w_out': nrm((NE, AB_MIX, D_MODEL), AB_MIX ** -0.5),
        'nsa_norm_g': gain((NO, D_MODEL)),
        'nsa_w_in': nrm((NO, D_MODEL, NSA_COLS), D_MODEL ** -0.5),
        'nsa_q_norm_g': gain((NO, HEAD_DIM)),
        'nsa_k_norm_g': gain((NO, 3, HEAD_DIM)),
        'nsa_cmp_pos_k': nrm((NO, CMP_BLOCK, HEAD_DIM), 0.1),
        'nsa_cmp_pos_v': nrm((NO, CMP_BLOCK, HEAD_DIM), 0.1),
        'nsa_cmp_w1k': nrm((NO, CMP_BLOCK * HEAD_DIM, CMP_HIDDEN), (CMP_BLOCK * HEAD_DIM) ** -0.5),
        'nsa_cmp_w2k': nrm((NO, CMP_HIDDEN, HEAD_DIM), CMP_HIDDEN ** -0.5),
        'nsa_cmp_w1v': nrm((NO, CMP_BLOCK * HEAD_DIM, CMP_HIDDEN), (CMP_BLOCK * HEAD_DIM) ** -0.5),
        'nsa_cmp_w2v': nrm((NO, CMP_HIDDEN, HEAD_DIM), CMP_HIDDEN ** -0.5),
        'nsa_gate_b': nrm((NO, N_HEADS * 3), 0.1),
        'nsa_w_out': nrm((NO, N_HEADS * HEAD_DIM, D_MODEL), (N_HEADS * HEAD_DIM) ** -0.5),
        'ffn_norm_g': gain((DEPTH, D_MODEL)),
        'ffn_w_up': nrm((DEPTH, D_MODEL, 2 * D_FF), D_MODEL ** -0.5),
        'ffn_conv_w': nrm((DEPTH, FFN_CONV, D_FF), FFN_CONV ** -0.5),
        'ffn_conv_b': nrm((DEPTH, D_FF), 0.02),
        'ffn_w_down': nrm((DEPTH, D_FF, D_MODEL), D_FF ** -0.5),
        'ple_w': nrm((DEPTH, PLE_DIM, D_MODEL), PLE_DIM ** -0.5),
        'ple_norm_g': gain((DEPTH, D_MODEL)),
        'ple_gate_norm_g': gain((DEPTH, D_MODEL)),
        'ple_w_gate': nrm((DEPTH, D_MODEL, D_MODEL), D_MODEL ** -0.5),
    }

def first_block(x, p, ab_norm_g, ab_w_in, ab_conv_w, ab_conv_b, ab_ret_norm_g, ab_ig_b, ab_fg_b,
              ab_m_norm_g, ab_w_out, nsa_norm_g, nsa_w_in, nsa_q_norm_g, nsa_k_norm_g,
              nsa_cmp_pos_k, nsa_cmp_pos_v, nsa_cmp_w1k, nsa_cmp_w2k, nsa_cmp_w1v, nsa_cmp_w2v,
              nsa_gate_b, nsa_w_out, ffn_norm_g, ffn_w_up, ffn_conv_w, ffn_conv_b, ffn_w_down,
              ple_w, ple_norm_g, ple_gate_norm_g, ple_w_gate):
    h = x
    for i in range(DEPTH):
        j = i // 2
        if i % 2 == 0:
            h = h + ab_mixer(rms_norm(h, ab_norm_g[j]), ab_w_in[j], ab_conv_w[j], ab_conv_b[j],
                             ab_ret_norm_g[j], ab_ig_b[j], ab_fg_b[j], ab_m_norm_g[j], ab_w_out[j])
        else:
            h = h + nsa_mixer(rms_norm(h, nsa_norm_g[j]), nsa_w_in[j], nsa_q_norm_g[j], nsa_k_norm_g[j],
                              nsa_cmp_pos_k[j], nsa_cmp_pos_v[j], nsa_cmp_w1k[j], nsa_cmp_w2k[j],
                              nsa_cmp_w1v[j], nsa_cmp_w2v[j], nsa_gate_b[j], nsa_w_out[j])
        h = h + conv_ffn(rms_norm(h, ffn_norm_g[i]), ffn_w_up[i], ffn_conv_w[i], ffn_conv_b[i], ffn_w_down[i])
        e = rms_norm(p[i] @ ple_w[i], ple_norm_g[i])
        gate = jax.nn.sigmoid(rms_norm(h, ple_gate_norm_g[i]) @ ple_w_gate[i])
        h = h + gate * e
    return h


GRID_W = 64
CTX_LEN = 256
N_EVEN = (DEPTH + 1) // 2
N_ODD = DEPTH // 2

FOURIER_GROUPS = 4
FOURIER_GROUP_DIM = 128
FOURIER_WIDTH = FOURIER_GROUPS * FOURIER_GROUP_DIM
CONV_GROUPS = 4
CONV_WIDTH = 512
CONV_K = 3
EVEN_IN = FOURIER_WIDTH + 3 * CONV_WIDTH
EVEN_OUT = FOURIER_WIDTH + CONV_WIDTH

N_KV_HEADS = 4
GQA_GROUP = N_HEADS // N_KV_HEADS
Q_DIM = N_HEADS * HEAD_DIM
KV_DIM = N_KV_HEADS * HEAD_DIM
QKV_OUT = Q_DIM + 2 * KV_DIM
WINDOW_2 = 128
ATT_BLOCK = 128
ROPE_PAIRS_PER_AXIS = HEAD_DIM // 4
NEG_INF = -1e30

N_GROUPS = 4
EXPERTS_PER_GROUP = 8
N_EXPERTS = N_GROUPS * EXPERTS_PER_GROUP
TOP_K = 2
D_FF_EXPERT = 512
MOE_BLOCK = 128


def rms_norm_2(x, g):
    xf = x.astype(jnp.float32)
    y = xf * lax.rsqrt(jnp.mean(xf * xf, axis=-1, keepdims=True) + EPS)
    return (y * g.astype(jnp.float32)).astype(x.dtype)

def modulate(h, shift, scale):
    return h * (1 + scale) + shift

def fourier_mix(a):
    b_, l_, _ = a.shape
    a4 = a.reshape(b_, l_, FOURIER_GROUPS, FOURIER_GROUP_DIM).astype(jnp.float32)
    f = jnp.fft.fftn(a4, axes=(1, 3), norm="ortho").real
    return f.reshape(b_, l_, FOURIER_WIDTH).astype(a.dtype)

def short_conv_mix(b_gate, c_gate, h, w):
    u = c_gate * h
    up = jnp.pad(u, ((0, 0), (1, 1), (0, 0)))
    y = w[0] * up[:, :-2] + w[1] * up[:, 1:-1] + w[2] * up[:, 2:]
    return b_gate * y

def even_mixer(h, w_in, conv_w, w_out):
    p = h @ w_in
    a, b_gate, c_gate, hv = jnp.split(
        p, [FOURIER_WIDTH, FOURIER_WIDTH + CONV_WIDTH, FOURIER_WIDTH + 2 * CONV_WIDTH], axis=-1)
    y = jnp.concatenate([fourier_mix(a), short_conv_mix(b_gate, c_gate, hv, conv_w)], axis=-1)
    return y @ w_out

def axial_rope_tables(n_tok):
    t = jnp.arange(n_tok, dtype=jnp.int32)
    pos = jnp.stack([t // GRID_W, t % GRID_W], axis=-1).astype(jnp.float32)
    freqs = ROPE_BASE ** (-jnp.arange(ROPE_PAIRS_PER_AXIS, dtype=jnp.float32) / ROPE_PAIRS_PER_AXIS)
    ang = pos[:, :, None] * freqs
    return jnp.cos(ang), jnp.sin(ang)

def apply_axial_rope(x, cos, sin):
    b_, l_, h_, _ = x.shape
    xf = x.astype(jnp.float32).reshape(b_, l_, h_, 2, 2, ROPE_PAIRS_PER_AXIS)
    x1, x2 = xf[..., 0, :], xf[..., 1, :]
    cs, sn = cos[None, :, None], sin[None, :, None]
    out = jnp.stack([x1 * cs - x2 * sn, x1 * sn + x2 * cs], axis=-2)
    return out.reshape(x.shape).astype(x.dtype)

def project_q(h, w_qkv, q_g):
    b_, l_, _ = h.shape
    q = (h @ w_qkv[:, :Q_DIM]).reshape(b_, l_, N_HEADS, HEAD_DIM)
    return rms_norm_2(q, q_g)

def project_kv(h, w_qkv, k_g):
    b_, l_, _ = h.shape
    kv = h @ w_qkv[:, Q_DIM:]
    k = rms_norm_2(kv[..., :KV_DIM].reshape(b_, l_, N_KV_HEADS, HEAD_DIM), k_g)
    v = kv[..., KV_DIM:].reshape(b_, l_, N_KV_HEADS, HEAD_DIM)
    return k, v

def window_attention(hl, hc, w_qkv, q_g, k_g, sink, w_o, need_ctx_out):
    B, L, _ = hl.shape
    Lc = hc.shape[1]
    scale = HEAD_DIM ** -0.5
    cos, sin = axial_rope_tables(L)
    ql = apply_axial_rope(project_q(hl, w_qkv, q_g), cos, sin) * scale
    kl, vl = project_kv(hl, w_qkv, k_g)
    kl = apply_axial_rope(kl, cos, sin)
    kc, vc = project_kv(hc, w_qkv, k_g)
    sink_g = sink.reshape(N_KV_HEADS, GQA_GROUP).astype(jnp.float32)

    n_blocks = L // ATT_BLOCK
    qg = ql.reshape(B, L, N_KV_HEADS, GQA_GROUP, HEAD_DIM)
    pad = ((0, 0), (ATT_BLOCK, ATT_BLOCK), (0, 0), (0, 0))
    kp, vp = jnp.pad(kl, pad), jnp.pad(vl, pad)
    qi = jnp.arange(ATT_BLOCK)
    kj = jnp.arange(3 * ATT_BLOCK)
    band = jnp.abs(kj[None, :] - ATT_BLOCK - qi[:, None]) <= WINDOW_2

    def block(bidx):
        start = bidx * ATT_BLOCK
        qb = lax.dynamic_slice_in_dim(qg, start, ATT_BLOCK, axis=1)
        kb = lax.dynamic_slice_in_dim(kp, start, 3 * ATT_BLOCK, axis=1)
        vb = lax.dynamic_slice_in_dim(vp, start, 3 * ATT_BLOCK, axis=1)
        kpos = start - ATT_BLOCK + kj
        mask = band & ((kpos >= 0) & (kpos < L))[None, :]
        s_loc = jnp.einsum("bqkgd,bskd->bkgqs", qb, kb, preferred_element_type=jnp.float32)
        s_loc = jnp.where(mask, s_loc, NEG_INF)
        s_ctx = jnp.einsum("bqkgd,bskd->bkgqs", qb, kc, preferred_element_type=jnp.float32)
        s_sink = jnp.broadcast_to(sink_g[None, :, :, None, None], s_loc.shape[:-1] + (1,))
        p = jax.nn.softmax(jnp.concatenate([s_loc, s_ctx, s_sink], axis=-1), axis=-1)
        p_loc = p[..., :3 * ATT_BLOCK].astype(vb.dtype)
        p_ctx = p[..., 3 * ATT_BLOCK:3 * ATT_BLOCK + Lc].astype(vc.dtype)
        return (jnp.einsum("bkgqs,bskd->bqkgd", p_loc, vb)
                + jnp.einsum("bkgqs,bskd->bqkgd", p_ctx, vc))

    ob = lax.map(block, jnp.arange(n_blocks))
    yl = jnp.moveaxis(ob, 0, 1).reshape(B, L, Q_DIM) @ w_o

    if not need_ctx_out:
        return yl, None
    qc = project_q(hc, w_qkv, q_g).reshape(B, Lc, N_KV_HEADS, GQA_GROUP, HEAD_DIM) * scale
    s = jnp.einsum("bqkgd,bskd->bkgqs", qc, kc, preferred_element_type=jnp.float32)
    s_sink = jnp.broadcast_to(sink_g[None, :, :, None, None], s.shape[:-1] + (1,))
    p = jax.nn.softmax(jnp.concatenate([s, s_sink], axis=-1), axis=-1)[..., :Lc].astype(vc.dtype)
    yc = jnp.einsum("bkgqs,bskd->bqkgd", p, vc).reshape(B, Lc, Q_DIM) @ w_o
    return yl, yc

def hier_moe(xf, w_rg, b_rg, w_re, b_re, w1, w3, w2):
    T, D = xf.shape
    xr = xf.astype(jnp.float32)
    g_logits = xr @ w_rg.astype(jnp.float32) + b_rg.astype(jnp.float32)
    g_prob = jax.nn.softmax(g_logits, axis=-1)
    g_val, g_idx = lax.top_k(g_prob, 1)
    e_logits = (xr @ w_re.astype(jnp.float32) + b_re.astype(jnp.float32)).reshape(
        T, N_GROUPS, EXPERTS_PER_GROUP)
    e_in = jnp.take_along_axis(e_logits, g_idx[:, :, None], axis=1)[:, 0]
    top_v, top_i = lax.top_k(e_in, TOP_K)
    gate = jax.nn.softmax(top_v, axis=-1) * g_val
    expert = g_idx * EXPERTS_PER_GROUP + top_i

    A = T * TOP_K
    e_flat = expert.reshape(A)
    t_flat = jnp.repeat(jnp.arange(T, dtype=jnp.int32), TOP_K)
    g_flat = gate.reshape(A)
    counts = jnp.bincount(e_flat, length=N_EXPERTS)
    padded = (counts + MOE_BLOCK - 1) // MOE_BLOCK * MOE_BLOCK
    pad_end = jnp.cumsum(padded)
    pad_start = pad_end - padded
    raw_start = jnp.cumsum(counts) - counts
    order = jnp.argsort(e_flat)
    e_s = e_flat[order]
    dest = pad_start[e_s] + jnp.arange(A) - raw_start[e_s]
    n_blocks = -(-A // MOE_BLOCK) + N_EXPERTS
    R = n_blocks * MOE_BLOCK
    row_tok = jnp.full((R,), T, jnp.int32).at[dest].set(t_flat[order])
    row_gate = jnp.zeros((R,), jnp.float32).at[dest].set(g_flat[order])
    block_exp = jnp.clip(jnp.searchsorted(pad_end, jnp.arange(n_blocks) * MOE_BLOCK, side="right"),
                         0, N_EXPERTS - 1)

    x_pad = jnp.concatenate([xf, jnp.zeros((1, D), xf.dtype)], axis=0)
    xb = x_pad[row_tok].reshape(n_blocks, MOE_BLOCK, D)

    def expert_block(args):
        xblk, e = args
        return (jax.nn.silu(xblk @ w1[e]) * (xblk @ w3[e])) @ w2[e]

    yb = lax.map(expert_block, (xb, block_exp)).reshape(R, D)
    out = jnp.zeros((T + 1, D), yb.dtype).at[row_tok].add(yb * row_gate[:, None].astype(yb.dtype))
    return out[:T]

def second_inputs(seed: int = 0) -> dict:
    key = jax.random.key(seed)
    ks = jax.random.split(key, 24)
    D = D_MODEL

    def nrm(k, shape, s):
        return jax.random.normal(k, shape, jnp.float32) * s

    return {
        "x": nrm(ks[0], (BATCH, SEQ, D), 1.0),
        "c": nrm(ks[1], (BATCH, D), 1.0),
        "ctx": nrm(ks[2], (BATCH, CTX_LEN, D), 1.0),
        "c_ctx": nrm(ks[3], (D,), 1.0),
        "w_mod": nrm(ks[4], (DEPTH, D, 6 * D), 0.5 * D ** -0.5),
        "b_mod": nrm(ks[5], (DEPTH, 6 * D), 0.01),
        "norm_mix_g": 1.0 + nrm(ks[6], (DEPTH, D), 0.02),
        "norm_ffn_g": 1.0 + nrm(ks[7], (DEPTH, D), 0.02),
        "w_in_even": nrm(ks[8], (N_EVEN, D, EVEN_IN), D ** -0.5),
        "conv_w": nrm(ks[9], (N_EVEN, CONV_K, CONV_WIDTH), CONV_K ** -0.5),
        "w_out_even": nrm(ks[10], (N_EVEN, EVEN_OUT, D), EVEN_OUT ** -0.5),
        "w_qkv": nrm(ks[11], (N_ODD, D, QKV_OUT), D ** -0.5),
        "q_norm_g": 1.0 + nrm(ks[12], (N_ODD, HEAD_DIM), 0.02),
        "k_norm_g": 1.0 + nrm(ks[13], (N_ODD, HEAD_DIM), 0.02),
        "sink_logit": nrm(ks[14], (N_ODD, N_HEADS), 1.0),
        "w_o": nrm(ks[15], (N_ODD, Q_DIM, D), Q_DIM ** -0.5),
        "w_router_g": nrm(ks[16], (DEPTH, D, N_GROUPS), D ** -0.5),
        "b_router_g": nrm(ks[17], (DEPTH, N_GROUPS), 0.01),
        "w_router_e": nrm(ks[18], (DEPTH, D, N_EXPERTS), D ** -0.5),
        "b_router_e": nrm(ks[19], (DEPTH, N_EXPERTS), 0.01),
        "w1": nrm(ks[20], (DEPTH, N_EXPERTS, D, D_FF_EXPERT), D ** -0.5),
        "w3": nrm(ks[21], (DEPTH, N_EXPERTS, D, D_FF_EXPERT), D ** -0.5),
        "w2": nrm(ks[22], (DEPTH, N_EXPERTS, D_FF_EXPERT, D), D_FF_EXPERT ** -0.5),
    }

def second_block(x, c, ctx, c_ctx, w_mod, b_mod, norm_mix_g, norm_ffn_g, w_in_even, conv_w, w_out_even,
              w_qkv, q_norm_g, k_norm_g, sink_logit, w_o, w_router_g, b_router_g, w_router_e, b_router_e,
              w1, w3, w2):
    B, L, D = x.shape
    Lc = ctx.shape[1]
    xl, xc = x, ctx
    for layer in range(DEPTH):
        last = layer == DEPTH - 1
        is_even = layer % 2 == 0
        j = layer // 2
        mod_l = (jax.nn.silu(c) @ w_mod[layer] + b_mod[layer])[:, None, :]
        mod_c = jax.nn.silu(c_ctx) @ w_mod[layer] + b_mod[layer]
        sh1_l, sc1_l, g1_l, sh2_l, sc2_l, g2_l = jnp.split(mod_l, 6, axis=-1)
        sh1_c, sc1_c, g1_c, sh2_c, sc2_c, g2_c = jnp.split(mod_c, 6, axis=-1)

        hl = modulate(rms_norm_2(xl, norm_mix_g[layer]), sh1_l, sc1_l)
        if is_even:
            yl = even_mixer(hl, w_in_even[j], conv_w[j], w_out_even[j])
            yc = None
            if not last:
                hc = modulate(rms_norm_2(xc, norm_mix_g[layer]), sh1_c, sc1_c)
                yc = even_mixer(hc, w_in_even[j], conv_w[j], w_out_even[j])
        else:
            hc = modulate(rms_norm_2(xc, norm_mix_g[layer]), sh1_c, sc1_c)
            yl, yc = window_attention(hl, hc, w_qkv[j], q_norm_g[j], k_norm_g[j], sink_logit[j], w_o[j],
                                      not last)
        xl = xl + g1_l * yl

        hl2 = modulate(rms_norm_2(xl, norm_ffn_g[layer]), sh2_l, sc2_l).reshape(B * L, D)
        moe_args = (w_router_g[layer], b_router_g[layer], w_router_e[layer], b_router_e[layer],
                    w1[layer], w3[layer], w2[layer])
        if last:
            xl = xl + g2_l * hier_moe(hl2, *moe_args).reshape(B, L, D)
        else:
            xc = xc + g1_c * yc
            hc2 = modulate(rms_norm_2(xc, norm_ffn_g[layer]), sh2_c, sc2_c).reshape(B * Lc, D)
            f = hier_moe(jnp.concatenate([hl2, hc2], axis=0), *moe_args)
            xl = xl + g2_l * f[:B * L].reshape(B, L, D)
            xc = xc + g2_c * f[B * L:].reshape(B, Lc, D)
    return xl


def setup_inputs(seed=0):
    out = dict(first_inputs(seed))
    for name, value in second_inputs(seed + 1).items():
        if name != "x":
            out[name + "_2"] = value
    return out


def reference(
    x, p, ab_norm_g, ab_w_in, ab_conv_w, ab_conv_b, ab_ret_norm_g, ab_ig_b, ab_fg_b,
    ab_m_norm_g, ab_w_out, nsa_norm_g, nsa_w_in, nsa_q_norm_g, nsa_k_norm_g, nsa_cmp_pos_k,
    nsa_cmp_pos_v, nsa_cmp_w1k, nsa_cmp_w2k, nsa_cmp_w1v, nsa_cmp_w2v, nsa_gate_b, nsa_w_out,
    ffn_norm_g, ffn_w_up, ffn_conv_w, ffn_conv_b, ffn_w_down, ple_w, ple_norm_g,
    ple_gate_norm_g, ple_w_gate, c_2, ctx_2, c_ctx_2, w_mod_2, b_mod_2, norm_mix_g_2,
    norm_ffn_g_2, w_in_even_2, conv_w_2, w_out_even_2, w_qkv_2, q_norm_g_2, k_norm_g_2,
    sink_logit_2, w_o_2, w_router_g_2, b_router_g_2, w_router_e_2, b_router_e_2, w1_2, w3_2,
    w2_2,
):
    x = first_block(
        x, p, ab_norm_g, ab_w_in, ab_conv_w, ab_conv_b, ab_ret_norm_g, ab_ig_b, ab_fg_b,
        ab_m_norm_g, ab_w_out, nsa_norm_g, nsa_w_in, nsa_q_norm_g, nsa_k_norm_g, nsa_cmp_pos_k,
        nsa_cmp_pos_v, nsa_cmp_w1k, nsa_cmp_w2k, nsa_cmp_w1v, nsa_cmp_w2v, nsa_gate_b,
        nsa_w_out, ffn_norm_g, ffn_w_up, ffn_conv_w, ffn_conv_b, ffn_w_down, ple_w, ple_norm_g,
        ple_gate_norm_g, ple_w_gate,
    )
    return second_block(
        x, c_2, ctx_2, c_ctx_2, w_mod_2, b_mod_2, norm_mix_g_2, norm_ffn_g_2, w_in_even_2,
        conv_w_2, w_out_even_2, w_qkv_2, q_norm_g_2, k_norm_g_2, sink_logit_2, w_o_2,
        w_router_g_2, b_router_g_2, w_router_e_2, b_router_e_2, w1_2, w3_2, w2_2,
    )


_drawn_inputs = setup_inputs


def setup_inputs(seed=0):
    import zlib

    import numpy as np

    out = dict(_drawn_inputs(seed))
    spreads = {}
    factors = {'ab_conv_b': 4.736,
     'ab_ret_norm_g': 5.344,
     'ab_ig_b': 8.0,
     'ab_m_norm_g': 5.768,
     'nsa_norm_g': 7.436,
     'nsa_q_norm_g': 8.0,
     'nsa_k_norm_g': 8.0,
     'nsa_cmp_pos_k': 8.0,
     'nsa_gate_b': 6.603,
     'ffn_norm_g': 2.882,
     'ffn_conv_b': 4.158,
     'ple_norm_g': 4.304,
     'ple_gate_norm_g': 8.0,
     'ctx_2': 13.323,
     'b_mod_2': 5.339,
     'norm_mix_g_2': 7.407,
     'norm_ffn_g_2': 36.559,
     'q_norm_g_2': 64.0,
     'k_norm_g_2': 64.0,
     'sink_logit_2': 8.0,
     'b_router_g_2': 57.612,
     'b_router_e_2': 64.0,
     'nsa_cmp_pos_v': 5.985,
     'c_ctx_2': 2.701}
    for name, (base, spread) in spreads.items():
        noise = np.random.default_rng([zlib.crc32(name.encode()), seed]).standard_normal(out[name].shape)
        drawn = base * np.exp(spread * noise) if base else spread * noise
        out[name] = __import__('jax').numpy.asarray(drawn.astype(out[name].dtype))
    for name, factor in factors.items():
        out[name] = (out[name] * factor).astype(out[name].dtype)
    return out
```

```python
from contextlib import ExitStack

import numpy as np
import concourse.bass as bass
from concourse import mybir

F32 = mybir.dt.float32
I32 = mybir.dt.int32
U32 = mybir.dt.uint32
ALU = mybir.AluOpType
ACT = mybir.ActivationFunctionType
AXX = mybir.AxisListType.X

P = 128
D = 1024
T = 256
KC = D // P
EPS = 1e-6
NEG = -1e30
FF = 2816
FC = FF // P
NC_CMP = (T - 32) // 16 + 1
NE = 32
FE = 512
CAP = 64
RING = 5


def constant_table():
    at, cols = {}, []

    def add(name, a):
        a = np.asarray(a, np.float64)
        full = np.zeros((P, a.shape[1]))
        full[:a.shape[0]] = a
        at[name] = (sum(c.shape[1] for c in cols), a.shape[1])
        cols.append(full)

    i = np.arange(P)
    add("ident", np.eye(P))
    add("ones", np.ones((P, T)))
    diff = i[None, :] - i[:, None]
    for h in range(4):
        lg = np.log1p(-(2.0 ** (-5.0 - h)))
        diag = np.where(diff >= 0, np.exp(np.where(diff >= 0, diff, 0) * lg), 0.0)
        add(f"decay{h}", np.concatenate([diag, np.exp((diff + P) * lg), diag], 1) / 8)
    c = (diff >= 0) / 8.0
    add("causal_mul", np.concatenate([c, np.full((P, P), 0.125), c], 1))
    add("causal_add", np.concatenate([np.zeros((P, P)), np.where(i[None, :] <= i[:, None], 0.0, NEG)], 1))
    inv = 10000.0 ** (-np.arange(32) / 32.0)
    inv16 = 10000.0 ** (-np.arange(16) / 16.0)
    t = np.arange(T)
    ang = (t[:, None].astype(np.float32) * inv.astype(np.float32)[None, :]).astype(np.float64)
    ax = np.stack([(t // 64)[:, None] * inv16, (t % 64)[:, None] * inv16], 1).reshape(T, 32)
    for j in range(2):
        r = slice(j * P, (j + 1) * P)
        add(f"cos{j}", np.cos(ang[r]))
        add(f"sin{j}", np.sin(ang[r]))
        add(f"axcos{j}", np.cos(ax[r]))
        add(f"axsin{j}", np.sin(ax[r]))
        valid = (16 * np.arange(NC_CMP) + 31)[None, :] <= t[r][:, None]
        add(f"cmp_add{j}", np.where(valid, 0.0, NEG))
        add(f"cmp_mul{j}", valid)
        band = np.where(np.abs(t[None, :] - t[r][:, None]) <= P, 0.0, NEG)
        add(f"band{j}", np.concatenate([band, np.zeros((P, T))], 1))
        w = 2 * np.pi * np.outer(t[r], t) / T
        add(f"dft{j}", np.concatenate([np.cos(w), np.sin(w)], 1) / np.sqrt(T))
    w = 2 * np.pi * np.outer(i, i) / P
    add("dft_cos", np.cos(w) / np.sqrt(P))
    add("dft_nsin", -np.sin(w) / np.sqrt(P))
    r = np.arange(8 * NC_CMP)
    add("cmp_rep", (np.arange(NC_CMP)[:, None] == r[None, :] % NC_CMP))
    add("cmp_own", (r[:, None] // NC_CMP == np.arange(8)[None, :]))
    add("before", (i[:, None] < i[None, :]))
    add("iota", np.broadcast_to(np.arange(32), (P, 32)))
    sel = np.zeros((P, 2))
    sel[np.arange(4) * 32, 0] = sel[np.arange(4) * 32 + 1, 1] = 1
    add("sel2", sel)
    for h in range(4):
        s = np.zeros((4, P))
        s[h] = 1
        add(f"head{h}", s)
    return np.concatenate(cols, 1).astype(np.float32), at


CONST, CONST_AT = constant_table()


def pk(v):
    return v.reshape(P, -1)


def kp(v):
    return v.reshape(-1, P).T


def two(v):
    return np.concatenate([v, v]).reshape(P, 1)


def column(v):
    return v.reshape(-1, 1)


def param_table(x):
    at, cols, o = {}, [], 0
    items = [("g_ab", pk(x["ab_norm_g"][0])), ("g_nsa", pk(x["nsa_norm_g"][0]))]
    items += [(f"g_ffn{i}", pk(x["ffn_norm_g"][i])) for i in range(2)]
    items += [(f"g_plg{i}", pk(x["ple_gate_norm_g"][i])) for i in range(2)]
    items += [("g_ret", kp(x["ab_ret_norm_g"][0])), ("g_m", kp(x["ab_m_norm_g"][0])),
              ("ab_cw", np.concatenate([kp(x["ab_conv_w"][0, j]) for j in range(4)], 1)),
              ("ab_cb", kp(x["ab_conv_b"][0])), ("ig_b", column(x["ab_ig_b"][0])), ("fg_b", column(x["ab_fg_b"][0]))]
    for i in range(2):
        items += [(f"f_cw{i}{j}", kp(x["ffn_conv_w"][i, j])) for j in range(3)]
        items += [(f"f_cb{i}", kp(x["ffn_conv_b"][i]))]
    items += [("nsa_qg", two(x["nsa_q_norm_g"][0]))]
    items += [(f"nsa_kg{j}", two(x["nsa_k_norm_g"][0, j])) for j in range(3)]
    items += [(f"pos{n}", x[f"nsa_cmp_pos_{n}"][0].reshape(16, P).T) for n in "kv"]
    items += [(f"g_mix2{i}", pk(x["norm_mix_g_2"][i])) for i in range(2)]
    items += [(f"g_ffn2{i}", pk(x["norm_ffn_g_2"][i])) for i in range(2)]
    items += [(f"b_mod{i}{v}", pk(x["b_mod_2"][i, D * v:D * v + D])) for i in range(2) for v in range(6)]
    items += [("cvec", np.stack([pk(x["c_2"][0]), pk(x["c_ctx_2"])], 2).reshape(P, 16))]
    items += [("conv2", np.concatenate([kp(x["conv_w_2"][0, j]) for j in range(3)], 1))]
    every = lambda v: np.broadcast_to(v.reshape(1, -1), (P, v.size))
    items += [("gate_b", every(x["nsa_gate_b"][0])), ("qg2", every(x["q_norm_g_2"][0])), ("kg2", every(x["k_norm_g_2"][0])),
              ("sink2", every(x["sink_logit_2"][0]))]
    items += [(f"b_rt{i}", every(np.concatenate([x["b_router_g_2"][i], x["b_router_e_2"][i]]))) for i in range(2)]
    for name, v in items:
        full = np.zeros((P, v.shape[1]), np.float32)
        full[:v.shape[0]] = v
        at[name] = (o, v.shape[1])
        o += v.shape[1]
        cols.append(full)
    return np.ascontiguousarray(np.concatenate(cols, 1)), at


class Progress:

    def __init__(self, name, sem, eng, table):
        self.name, self.sem, self.eng, self.table, self.n = name, sem, eng, table, 0

    def step(self, instr, *keys):
        instr.then_inc(self.sem, 1)
        self.n += 1
        for k in keys:
            assert (self.name, k) not in self.table or self.table[self.name, k] == self.n, k
            self.table[self.name, k] = self.n
        return instr

    def settle(self):
        self.eng.wait_ge(self.sem, self.n)


def build_program(nc, a, out, table, PARAM_AT, stop=None):
    ctx = ExitStack()
    with ctx:
        def sb(name, cols, dt=F32):
            return ctx.enter_context(nc.sbuf_tensor(name, [P, cols], dt))

        def sem(name):
            return ctx.enter_context(nc.semaphore(name))

        X = sb("resid", 4 * D)[:, :].rearrange("p (t d) -> p t d", t=4)
        HT = sb("normed_t", KC * 512)[:, :].rearrange("p (k t) -> p k t", k=KC)
        XS = sb("scaled", 2 * D)[:, :].rearrange("p (t d) -> p t d", t=2)
        ring = sb("ring", RING * 4096)
        CST = sb("consts", CONST.shape[1])
        Z = sb("arena", 12288)
        GB = sb("rows_bcast", 2 * D)[:, :].rearrange("p (t d) -> p t d", t=2)
        PRM = sb("params", a["params"].shape[1])
        MODC = sb("modulation", 192)[:, :].rearrange("p (l r v k) -> p l r v k", l=2, r=2, v=6)
        CSILU = sb("silu_c", 16)
        SM = sb("small", 1024)
        PS = ctx.enter_context(nc.psum_tensor("psum", [P, 8, 512], F32))
        slots = [ring[:, i * 4096:(i + 1) * 4096] for i in range(RING)]

        sems = {n: sem(f"{n}_done") for n in ("pe", "act", "dve", "pool")}
        ring_sem = [sem(f"slot{i}_loaded") for i in range(RING)]
        x_loaded, ident_loaded, params_loaded, consts_loaded, ctx_loaded = [
            sem(n + "_loaded") for n in ("x", "identity", "params", "consts", "context")]
        emb_sem = [sem(f"ple_norm_g{i}_loaded") for i in range(2)]
        out_sem = sem("out_written")

        def cst(name, rows=P):
            o, n = CONST_AT[name]
            return CST[0:rows, o:o + n]

        ident = cst("ident")

        def wait(eng, who, key):
            eng.wait_ge(sems[who], table.get((who, key), 1))

        def prm(name, rows=P):
            o, n = PARAM_AT[name]
            return PRM[0:rows, o:o + n]

        g_ab, g_nsa = prm("g_ab"), prm("g_nsa")
        g_ffn = [prm(f"g_ffn{i}") for i in range(2)]
        g_plg = [prm(f"g_plg{i}") for i in range(2)]
        g_ret, g_m, ab_cw, ab_cb = prm("g_ret"), prm("g_m"), prm("ab_cw"), prm("ab_cb")
        ig_b, fg_b = prm("ig_b", 4), prm("fg_b", 4)
        f_cw = [[prm(f"f_cw{i}{j}") for j in range(3)] for i in range(2)]
        f_cb = [prm(f"f_cb{i}") for i in range(2)]

        order = ["ab", "ffn0", "ple0", "nsa", "ffn1", "ple1", "mod", "em", "moe0", "at", "out"]
        on = lambda st: stop is None or order.index(st) <= order.index(stop)

        stream = []

        def wtile(name, *parts):
            stream.append((name, parts))

        def v8(n):
            return lambda s: s[:, 0:8 * n].rearrange("p (k n) -> p k n", k=8)

        def after_norm(name, w, c0, n):
            wtile(name, (v8(n), w.rearrange("(p k) n -> p k n", k=KC)[:, :, c0:c0 + n]))

        def after_heads(name, w, c0, n):
            wtile(name, (v8(n), w.rearrange("(k p) n -> p k n", p=P)[:, :, c0:c0 + n]))

        AB_TILES = [("qk", 0, 512), ("v", 512, 512), ("rg", 1024, 512), ("mqk", 1536, 512),
                    ("mv", 2048, 512), ("mo", 2560, 512), ("if", 3072, 8)]
        for nm, c0, n in AB_TILES:
            after_norm(f"ab.{nm}", a["ab_w_in"][0], c0, n)
        for n in range(2):
            after_heads(f"ab.out{n}", a["ab_w_out"][0], 512 * n, 512)

        MOD_BEHIND = {"up0": (0,), "up1": (1,), "up2": (2,), "down0": (3,), "up4": (4,), "down1": (5,),
                      "up5": (6,), "up6": (7,), "down2": (8,), "up8": (9,), "down3": (10,), "up9": (11,)}
        MOD_SUM_AFTER = {2: 0, 4: 1, 6: 2, 8: 3, 10: 4}

        def mod_tile(i, m_):
            w = a["w_mod_2"][i].rearrange("(p k) n -> p k n", k=KC)
            wtile(f"mod{i}.{m_}", (lambda s: s.rearrange("p (k n) -> p k n", k=4),
                                   w[:, 4 * (m_ % 2):4 * (m_ % 2) + 4, D * (m_ // 2):D * (m_ // 2) + D]))

        def ffn_tiles(i):
            up = a["ffn_w_up"][i].rearrange("(p k) n -> p k n", k=KC)

            def mods(behind):
                for m_ in MOD_BEHIND.get(behind, ()) if on("mod") else ():
                    mod_tile(i, m_)

            for j in range(FC // 2):
                wtile(f"ffn{i}.up{j}",
                      (lambda s: s.rearrange("p (h k n) -> p h k n", h=2, k=8)[:, 0], up[:, :, 256 * j:256 * j + 256]),
                      (lambda s: s.rearrange("p (h k n) -> p h k n", h=2, k=8)[:, 1],
                       up[:, :, FF + 256 * j:FF + 256 * j + 256]))
                mods(f"up{j}")
                for d in ([j // 2 - 1] if j >= 2 and j % 2 == 0 else []) + ([FC // 4] if j == FC // 2 - 1 else []):
                    nk = min(4, FC - 4 * d)
                    wtile(f"ffn{i}.down{d}",
                          (lambda s, nk=nk: s[:, 0:nk * D].rearrange("p (c n) -> p c n", n=D),
                           a["ffn_w_down"][i].rearrange("(c p) n -> p c n", p=P)[:, 4 * d:4 * d + nk, :]))
                    mods(f"down{d}")

        def ple_tiles(i):
            wtile(f"ple{i}.w", (lambda s: s[:, 0:2048].rearrange("p (k n) -> p k n", k=2),
                                a["ple_w"][i].rearrange("(k p) n -> p k n", p=P)),
                  (lambda s: s[:, 2048:2560].rearrange("p (t n) -> p t n", t=2),
                   a["p"][i, 0].rearrange("(t p) n -> p t n", p=P)))
            for n in range(2):
                after_norm(f"ple{i}.gate{n}", a["ple_w_gate"][i], 512 * n, 512)

        if on("ffn0"):
            ffn_tiles(0)
        if on("ple0"):
            ple_tiles(0)
        if on("nsa"):
            for nm, c0, n in [("c", 1024, 256), ("q0", 0, 512), ("q1", 512, 512), ("s", 1280, 512), ("gt", 1792, 48)]:
                after_norm(f"nsa.{nm}", a["nsa_w_in"][0], c0, n)
            for n in "kv":
                wtile(f"nsa.w1{n}", (lambda s: s.rearrange("p (c n) -> p c n", c=16),
                                     a[f"nsa_cmp_w1{n}"][0].rearrange("(c p) n -> p c n", p=P)))
            wtile("nsa.w2", *[((lambda s, j=j: s[:, P * j:P * j + P].rearrange("p (c n) -> p c n", c=2)),
                               a[f"nsa_cmp_w2{n}"][0].rearrange("(c p) n -> p c n", p=P)) for j, n in enumerate("kv")])
            for n in range(2):
                after_heads(f"nsa.out{n}", a["nsa_w_out"][0], 512 * n, 512)
        if on("ffn1"):
            ffn_tiles(1)
        if on("ple1"):
            ple_tiles(1)

        def router_tile(i):
            wtile(f"moe{i}.r", (lambda s: s[:, 0:288].rearrange("p (k n) -> p k n", k=8)[:, :, 0:4],
                                a["w_router_g_2"][i].rearrange("(p k) n -> p k n", k=KC)),
                  (lambda s: s[:, 0:288].rearrange("p (k n) -> p k n", k=8)[:, :, 4:36],
                   a["w_router_e_2"][i].rearrange("(p k) n -> p k n", k=KC)))

        if on("em"):
            for nm, c0 in [("a", 0), ("c", 1024), ("h", 1536), ("b", 512)]:
                after_norm(f"em.{nm}", a["w_in_even_2"][0], c0, 512)
            for n in range(2):
                after_heads(f"em.out{n}", a["w_out_even_2"][0], 512 * n, 512)
        if on("moe0"):
            router_tile(0)
        moe_at = {0: len(stream)}
        if on("at"):
            for nm, c0 in [("q0", 0), ("q1", 512), ("kv", 1024)]:
                after_norm(f"at.{nm}", a["w_qkv_2"][0], c0, 512)
            for n in range(2):
                after_heads(f"at.out{n}", a["w_o_2"][0], 512 * n, 512)
        if on("out"):
            router_tile(1)
        moe_at[1] = len(stream)

        owner_of, slot_of, need = {}, {}, {}
        before_moe = {}
        counts, last = [0] * RING, [None] * RING
        for n, (name, parts) in enumerate(stream):
            s = n % RING
            owner_of[name], slot_of[name] = last[s], s
            counts[s] += 16 * len(parts)
            need[name], last[s] = counts[s], name
            for i in range(2):
                if moe_at[i] == n + 1:
                    before_moe[i] = list(last)

        def W(name):
            return slots[slot_of[name]]

        mod_dram = nc.dram_tensor("mod_rows", (2, 2, 6 * D), F32, kind="Internal").ap()
        xb_dram = nc.dram_tensor("expert_rows", (48 * CAP, D), F32, kind="Internal").ap()
        yb_dram = nc.dram_tensor("expert_outputs", (48 * CAP, D), F32, kind="Internal").ap()
        zero_set, zeroed = sem("zero_tile_set"), sem("expert_rows_zeroed")
        ROWS, OVF, EIDX = sb("row_of_choice", 8, I32), sb("overflow_blocks", 20, I32), sb("expert_index", 32, U32)
        GWK = sb("choice_gates", 8)
        rows_written = [sem(f"mod_rows{i}_written") for i in range(2)]
        modc_loaded = [sem(f"mod_columns{i}_loaded") for i in range(2)]
        gates_written = [sem(f"gate_rows{i}_written") for i in range(2)]
        gate_loaded = [sem(f"gate{j}_loaded") for j in range(4)]
        block = ctx.enter_context(nc.Block())

        def freed(eng, tile):
            wait(eng, "dve" if tile.startswith("mod") else "pe", tile + ".used")

        def load_tile(sp, name, parts):
            if owner_of[name]:
                freed(sp, owner_of[name])
            for view, src in parts:
                sp.dma_start(view(W(name)), src).then_inc(ring_sem[slot_of[name]], 16)

        class Tensor:

            def __init__(self, eng):
                self.eng = eng
                self.p = Progress("pe", sems["pe"], eng, table)
                self.banks = {}

            def take(self, b, who, key):
                if b in self.banks:
                    wait(self.eng, *self.banks[b])
                self.banks[b] = (who, key)

            def weights(self, name):
                self.eng.wait_ge(ring_sem[slot_of[name]], need[name])
                return W(name)

        def arena(o, n, **kw):
            v = Z[:, o:o + n]
            return v

        QKR = Z[:, 0:1024].rearrange("p (t n) -> p t n", t=2)
        RT = Z[:, 1024:2048].rearrange("p (c t) -> p c t", c=4)
        V = Z[:, 2048:3072].rearrange("p (t n) -> p t n", t=2)
        SRG = Z[:, 3072:4096].rearrange("p (t n) -> p t n", t=2)
        MPAD = Z[:, 4096:4096 + 4 * 259].rearrange("p (c t) -> p c t", c=4)
        MQK = Z[:, 5136:6160].rearrange("p (c t) -> p c t", c=4)
        MV = Z[:, 6160:6160 + 1032].rearrange("p (t h e) -> p t h e", t=2, h=4)
        SMO = Z[:, 7200:8224].rearrange("p (t n) -> p t n", t=2)
        RTMP = Z[:, 8224:9248].rearrange("p (j n) -> p j n", j=4)
        PB = Z[:, 9248:9248 + 1536].rearrange("p (b n) -> p b n", b=4)
        EB = Z[:, 10784:10784 + 768].rearrange("p (b n) -> p b n", b=2)
        YH = HT[:, :, 256:512]
        YTOK = XS
        gates4 = SM[0:4, :]

        def norm_act(ac, p, name, tiles, after):
            for t in tiles:
                wait(ac, "dve", after) if after else None
                if t >= 2:
                    wait(ac, "pe", f"{name}.tr{t - 2}1")
                p.step(ac.activation(XS[:, t % 2, :], X[:, t, :], ACT.Square, accum_out=SM[:, 800 + t:801 + t]),
                       f"{name}.sq{t}")
                wait(ac, "dve", f"{name}.inv{t}")
                p.step(ac.activation(SM[:, 804 + t:805 + t], SM[:, 808 + t:809 + t], ACT.Sqrt), f"{name}.rs{t}")

        def norm_dve(dv, p, name, tiles, g, shift=None):
            for t in tiles:
                wait(dv, "act", f"{name}.sq{t}")
                p.step(dv.tensor_scalar(SM[:, 812 + t:813 + t], SM[:, 800 + t:801 + t], 1.0 / D, EPS, ALU.mult, ALU.add))
                p.settle()
                p.step(dv.reciprocal(SM[:, 808 + t:809 + t], SM[:, 812 + t:813 + t]), f"{name}.inv{t}")
                wait(dv, "act", f"{name}.rs{t}")
                p.step(dv.tensor_scalar(XS[:, t % 2, :], X[:, t, :], SM[:, 804 + t:805 + t], None, ALU.mult),
                       f"{name}.xs{t}")
            for t in tiles:
                for hf in range(2):
                    wait(dv, "pe", f"{name}.tr{t}{hf}")
                    dst = HT[:, 4 * hf:4 * hf + 4, P * t:P * t + P]
                    src = PS[:, 2 * (t % 2) + hf, :].rearrange("p (k t) -> p k t", k=4)
                    gb = g(t)[:, 4 * hf:4 * hf + 4].unsqueeze(2).to_broadcast([P, 4, P])
                    p.step(dv.tensor_tensor(dst, src, gb, ALU.mult), f"{name}.bank{t}{hf}")
                    if shift is not None:
                        p.settle()
                        sbc = shift(t)[:, 4 * hf:4 * hf + 4].unsqueeze(2).to_broadcast([P, 4, P])
                        p.step(dv.tensor_tensor(dst, dst, sbc, ALU.add))
            p.step(dv.memset(SM[0:1, 820:820 + 1], 0.0), f"{name}.ht")

        def norm_pe(te, name, tiles):
            for t in tiles:
                wait(te.eng, "dve", f"{name}.xs{t}")
                for hf in range(2):
                    b = 2 * (t % 2) + hf
                    te.take(b, "dve", f"{name}.bank{t}{hf}")
                    for j in range(4):
                        m = te.eng.transpose(PS[:, b, P * j:P * j + P], XS[:, t % 2, 4 * hf + j::8], ident)
                    te.p.step(m, f"{name}.tr{t}{hf}")
            wait(te.eng, "dve", f"{name}.ht")

        def rows(te, name, t, bank, reader, n=512, c0=0, src=None, tag=None, last=False, kc=KC, k0=0):
            w = te.weights(name)[:, 0:kc * n].rearrange("p (k n) -> p k n", k=kc)
            te.take(bank, *reader)
            src = HT if src is None else src
            for k in range(kc):
                m = te.eng.matmul(PS[:, bank, 0:n], src[:, k0 + k, P * t:P * t + P], w[:, k, :],
                                  start=(k == 0), stop=(k == kc - 1))
            te.p.step(m, f"{name}.t{t}", *([f"{name}.used"] if last else []))

        def ab_pe(te):
            pe, p = te.eng, te.p
            norm_pe(te, "n.ab", (0, 1))
            for t in range(2):
                rows(te, "ab.qk", t, t, ("dve", f"ab.rot{t}"), last=t == 1)
            for t in range(2):
                rows(te, "ab.v", t, 2 + t, ("act", f"ab.v{t}"), last=t == 1)
            for t in range(2):
                rows(te, "ab.rg", t, 4 + t, ("act", f"ab.rg{t}"), last=t == 1)
            w = te.weights("ab.mqk").rearrange("p (k n) -> p k n", k=8)
            for c in range(4):
                b = 6 + c // 2
                if c % 2 == 0:
                    te.take(b, "act", f"ab.mpad{c + 1}")
                for k in range(KC):
                    m = pe.matmul(PS[:, b, 256 * (c % 2):256 * (c % 2) + 256], w[:, k, P * c:P * c + P], HT[:, k, 0:T],
                                  start=(k == 0), stop=(k == KC - 1))
                p.step(m, f"ab.mqk{c}", *(["ab.mqk.used"] if c == 3 else []))
            for t in range(2):
                wait(pe, "dve", f"ab.rot{t}")
                te.take(t, "act", f"ab.rt{t}")
                for c in range(4):
                    m = pe.transpose(PS[:, t, P * c:P * c + P], QKR[:, t, P * c:P * c + P], ident)
                p.step(m, f"ab.rtr{t}")
            for t in range(2):
                rows(te, "ab.mv", t, 2 + t, ("dve", f"ab.mv{t}"), last=t == 1)
            for t in range(2):
                rows(te, "ab.mo", t, 4 + t, ("act", f"ab.mo{t}"), last=t == 1)
            w = te.weights("ab.if")[:, 0:64].rearrange("p (k n) -> p k n", k=8)
            te.take(6, "act", "ab.fabs")
            for j in range(2):
                for k in range(KC):
                    m = pe.matmul(PS[0:4, 6, 256 * j:256 * j + 256], w[:, k, 4 * j:4 * j + 4], HT[:, k, 0:T],
                                  start=(k == 0), stop=(k == KC - 1))
            p.step(m, "ab.if.done", "ab.if.used")

            def scores(tag, h, src, b, reader):
                o = 64 * (h % 2)
                q, kk = src[o:o + 64, h // 2, :], src[o:o + 64, 2 + h // 2, :]
                te.take(b, *reader)
                pe.matmul(PS[:, b, 0:256], kk[:, 0:P], q, start=True, stop=True)
                p.step(pe.matmul(PS[:, b, 256:384], kk[:, P:T], q[:, P:T], start=True, stop=True), f"{tag}.s{h}")

            wait(pe, "act", "ab.rt1")
            wait(pe, "act", "ab.v1")
            for h in range(5):
                if h < 4:
                    scores("ret", h, RT, h % 2, ("dve", f"ret.p{h}"))
                if h >= 1:
                    g = h - 1
                    wait(pe, "dve", f"ret.p{g}")
                    if g == 0:
                        te.take(6 + 1, "dve", "ret.o1")
                        te.take(2, "dve", "ret.o0")
                    vv = lambda t: V[:, t, P * g:P * g + P]
                    pe.matmul(PS[:, 2, P * g:P * g + P], PB[:, g, 0:P], vv(0), start=True, stop=True)
                    pe.matmul(PS[:, 7, P * g:P * g + P], PB[:, g, P:2 * P], vv(0), start=True, stop=False)
                    m = pe.matmul(PS[:, 7, P * g:P * g + P], PB[:, g, 2 * P:3 * P], vv(1), start=False, stop=True)
                    p.step(m, f"ret.pv{g}")
            wait(pe, "dve", "ml.rows")
            pe.wait_ge(consts_loaded, 16)
            te.take(3, "dve", "ml.cols")
            for t in range(2):
                pe.transpose(PS[:, 3, 4 * t:4 * t + 4], gates4[:, 0 + P * t:P * t + P], ident[0:4, 0:4])
                m = pe.transpose(PS[:, 3, 8 + 4 * t:12 + 4 * t], gates4[:, 256 + P * t:256 + P * t + P], ident[0:4, 0:4])
            p.step(m, "ml.colt")
            wait(pe, "dve", "ml.mqk")
            for h in range(5):
                if h < 4:
                    te.take(4 + h % 2, "dve", f"ml.g{h}")
                    p.step(pe.matmul(PS[:, 4 + h % 2, 0:256], cst(f"head{h}", 4), G4, start=True, stop=True), f"ml.gb{h}")
                    scores("ml", h, MQK, h % 2, ("dve", f"ml.ps{h}"))
                if h >= 1:
                    g = h - 1
                    wait(pe, "dve", f"ml.p{g}")
                    if g % 2 == 0:
                        te.take((3, 6)[g // 2], "dve", f"ml.o0{g // 2}")
                        te.take((2, 7)[g // 2], "dve", f"ml.o1{g // 2}")
                    b0, b1 = (3, 6)[g // 2], (2, 7)[g // 2]
                    o = 129 * (g % 2)
                    pe.matmul(PS[:, b0, o:o + 129], PB[:, g, 0:P], MV[:, 0, g, :], start=True, stop=True)
                    pe.matmul(PS[:, b1, o:o + 129], PB[:, g, P:2 * P], MV[:, 0, g, :], start=True, stop=False)
                    m = pe.matmul(PS[:, b1, o:o + 129], PB[:, g, 2 * P:3 * P], MV[:, 1, g, :], start=False, stop=True)
                    p.step(m, f"ml.pv{g}")
            for j in range(2):
                for t in range(2):
                    wait(pe, "dve", f"ab.y{j}{t}")
                    b = 2 * j + t
                    te.take((0, 1, 4, 5)[b], "dve", f"ab.yt{j}{t}")
                    for c in range(4):
                        m = pe.transpose(PS[:, (0, 1, 4, 5)[b], P * c:P * c + P],
                                         YTOK[:, t, 512 * j + P * c:512 * j + P * c + P], ident)
                    p.step(m, f"ab.ytr{j}{t}")
            wait(pe, "dve", "ab.yt11")
            for n in range(2):
                for t in range(2):
                    rows(te, f"ab.out{n}", t, 2 * n + t, ("dve", f"ab.res{n}{t}"), src=YH, last=t == 1)

        G4 = SM[0:4, 512:768]

        def ab_act(ac, p):
            norm_act(ac, p, "n.ab", (0, 1), None)
            for t in range(2):
                wait(ac, "pe", f"ab.v.t{t}")
                p.step(ac.activation(V[:, t, :], PS[:, 2 + t, :], ACT.Copy), f"ab.v{t}")
            for t in range(2):
                wait(ac, "pe", f"ab.rg.t{t}")
                p.step(ac.activation(SRG[:, t, :], PS[:, 4 + t, :], ACT.Silu), f"ab.rg{t}")
            for c in range(4):
                wait(ac, "pe", f"ab.mqk{c | 1}")
                p.step(ac.activation(MPAD[:, c, 3:259], PS[:, 6 + c // 2, 256 * (c % 2):256 * (c % 2) + 256], ACT.Copy),
                       f"ab.mpad{c}")
            for t in range(2):
                wait(ac, "pe", f"ab.rtr{t}")
                p.step(ac.activation(RT[:, :, P * t:P * t + P], PS[:, t, :].rearrange("p (c t) -> p c t", c=4), ACT.Copy),
                       f"ab.rt{t}")
            for t in range(2):
                wait(ac, "pe", f"ab.mo.t{t}")
                p.step(ac.activation(SMO[:, t, :], PS[:, 4 + t, :], ACT.Sigmoid), f"ab.mo{t}")
            wait(ac, "pe", "ab.if.done")
            ac.wait_ge(params_loaded, 16)
            ac.wait_ge(consts_loaded, 16)
            p.step(ac.activation(gates4[:, 0:256], PS[0:4, 6, 0:256], ACT.Identity, bias=ig_b), "ab.i")
            p.step(ac.activation(G4, PS[0:4, 6, 256:512], ACT.Identity, bias=fg_b), "ab.f")
            p.settle()
            p.step(ac.activation(gates4[:, 256:512], G4, ACT.Abs), "ab.fabs")
            p.settle()
            p.step(ac.activation(gates4[:, 256:512], gates4[:, 256:512], ACT.Exp, scale=-1.0))
            p.settle()
            p.step(ac.activation(gates4[:, 256:512], gates4[:, 256:512], ACT.Ln, bias=cst("ones", 4)[:, 0:1]), "ab.ln")
            for c in range(4):
                wait(ac, "dve", f"ml.conv{c}")
                p.step(ac.activation(MQK[:, c, :], RTMP[:, c, :], ACT.Silu), f"ml.mqk{c}")
            for t in range(2):
                wait(ac, "pe", "ret.pv3")
                p.settle()
                p.step(ac.activation(RTMP[:, 2 * t:2 * t + 2, :].rearrange("p a b -> p (a b)"), PS[:, (2, 7)[t], :], ACT.Square),
                       f"ret.sq{t}")
                wait(ac, "dve", f"ret.inv{t}")
                p.step(ac.activation(SR[:, t, 4:8], SR[:, t, 0:4], ACT.Sqrt), f"ret.rs{t}")
            wait(ac, "dve", "ml.cols")
            p.step(ac.activation(MC[:, 16:24], MC[:, 8:16], ACT.Exp, scale=-1.0), "ml.em")
            for h in range(4):
                wait(ac, "dve", f"ml.g{h}")
                if h >= 2:
                    wait(ac, "dve", f"ml.p{h - 2}")
                p.step(ac.activation(EB[:, h % 2, 0:256], EB[:, h % 2, 0:256], ACT.Exp, bias=MC[:, h:h + 1], scale=-1.0))
                p.step(ac.activation(EB[:, h % 2, 256:384], EB[:, h % 2, 256:384], ACT.Exp, bias=MC[:, 4 + h:5 + h], scale=-1.0),
                       f"ml.e{h}")
            for t in range(2):
                wait(ac, "dve", f"ml.h{t}")
                p.settle()
                p.step(ac.activation(RTMP[:, 2 * t:2 * t + 2, :].rearrange("p a b -> p (a b)"), HM[:, t, :], ACT.Square),
                       f"ml.sq{t}")
                wait(ac, "dve", f"ml.inv{t}")
                p.step(ac.activation(SR[:, t, 4:8], SR[:, t, 0:4], ACT.Sqrt), f"ml.rs{t}")

        SR = SM[:, 830:846].rearrange("p (t n) -> p t n", t=2)
        SR2 = SM[:, 846:862].rearrange("p (t n) -> p t n", t=2)
        MC = SM[:, 862:890]
        HM = Z[:, 0:1024].rearrange("p (t n) -> p t n", t=2)

        def bc4(col4, n=P):
            return col4.unsqueeze(2).to_broadcast([P, 4, n])

        def h4(v):
            return v.rearrange("p (h e) -> p h e", h=4)

        def head_norm_dve(dv, p, tag, t, src, gate, dst, key):
            wait(dv, "act", f"{tag}.sq{t}")
            p.step(dv.tensor_reduce(SR2[:, t, 0:4], h4(RTMP[:, 2 * t:2 * t + 2, :].rearrange("p a b -> p (a b)")), AXX, ALU.add))
            p.settle()
            p.step(dv.tensor_scalar(SR2[:, t, 4:8], SR2[:, t, 0:4], 1.0 / P, EPS, ALU.mult, ALU.add))
            p.settle()
            p.step(dv.reciprocal(SR[:, t, 0:4], SR2[:, t, 4:8]), f"{tag}.inv{t}")
            wait(dv, "act", f"{tag}.rs{t}")
            p.step(dv.tensor_tensor(h4(dst), h4(src), bc4(SR[:, t, 4:8]), ALU.mult), f"{tag}.o{t}" if tag == "ret" else f"{tag}.n{t}")
            p.settle()
            p.step(dv.tensor_tensor(dst, dst, gate, ALU.mult), key)

        def ab_dve(dv, p):
            norm_dve(dv, p, "n.ab", (0, 1), lambda t: g_ab)
            dv.wait_ge(consts_loaded, 16)
            for t in range(2):
                wait(dv, "pe", f"ab.qk.t{t}")
                q = PS[:, t, :].rearrange("p (h s e) -> p h s e", h=8, s=2)
                o = QKR[:, t, :].rearrange("p (h s e) -> p h s e", h=8, s=2)
                cs = cst(f"cos{t}").unsqueeze(1).to_broadcast([P, 8, 32])
                sn = cst(f"sin{t}").unsqueeze(1).to_broadcast([P, 8, 32])
                tm = [RTMP[:, j, :].rearrange("p (h e) -> p h e", h=8) for j in range(4)]
                p.settle()
                p.step(dv.tensor_tensor(tm[0], q[:, :, 0, :], cs, ALU.mult))
                p.step(dv.tensor_tensor(tm[1], q[:, :, 1, :], sn, ALU.mult))
                p.step(dv.tensor_tensor(tm[2], q[:, :, 0, :], sn, ALU.mult))
                p.step(dv.tensor_tensor(tm[3], q[:, :, 1, :], cs, ALU.mult))
                p.settle()
                p.step(dv.tensor_tensor(o[:, :, 0, :], tm[0], tm[1], ALU.subtract))
                p.step(dv.tensor_tensor(o[:, :, 1, :], tm[2], tm[3], ALU.add), f"ab.rot{t}")
            p.step(dv.memset(MPAD[:, :, 0:3], 0.0))
            p.step(dv.memset(MV[:, :, :, 128:129], 1.0))
            for t in range(2):
                wait(dv, "pe", f"ab.mv.t{t}")
                p.step(dv.tensor_copy(MV[:, t, :, 0:128], h4(PS[:, 2 + t, :])), f"ab.mv{t}")
            for c in range(4):
                wait(dv, "act", f"ab.mpad{c}")
                p.settle()
                p.step(dv.tensor_scalar(RTMP[:, c, :], MPAD[:, c, 0:256], ab_cw[:, c:c + 1], ab_cb[:, c:c + 1], ALU.mult, ALU.add))
                for j in range(1, 4):
                    p.settle()
                    p.step(dv.scalar_tensor_tensor(out=RTMP[:, c, :], in0=MPAD[:, c, j:j + 256],
                                                   scalar=ab_cw[:, 4 * j + c:4 * j + c + 1], in1=RTMP[:, c, :],
                                                   op0=ALU.mult, op1=ALU.add), *([f"ml.conv{c}"] if j == 3 else []))
            for h in range(4):
                wait(dv, "pe", f"ret.s{h}")
                p.step(dv.tensor_tensor(PB[:, h, :], PS[:, h % 2, 0:384], cst(f"decay{h}"), ALU.mult), f"ret.p{h}")
            wait(dv, "act", "ab.ln")
            lf, LN, A4 = G4, gates4[:, 256:512], gates4[:, 0:256]
            p.step(dv.tensor_scalar(lf, lf, 0.0, None, ALU.min))
            p.settle()
            p.step(dv.tensor_tensor(lf, lf, LN, ALU.subtract))
            p.settle()
            p.step(dv.tensor_tensor_scan(LN, cst("ones", 4), lf, 0.0, ALU.mult, ALU.add))
            p.settle()
            p.step(dv.tensor_tensor(A4, A4, LN, ALU.subtract))
            p.settle()
            p.step(dv.tensor_tensor_scan(G4, A4, A4, 0.0, ALU.max, ALU.max))
            p.settle()
            p.step(dv.tensor_tensor(LN, LN, G4, ALU.add), "ml.rows")
            for t in range(2):
                head_norm_dve(dv, p, "ret", t, PS[:, (2, 7)[t], :], SRG[:, t, :], YTOK[:, t, 0:512], f"ab.y0{t}")
            wait(dv, "pe", "ml.colt")
            p.step(dv.tensor_copy(MC[:, 0:16], PS[:, 3, 0:16]), "ml.cols")
            wait(dv, "act", "ml.mqk3")
            p.step(dv.memset(SM[0:1, 821:821 + 1], 0.0), "ml.mqk")
            p.settle()

            def g_max(h):
                wait(dv, "pe", f"ml.gb{h}")
                if h >= 2:
                    wait(dv, "dve", f"ml.p{h - 2}")
                gb = PS[:, 4 + h % 2, 0:256]
                p.step(dv.tensor_scalar(EB[:, h % 2, 0:256], gb, MC[:, h:h + 1], None, ALU.max))
                p.step(dv.tensor_scalar(EB[:, h % 2, 256:384], gb[:, P:T], MC[:, 4 + h:5 + h], None, ALU.max), f"ml.g{h}")

            g_max(0)
            for h in range(4):
                wait(dv, "pe", f"ml.s{h}")
                if h == 0:
                    wait(dv, "pe", "ret.pv3")
                p.step(dv.tensor_tensor(PB[:, h, :], PS[:, h % 2, 0:384], cst("causal_mul"), ALU.mult), f"ml.ps{h}")
                if h < 3:
                    g_max(h + 1)
                p.settle()
                wait(dv, "act", f"ml.e{h}")
                p.step(dv.tensor_tensor(PB[:, h, :], PB[:, h, :], EB[:, h % 2, :], ALU.mult), f"ml.p{h}")
            wait(dv, "pe", "ml.pv3")
            wait(dv, "act", "ml.em")
            for t in range(2):
                for j in range(2):
                    src = PS[:, ((3, 6), (2, 7))[t][j], 0:258].rearrange("p (h e) -> p h e", h=2)
                    den = SR2[:, t, 2 * j:2 * j + 2]
                    c2 = lambda v: v.unsqueeze(2)
                    p.settle()
                    p.step(dv.tensor_copy(c2(den), src[:, :, 128:129]))
                    p.settle()
                    ab = SR2[:, t, 4 + 2 * j:6 + 2 * j]
                    p.step(dv.scalar_tensor_tensor(out=ab, in0=den, scalar=-1.0, in1=den, op0=ALU.mult, op1=ALU.max))
                    p.settle()
                    p.step(dv.tensor_tensor(ab, ab, MC[:, 16 + 4 * t + 2 * j:18 + 4 * t + 2 * j], ALU.max))
                    p.settle()
                    p.step(dv.reciprocal(den, ab))
                    p.settle()
                    p.step(dv.tensor_tensor(HM[:, t, 256 * j:256 * j + 256].rearrange("p (h e) -> p h e", h=2), src[:, :, 0:128],
                                            den.unsqueeze(2).to_broadcast([P, 2, P]), ALU.mult),
                           f"ml.o{t}{j}", *([f"ml.h{t}"] if j == 1 else []))
                p.settle()
            for t in range(2):
                head_norm_dve(dv, p, "ml", t, HM[:, t, :], SMO[:, t, :], YTOK[:, t, 512:1024], f"ab.y1{t}")
            for j in range(2):
                for t in range(2):
                    wait(dv, "pe", f"ab.ytr{j}{t}")
                    p.step(dv.tensor_tensor(YH[:, 4 * j:4 * j + 4, P * t:P * t + P], h4(PS[:, (0, 1, 4, 5)[2 * j + t], :]),
                                            bc4(g_ret if j == 0 else g_m), ALU.mult), f"ab.yt{j}{t}")
            for n in range(2):
                for t in range(2):
                    wait(dv, "pe", f"ab.out{n}.t{t}")
                    xr = X[:, t, 512 * n:512 * n + 512]
                    p.step(dv.tensor_tensor(xr, xr, PS[:, 2 * n + t, :], ALU.add), f"ab.res{n}{t}")

        MACC = Z[:, 7168:7168 + 4096].rearrange("p (b r n) -> p b r n", b=2, r=2)

        MOD_PAIRS = [(m_, k) for m_ in range(12) for k in range(4)]

        def mod_products(dv, p, i, c):
            first, end = [-(-len(MOD_PAIRS) * x // FC) for x in (c, c + 1)]
            for m_, k in MOD_PAIRS[first:end]:
                v, b = m_ // 2, m_ // 2 % 2
                name = f"mod{i}.{m_}"
                if k == 0:
                    dv.wait_ge(ring_sem[slot_of[name]], need[name])
                    if m_ % 2 == 0 and v >= 2:
                        wait(dv, "pe", f"mod{i}.sum{v - 2}")
                w = W(name).rearrange("p (k n) -> p k n", k=4)[:, k, :]
                for r in range(2):
                    o = 8 * r + 4 * (m_ % 2) + k
                    acc, sc = MACC[:, b, r, :], CSILU[:, o:o + 1]
                    if m_ % 2 == 0 and k == 0:
                        ins = dv.tensor_scalar(acc, w, sc, None, ALU.mult)
                    else:
                        dv.wait_ge(sems["dve"], p.n - 1)
                        ins = dv.scalar_tensor_tensor(out=acc, in0=w, scalar=sc, in1=acc, op0=ALU.mult, op1=ALU.add)
                    p.step(ins, *([name + ".used"] if (k, r) == (3, 1) else []))

        MROW = Z[:, 5632:6144]

        def mod_sum(te, i, v):
            wait(te.eng, "dve", f"mod{i}.{2 * v + 1}.used")
            te.take(3, "dve", f"mod{i}.row{v}")
            for r in range(2):
                for h in range(2):
                    g = 32 * (2 * r + h)
                    m = te.eng.matmul(PS[g:g + 32, 3, :], cst("ones")[:, 0:32], MACC[:, v % 2, r, 512 * h:512 * h + 512], start=True, stop=True)
            te.p.step(m, f"mod{i}.sum{v}")

        def mod_row_dve(dv, p, i, v):
            wait(dv, "pe", f"mod{i}.sum{v}")
            if v:
                dv.wait_ge(rows_written[i], 32 * v)
            p.step(dv.tensor_copy(MROW, PS[:, 3, :]), f"mod{i}.row{v}")

        def mod_row_act(ac, i, v):
            wait(ac, "dve", f"mod{i}.row{v}")
            for r in range(2):
                ac.dma_start(mod_dram[i, r, D * v:D * v + D].rearrange("(h n) -> h n", h=2), MROW[64 * r:64 * r + 64:32, :])\
                    .then_inc(rows_written[i], 16)

        def mod_columns_pool(po, i):
            po.wait_ge(rows_written[i], 32 * 6)
            for r in range(2):
                po.dma_start(MODC[:, i, r], mod_dram[i, r].rearrange("(v p k) -> p v k", v=6, p=P)).then_inc(modc_loaded[i], 16)
            wait(po, "dve", f"mod{i}.col")
            for v in (2, 5):
                for r in range(2):
                    po.dma_start(mod_dram[i, r, D * v:D * v + D].rearrange("(p k) -> p k", p=P), MODC[:, i, r, v, :])\
                        .then_inc(gates_written[i], 16)

        def mod_columns_dve(dv, p, i):
            dv.wait_ge(modc_loaded[i], 32)
            bias = PRM[:, PARAM_AT[f"b_mod{i}0"][0]:][:, 0:48]
            p.step(dv.tensor_tensor(MODC[:, i], MODC[:, i], bias.rearrange("p (v k) -> p v k", v=6).unsqueeze(1).to_broadcast([P, 2, 6, 8]), ALU.add),
                   f"mod{i}.col")
            p.settle()
            for v, g in ((1, f"g_mix2{i}"), (4, f"g_ffn2{i}")):
                p.step(dv.scalar_tensor_tensor(out=MODC[:, i, :, v, :], in0=MODC[:, i, :, v, :], scalar=1.0,
                                               in1=prm(g).unsqueeze(1).to_broadcast([P, 2, 8]), op0=ALU.add, op1=ALU.mult))

        GT = Z[:, 0:FC * 256].rearrange("p (c t) -> p c t", c=FC)
        AC = Z[:, 6144:6144 + 1024].rearrange("p (b t) -> p b t", b=4)

        def ffn_pe(te, i):
            pe, p = te.eng, te.p
            norm_pe(te, f"n.ffn{i}", (0, 1))

            def down(j):
                w = te.weights(f"ffn{i}.down{j}").rearrange("p (c n) -> p c n", n=D)
                nk = min(4, FC - 4 * j)
                for cc in range(nk):
                    c = 4 * j + cc
                    wait(pe, "dve", f"ffn{i}.g{c}")
                    for t in range(2):
                        for n in range(2):
                            if c == 0:
                                te.take(4 + 2 * n + t, "dve", f"ffn{i}.res{n}{t}")
                            m = pe.matmul(PS[:, 4 + 2 * n + t, :], GT[:, c, P * t:P * t + P], w[:, cc, 512 * n:512 * n + 512],
                                          start=(c == 0), stop=(c == FC - 1))
                p.step(m, f"ffn{i}.down{j}.used")

            for j in range(FC // 2):
                w = te.weights(f"ffn{i}.up{j}").rearrange("p (h k n) -> p h k n", h=2, k=8)
                for cc in range(2):
                    c = 2 * j + cc
                    b = c % 3
                    te.take(b, "dve", f"ffn{i}.g{c}")
                    for hf in range(2):
                        for k in range(KC):
                            m = pe.matmul(PS[:, b, 256 * hf:256 * hf + 256], w[:, hf, k, P * cc:P * cc + P], HT[:, k, 0:T],
                                          start=(k == 0), stop=(k == KC - 1))
                    p.step(m, f"ffn{i}.u{c}", *([f"ffn{i}.up{j}.used"] if cc == 1 else []))
                if on("mod") and j in MOD_SUM_AFTER:
                    mod_sum(te, i, MOD_SUM_AFTER[j])
                if j >= 2 and j % 2 == 0:
                    down(j // 2 - 1)
            if on("mod"):
                mod_sum(te, i, 5)
            down(FC // 4)

        def ffn_act(ac, p, i, after):
            norm_act(ac, p, f"n.ffn{i}", (0, 1), after)
            for c in range(FC + 1):
                if c < FC:
                    wait(ac, "pe", f"ffn{i}.u{c}")
                    if c >= 4:
                        wait(ac, "dve", f"ffn{i}.g{c - 4}")
                    p.step(ac.activation(AC[:, c % 4, :], PS[:, c % 3, 0:256], ACT.Identity, bias=f_cb[i][:, c:c + 1],
                                         scale=f_cw[i][2][:, c:c + 1]), f"ffn{i}.a{c}")
                if c >= 1:
                    wait(ac, "dve", f"ffn{i}.c{c - 1}")
                    p.step(ac.activation(AC[:, (c - 1) % 4, :], AC[:, (c - 1) % 4, :], ACT.Gelu_apprx_tanh), f"ffn{i}.gelu{c - 1}")
                if on("mod") and c % 2 == 0 and (c - 4) // 2 in MOD_SUM_AFTER:
                    mod_row_act(ac, i, MOD_SUM_AFTER[(c - 4) // 2])
            if on("mod"):
                for v in (4, 5):
                    mod_row_act(ac, i, v)

        def ffn_dve(dv, p, i):
            norm_dve(dv, p, f"n.ffn{i}", (0, 1), lambda t: g_ffn[i])
            wait(dv, "act", "mod.silu")
            for c in range(FC + 1):
                if c < FC:
                    wait(dv, "act", f"ffn{i}.a{c}")
                    acc, a_ = AC[:, c % 4, :], PS[:, c % 3, 0:256]
                    p.step(dv.scalar_tensor_tensor(out=acc[:, 1:256], in0=a_[:, 0:255], scalar=f_cw[i][1][:, c:c + 1],
                                                   in1=acc[:, 1:256], op0=ALU.mult, op1=ALU.add))
                    p.settle()
                    p.step(dv.scalar_tensor_tensor(out=acc[:, 2:256], in0=a_[:, 0:254], scalar=f_cw[i][0][:, c:c + 1],
                                                   in1=acc[:, 2:256], op0=ALU.mult, op1=ALU.add), f"ffn{i}.c{c}")
                if c >= 1:
                    d = c - 1
                    wait(dv, "act", f"ffn{i}.gelu{d}")
                    p.step(dv.tensor_tensor(GT[:, d, :], AC[:, d % 4, :], PS[:, d % 3, 256:512], ALU.mult), f"ffn{i}.g{d}")
                if on("mod") and c % 2 == 1 and (c - 3) // 2 in MOD_SUM_AFTER:
                    mod_row_dve(dv, p, i, MOD_SUM_AFTER[(c - 3) // 2])
                if on("mod") and c < FC:
                    mod_products(dv, p, i, c)
            if on("mod"):
                for v in (4, 5):
                    mod_row_dve(dv, p, i, v)
            wait(dv, "pe", f"ffn{i}.down{FC // 4}.used")
            for n in range(2):
                for t in range(2):
                    xr = X[:, t, 512 * n:512 * n + 512]
                    p.step(dv.tensor_tensor(xr, xr, PS[:, 4 + 2 * n + t, :], ALU.add), f"ffn{i}.res{n}{t}")

        EE = Z[:, 0:2048].rearrange("p (t n) -> p t n", t=2)
        PT = Z[:, 2048:2560].rearrange("p (k t) -> p k t", k=2)
        SG = Z[:, 2560:4608].rearrange("p (t n) -> p t n", t=2)
        EJ = Z[:, 4608:5632]

        def ple_pe(te, i):
            pe, p = te.eng, te.p
            w = te.weights(f"ple{i}.w")
            ptok = w[:, 2048:2560].rearrange("p (t n) -> p t n", t=2)
            te.take(0, "act", f"ple{i}.pt")
            for t in range(2):
                for k in range(2):
                    m = pe.transpose(PS[:, 0, 256 * k + P * t:256 * k + P * t + P], ptok[:, t, P * k:P * k + P], ident)
            p.step(m, f"ple{i}.ptr")
            wait(pe, "act", f"ple{i}.pt")
            w2 = w[:, 0:2048].rearrange("p (k n) -> p k n", k=2)
            for t in range(2):
                for n in range(2):
                    te.take(4 + 2 * t + n, "dve", f"ple{i}.e{t}")
                    for k in range(2):
                        m = pe.matmul(PS[:, 4 + 2 * t + n, :], PT[:, k, P * t:P * t + P], w2[:, k, 512 * n:512 * n + 512],
                                      start=(k == 0), stop=(k == 1))
                p.step(m, f"ple{i}.e.t{t}", *([f"ple{i}.w.used"] if t == 1 else []))
            norm_pe(te, f"n.plg{i}", (0, 1))
            for n in range(2):
                for t in range(2):
                    rows(te, f"ple{i}.gate{n}", t, 2 * n + t, ("act", f"ple{i}.sg{n}{t}"), last=t == 1)

        def ple_act(ac, p, i, after):
            wait(ac, "pe", f"ple{i}.ptr")
            p.step(ac.activation(PT, PS[:, 0, :].rearrange("p (k t) -> p k t", k=2), ACT.Copy), f"ple{i}.pt")
            for t in range(2):
                wait(ac, "pe", f"ple{i}.e.t{t}")
                p.settle()
                p.step(ac.activation(EJ.rearrange("p (b n) -> p b n", b=2), PS[:, 4 + 2 * t:6 + 2 * t, :], ACT.Square,
                                     accum_out=SM[:, 890 + t:891 + t]), f"ple{i}.sq{t}")
                wait(ac, "dve", f"ple{i}.inv{t}")
                p.step(ac.activation(SM[:, 894 + t:895 + t], SM[:, 892 + t:893 + t], ACT.Sqrt), f"ple{i}.rs{t}")
            norm_act(ac, p, f"n.plg{i}", (0, 1), after)
            for n in range(2):
                for t in range(2):
                    wait(ac, "pe", f"ple{i}.gate{n}.t{t}")
                    p.step(ac.activation(SG[:, t, 512 * n:512 * n + 512], PS[:, 2 * n + t, :], ACT.Sigmoid), f"ple{i}.sg{n}{t}")

        def ple_dve(dv, p, i):
            for t in range(2):
                wait(dv, "act", f"ple{i}.sq{t}")
                p.step(dv.tensor_scalar(SM[:, 896 + t:897 + t], SM[:, 890 + t:891 + t], 1.0 / D, EPS, ALU.mult, ALU.add))
                p.settle()
                p.step(dv.reciprocal(SM[:, 892 + t:893 + t], SM[:, 896 + t:897 + t]), f"ple{i}.inv{t}")
                wait(dv, "act", f"ple{i}.rs{t}")
                dv.wait_ge(emb_sem[i], 16)
                p.step(dv.scalar_tensor_tensor(out=EE[:, t, :].rearrange("p (b n) -> p b n", b=2), in0=PS[:, 4 + 2 * t:6 + 2 * t, :],
                                               scalar=SM[:, 894 + t:895 + t],
                                               in1=GB[:, i, :].rearrange("p (b n) -> p b n", b=2), op0=ALU.mult, op1=ALU.mult),
                       f"ple{i}.e{t}")
            norm_dve(dv, p, f"n.plg{i}", (0, 1), lambda t: g_plg[i])
            for n in range(2):
                for t in range(2):
                    wait(dv, "act", f"ple{i}.sg{n}{t}")
                    c = slice(512 * n, 512 * n + 512)
                    p.step(dv.tensor_tensor(SG[:, t, c], SG[:, t, c], EE[:, t, c], ALU.mult))
                    p.settle()
                    p.step(dv.tensor_tensor(X[:, t, c], X[:, t, c], SG[:, t, c], ALU.add),
                           *([f"ple{i}.res"] if (n, t) == (1, 1) else []))


        NQ = Z[:, 0:2048].rearrange("p (t n) -> p t n", t=2)
        NO = NQ
        NQT = Z[:, 2048:4096].rearrange("p (c t) -> p c t", c=8)
        NK = Z[:, 4096:5120].rearrange("p (t a g u e) -> p t a g u e", t=2, a=2, g=2, u=2)
        NB = Z[:, 4096:5120].rearrange("p (b n) -> p b n", b=4)
        NV = Z[:, 5120:5632].rearrange("p (t a g e) -> p t a g e", t=2, a=2, g=2)
        NKT = Z[:, 5632:6656].rearrange("p (c t) -> p c t", c=4)
        NSQ = Z[:, 6656:7680].rearrange("p (b n) -> p b n", b=2)
        NPT = Z[:, 6656:7168].rearrange("p (b n) -> p b n", b=2)
        NTMP = Z[:, 7168:7680]
        BLK = Z[:, 7680:8640].rearrange("p (v l c) -> p v l c", v=2, l=16)
        HID = Z[:, 8640:9152].rearrange("p (v n) -> p v n", v=2)
        HIDT = Z[:, 9152:9272].rearrange("p (v c n) -> p v c n", v=2, c=2)
        KCN = Z[0:30, 9272:9400]
        KCT = Z[:, 9400:9430]
        VC = Z[0:NC_CMP, 9430:9558].rearrange("p (g e) -> p g e", g=2)
        VB = Z[0:120, 9558:10582].rearrange("p (g h e) -> p g h e", g=2, h=8)
        SC = Z[:, 10582:11062].rearrange("p (t h n) -> p t h n", t=2, h=16)
        PCT = Z[0:120, 11062:11574].rearrange("p (t g q) -> p t g q", t=2, g=2)
        GTS = Z[:, 11574:11670].rearrange("p (t n) -> p t n", t=2)
        NMX = Z[:, 11670:11734]
        NSUM = Z[:, 11734:11798]
        NGS = Z[:, 11798:11862]
        NST = Z[:, 11862:12102]
        UNITS = [(a_, t, h) for a_ in range(2) for t in range(2) for h in range(16)]

        def nsa_pe(te):
            pe, p = te.eng, te.p
            norm_pe(te, "n.nsa", (0, 1))
            w = te.weights("nsa.c")[:, 0:2048].rearrange("p (k n) -> p k n", k=8)
            for v in range(2):
                te.take(6 + v, "dve", f"nsa.blk{v}")
                for g in range(2):
                    lo = P * v + 64 * g
                    for k in range(KC):
                        pe.matmul(PS[0:64, 6 + v, 256 * g:256 * g + 256], w[:, k, lo:lo + 64], HT[:, k, 0:T],
                                  start=(k == 0), stop=(k == KC - 1))
                        m = pe.matmul(PS[64:128, 6 + v, 256 * g:256 * g + 255], w[:, k, lo:lo + 64], HT[:, k, 1:T],
                                      start=(k == 0), stop=(k == KC - 1))
                p.step(m, f"nsa.c{v}", *(["nsa.c.used"] if v == 1 else []))
            for n in range(2):
                for t in range(2):
                    rows(te, f"nsa.q{n}", t, 2 * n + t, ("dve", f"nsa.qn{n}{t}"), last=t == 1)
            for t in range(2):
                rows(te, "nsa.s", t, 4 + t, ("dve", f"nsa.kn{t}"), last=t == 1)
            w = te.weights("nsa.gt")[:, 0:384].rearrange("p (k n) -> p k n", k=8)
            te.take(6, "dve", "nsa.gb")
            for t in range(2):
                for k in range(KC):
                    m = pe.matmul(PS[:, 6, 64 * t:64 * t + 48], HT[:, k, P * t:P * t + P], w[:, k, :],
                                  start=(k == 0), stop=(k == KC - 1))
            p.step(m, "nsa.gt", "nsa.gt.used")
            for v, n in enumerate("kv"):
                w = te.weights(f"nsa.w1{n}").rearrange("p (c n) -> p c n", c=16)
                te.take((7, 0)[v], "act", f"nsa.hid{v}")
                wait(pe, "dve", f"nsa.blk{v}")
                for l in range(16):
                    m = pe.matmul(PS[0:30, (7, 0)[v], 0:256], BLK[:, v, l, :], w[:, l, :], start=(l == 0), stop=(l == 15))
                p.step(m, f"nsa.hidden{v}", f"nsa.w1{n}.used")
            te.take(7, "dve", "nsa.hidt")
            for v in range(2):
                wait(pe, "act", f"nsa.hid{v}")
                for c in range(2):
                    m = pe.transpose(PS[:, 7, 64 * v + 30 * c:64 * v + 30 * c + 30], HID[0:30, v, P * c:P * c + P], ident[0:30, 0:30])
            p.step(m, "nsa.hidtr")
            w = te.weights("nsa.w2")[:, 0:256].rearrange("p (v c n) -> p v c n", v=2, c=2)
            wait(pe, "dve", "nsa.hidt")
            te.take(7, "dve", "nsa.cmpn")
            for c in range(2):
                pe.matmul(PS[0:30, 7, 0:64], HIDT[:, 0, c, :], w[:, 0, c, :], start=(c == 0), stop=(c == 1))
            for g in range(2):
                for c in range(2):
                    m = pe.matmul(PS[0:15, 7, 64 + 64 * g:128 + 64 * g], HIDT[:, 1, c, 15 * g:15 * g + 15], w[:, 1, c, :],
                                  start=(c == 0), stop=(c == 1))
            p.step(m, "nsa.cmp", "nsa.w2.used")
            for t in range(2):
                for n in range(2):
                    b = 2 * t + n
                    wait(pe, "dve", f"nsa.qn{n}{t}")
                    te.take(b, "dve", f"nsa.qt{n}{t}")
                    for c in range(4):
                        m = pe.transpose(PS[:, b, P * c:P * c + P], NQ[:, t, 512 * n + P * c:512 * n + P * c + P], ident)
                    p.step(m, f"nsa.qtr{n}{t}")
                wait(pe, "dve", f"nsa.kn{t}")
                te.take(4 + t, "dve", f"nsa.kt{t}")
                for c in range(4):
                    m = pe.transpose(PS[:, 4 + t, P * c:P * c + P], NK[:, t, c // 2, c % 2].rearrange("p u e -> p (u e)"), ident)
                p.step(m, f"nsa.ktr{t}")
            wait(pe, "dve", "nsa.cmpn")
            te.take(7, "dve", "nsa.kct")
            p.step(pe.transpose(PS[:, 7, 0:30], KCN, ident[0:30, 0:30]), "nsa.kctr")
            te.take(6, "dve", "nsa.vb")
            for g in range(2):
                m = pe.matmul(PS[0:120, 6, 64 * g:64 * g + 64], cst("cmp_rep", NC_CMP), VC[:, g, :], start=True, stop=True)
            p.step(m, "nsa.vrep")
            wait(pe, "dve", "nsa.kct")
            wait(pe, "dve", "nsa.qt11")
            for t in range(2):
                te.take(t, "dve", f"nsa.sc{t}")
                te.take(2 + t, "dve", f"nsa.sc{t}")
                for h in range(16):
                    o = 64 * (h % 2)
                    m = pe.matmul(PS[:, t + 2 * (h % 2), 15 * (h // 2):15 * (h // 2) + 15], NQT[o:o + 64, h // 2, P * t:P * t + P],
                                  KCT[o:o + 64, 15 * (h // 8):15 * (h // 8) + 15], start=True, stop=True)
                p.step(m, f"nsa.cs{t}")
            for t in range(2):
                wait(pe, "dve", f"nsa.cp{t}")
                te.take(2 + t, "dve", f"nsa.pct{t}")
                for g in range(2):
                    m = pe.transpose(PS[0:120, 2 + t, P * g:P * g + P], SC[:, t, 8 * g:8 * g + 8, :].rearrange("p h n -> p (h n)"), ident)
                p.step(m, f"nsa.pctr{t}")
            wait(pe, "dve", "nsa.vb")
            for t in range(2):
                wait(pe, "dve", f"nsa.pct{t}")
                for g in range(2):
                    te.take(4 + g, "dve", f"nsa.oc{t}{g}")
                    p.step(pe.matmul(PS[:, 4 + g, :], PCT[:, t, g, :], VB[:, g].rearrange("p h e -> p (h e)"), start=True, stop=True),
                           f"nsa.cpv{t}{g}")
            wait(pe, "dve", "nsa.kt1")
            n = len(UNITS)
            for u in range(n + 4):
                if u < n:
                    a_, t, h = UNITS[u]
                    o, kt = 64 * (h % 2), NKT[:, 2 * a_ + h // 8, :]
                    te.take(u % 4, "dve", f"nsa.m{u}")
                    p.step(pe.matmul(PS[:, u % 4, 0:P * (t + 1)], NQT[o:o + 64, h // 2, P * t:P * t + P], kt[o:o + 64, 0:P * (t + 1)],
                                     start=True, stop=True), f"nsa.s{u}")
                if 3 <= u < n + 3:
                    v = u - 3
                    a_, t, h = UNITS[v]
                    wait(pe, "act", f"nsa.e{v}")
                    te.take(4 + v % 2, *(("act" if v % 2 else "dve"), f"nsa.pt{v}"))
                    for c in range(t + 1):
                        m = pe.transpose(PS[:, 4 + v % 2, P * c:P * c + P], NB[:, v % 4, P * c:P * c + P], ident)
                    p.step(m, f"nsa.ptr{v}")
                if u >= 4:
                    v = u - 4
                    a_, t, h = UNITS[v]
                    wait(pe, "act" if v % 2 else "dve", f"nsa.pt{v}")
                    gi = v // 8
                    if v % 8 == 0:
                        te.take(6 + gi % 2, "dve", f"nsa.acc{gi}")
                    for c in range(t + 1):
                        m = pe.matmul(PS[:, 6 + gi % 2, 64 * (h % 8):64 * (h % 8) + 64], NPT[:, v % 2, P * c:P * c + P],
                                      NV[:, c, a_, h // 8, :], start=(c == 0), stop=(c == t))
                    p.step(m, f"nsa.pv{v}")
            for t in range(2):
                wait(pe, "dve", f"nsa.acc{4 + 2 * t + 1}")
                for n in range(2):
                    b = 2 * t + n
                    te.take(b, "dve", f"nsa.yt{t}{n}")
                    for c in range(4):
                        m = pe.transpose(PS[:, b, P * c:P * c + P], NO[:, t, 512 * n + P * c:512 * n + P * c + P], ident)
                    p.step(m, f"nsa.ytr{t}{n}")
            wait(pe, "dve", "nsa.yt11")
            for n in range(2):
                for t in range(2):
                    rows(te, f"nsa.out{n}", t, 4 + 2 * n + t, ("dve", f"nsa.res{n}{t}"), src=YH, last=t == 1)

        def nsa_act(ac, p, after):
            norm_act(ac, p, "n.nsa", (0, 1), after)

            def squares(bank, key, cols=512, rows_=P):
                p.settle()
                p.step(ac.activation(NSQ[0:rows_, 0, 0:cols], PS[0:rows_, bank, 0:cols], ACT.Square), key + ".sq")

            def root(key, o, n, rows_=P):
                wait(ac, "dve", key + ".inv")
                p.step(ac.activation(NST[0:rows_, o:o + n], NST[0:rows_, o:o + n], ACT.Sqrt), key + ".rs")

            for n in range(2):
                for t in range(2):
                    wait(ac, "pe", f"nsa.q{n}.t{t}")
                    squares(2 * n + t, f"nsa.q{n}{t}")
                    root(f"nsa.q{n}{t}", 16 * (2 * n + t), 8)
            for t in range(2):
                wait(ac, "pe", f"nsa.s.t{t}")
                squares(4 + t, f"nsa.k{t}")
                root(f"nsa.k{t}", 64 + 16 * t, 8)
            wait(ac, "dve", "nsa.gb")
            p.step(ac.activation(GTS, GTS, ACT.Sigmoid), "nsa.gates")
            for v in range(2):
                wait(ac, "pe", f"nsa.hidden{v}")
                p.step(ac.activation(HID[0:30, v, :], PS[0:30, (7, 0)[v], 0:256], ACT.Gelu_apprx_tanh), f"nsa.hid{v}")
            wait(ac, "pe", "nsa.cmp")
            squares(7, "nsa.kc", 64, 30)
            root("nsa.kc", 96, 1, 30)
            for t in range(2):
                wait(ac, "dve", f"nsa.sub{t}")
                p.step(ac.activation(SC[:, t], SC[:, t], ACT.Exp), f"nsa.ce{t}")
            for u in range(len(UNITS) + 1):
                if u < len(UNITS):
                    t = UNITS[u][1]
                    wait(ac, "dve", f"nsa.m{u}")
                    p.step(ac.activation(NB[:, u % 4, 0:P * (t + 1)], NB[:, u % 4, 0:P * (t + 1)], ACT.Exp, bias=NMX[:, u:u + 1],
                                         scale=-1.0, accum_out=NSUM[:, u:u + 1]), f"nsa.e{u}")
                v = u - 1
                if v >= 0 and v % 2:
                    t = UNITS[v][1]
                    wait(ac, "pe", f"nsa.ptr{v}")
                    p.step(ac.activation(NPT[:, 1, 0:P * (t + 1)], PS[:, 5, 0:P * (t + 1)], ACT.Copy), f"nsa.pt{v}")

        def nsa_dve(dv, p):
            norm_dve(dv, p, "n.nsa", (0, 1), lambda t: g_nsa)
            for v in range(2):
                wait(dv, "pe", f"nsa.c{v}")
                src = PS[:, 6 + v, :].rearrange("p (g n b c) -> p g n b c", g=2, n=16, b=8)
                for j in range(2):
                    pos = prm(f"pos{'kv'[v]}")[:, 8 * j:8 * j + 8].unsqueeze(1).to_broadcast([P, NC_CMP, 8])
                    for g in range(2):
                        p.step(dv.tensor_tensor(BLK[:, v, 8 * j:8 * j + 8, 15 * g:15 * g + 15].rearrange("p b n -> p n b"),
                                                src[:, g, j:j + NC_CMP, :, 0], pos, ALU.add),
                               *([f"nsa.blk{v}"] if (j, g) == (1, 1) else []))

            def inverse(key, src, ng, o, rows_=P):
                wait(dv, "act", key + ".sq")
                s = NST[0:rows_, o:o + ng]
                p.step(dv.tensor_reduce(s, src.rearrange("p (h e) -> p h e", h=ng), AXX, ALU.add))
                p.settle()
                p.step(dv.tensor_scalar(s, s, 1.0 / 64, EPS, ALU.mult, ALU.add))
                p.settle()
                p.step(dv.reciprocal(s, s), key + ".inv")
                wait(dv, "act", key + ".rs")
                return s

            for n in range(2):
                for t in range(2):
                    r = inverse(f"nsa.q{n}{t}", NSQ[:, 0, :], 8, 16 * (2 * n + t))
                    p.step(dv.tensor_tensor(NQ[:, t, 512 * n:512 * n + 512].rearrange("p (h e) -> p h e", h=8),
                                            PS[:, 2 * n + t, :].rearrange("p (h e) -> p h e", h=8),
                                            r.unsqueeze(2).to_broadcast([P, 8, 64]), ALU.mult), f"nsa.qn{n}{t}")
            for t in range(2):
                r = inverse(f"nsa.k{t}", NSQ[:, 0, :], 8, 64 + 16 * t).rearrange("p (a j g) -> p a j g", a=2, j=2)
                src = PS[:, 4 + t, :].rearrange("p (a j g e) -> p a j g e", a=2, j=2, g=2)
                for a_ in range(2):
                    for u in range(2):
                        p.step(dv.tensor_tensor(NK[:, t, a_, :, u, :], src[:, a_, 0], r[:, a_, 0].unsqueeze(2).to_broadcast([P, 2, 64]),
                                                ALU.mult))
                p.step(dv.tensor_copy(NV[:, t], src[:, :, 1]), f"nsa.kn{t}")
            wait(dv, "pe", "nsa.gt")
            p.step(dv.tensor_tensor(GTS, PS[:, 6, 0:128].rearrange("p (t n) -> p t n", t=2)[:, :, 0:48],
                                    prm("gate_b").unsqueeze(1).to_broadcast([P, 2, 48]), ALU.add), "nsa.gb")
            wait(dv, "pe", "nsa.hidtr")
            p.step(dv.tensor_copy(HIDT, PS[:, 7, 0:128].rearrange("p (v n) -> p v n", v=2)[:, :, 0:60].rearrange("p v (c n) -> p v c n", c=2)),
                   "nsa.hidt")
            r = inverse("nsa.kc", NSQ[0:30, 0, 0:64], 1, 96, 30)
            p.step(dv.tensor_scalar(KCN[:, 0:64], PS[0:30, 7, 0:64], r, None, ALU.mult))
            p.step(dv.tensor_scalar(KCN[:, 64:128], PS[0:30, 7, 0:64], r, None, ALU.mult))
            p.step(dv.tensor_copy(VC, PS[0:15, 7, 64:192].rearrange("p (g e) -> p g e", g=2)), "nsa.cmpn")
            for t in range(2):
                for n in range(2):
                    wait(dv, "pe", f"nsa.qtr{n}{t}")
                    p.step(dv.tensor_scalar(NQT[:, 4 * n:4 * n + 4, P * t:P * t + P], PS[:, 2 * t + n, :].rearrange("p (c t) -> p c t", c=4),
                                            prm("nsa_qg"), 0.125, ALU.mult, ALU.mult), f"nsa.qt{n}{t}")
                wait(dv, "pe", f"nsa.ktr{t}")
                for a_ in range(2):
                    p.step(dv.tensor_scalar(NKT[:, 2 * a_:2 * a_ + 2, P * t:P * t + P],
                                            PS[:, 4 + t, 256 * a_:256 * a_ + 256].rearrange("p (c t) -> p c t", c=2),
                                            prm(f"nsa_kg{1 + a_}"), None, ALU.mult), *([f"nsa.kt{t}"] if a_ else []))
            wait(dv, "pe", "nsa.kctr")
            p.step(dv.tensor_scalar(KCT, PS[:, 7, 0:30], prm("nsa_kg0"), None, ALU.mult), "nsa.kct")
            wait(dv, "pe", "nsa.vrep")
            for g in range(2):
                p.step(dv.tensor_tensor(VB[:, g], PS[0:120, 6, 64 * g:64 * g + 64].unsqueeze(1).to_broadcast([120, 8, 64]),
                                        cst("cmp_own", 120).unsqueeze(2).to_broadcast([120, 8, 64]), ALU.mult),
                       *(["nsa.vb"] if g else []))
            wait(dv, "act", "nsa.gates")
            for t in range(2):
                st = NST[:, 100 + 32 * t:116 + 32 * t]
                gt = GTS[:, t, :].rearrange("p (h j) -> p h j", j=3)
                wait(dv, "pe", f"nsa.cs{t}")
                for u in range(2):
                    p.step(dv.tensor_tensor(SC[:, t, u::2], PS[:, t + 2 * u, 0:120].rearrange("p (h n) -> p h n", h=8),
                                            cst(f"cmp_add{t}").unsqueeze(1).to_broadcast([P, 8, 15]), ALU.add),
                           *([f"nsa.sc{t}"] if u else []))
                p.settle()
                p.step(dv.tensor_reduce(st, SC[:, t], AXX, ALU.max))
                p.settle()
                p.step(dv.tensor_tensor(SC[:, t], SC[:, t], st.unsqueeze(2).to_broadcast([P, 16, 15]), ALU.subtract), f"nsa.sub{t}")
                wait(dv, "act", f"nsa.ce{t}")
                p.step(dv.tensor_reduce(st, SC[:, t], AXX, ALU.add))
                p.settle()
                p.step(dv.reciprocal(st, st))
                p.step(dv.tensor_tensor(SC[:, t], SC[:, t], cst(f"cmp_mul{t}").unsqueeze(1).to_broadcast([P, 16, 15]), ALU.mult))
                p.settle()
                p.step(dv.tensor_tensor(st.unsqueeze(2), st.unsqueeze(2), gt[:, :, 0:1], ALU.mult))
                p.settle()
                p.step(dv.tensor_tensor(SC[:, t], SC[:, t], st.unsqueeze(2).to_broadcast([P, 16, 15]), ALU.mult), f"nsa.cp{t}")
            for t in range(2):
                wait(dv, "pe", f"nsa.pctr{t}")
                p.step(dv.tensor_copy(PCT[:, t], PS[0:120, 2 + t, 0:256].rearrange("p (g q) -> p g q", g=2)), f"nsa.pct{t}")
            for t in range(2):
                for g in range(2):
                    wait(dv, "pe", f"nsa.cpv{t}{g}")
                    p.step(dv.tensor_copy(NO[:, t, 512 * g:512 * g + 512], PS[:, 4 + g, :]), f"nsa.oc{t}{g}")
            p.settle()
            n = len(UNITS)
            for u in range(n + 5):
                if u < n:
                    t = UNITS[u][1]
                    wait(dv, "pe", f"nsa.s{u}")
                    if u >= 4:
                        wait(dv, "pe", f"nsa.ptr{u - 4}")
                    p.step(dv.tensor_tensor_reduce(NB[:, u % 4, 0:P * (t + 1)], PS[:, u % 4, 0:P * (t + 1)],
                                                   cst("causal_add")[:, P * (1 - t):256], -1.0, 3e38, ALU.add, ALU.min, NMX[:, u:u + 1]),
                           f"nsa.m{u}")
                v = u - 3
                if 0 <= v < n and v % 2 == 0:
                    t = UNITS[v][1]
                    wait(dv, "pe", f"nsa.ptr{v}")
                    if v >= 2:
                        wait(dv, "pe", f"nsa.pv{v - 2}")
                    p.step(dv.tensor_copy(NPT[:, 0, 0:P * (t + 1)], PS[:, 4, 0:P * (t + 1)]), f"nsa.pt{v}")
                v = u - 5
                if v >= 0 and v % 8 == 7:
                    gi = v // 8
                    a_, t, h = UNITS[v]
                    g = h // 8
                    gs = NGS[:, 8 * (gi % 2):8 * (gi % 2) + 8]
                    gt = GTS[:, t, :].rearrange("p (h j) -> p h j", j=3)[:, 8 * g:8 * g + 8, 1 + a_]
                    wait(dv, "pe", f"nsa.pv{v}")
                    p.step(dv.reciprocal(gs, NSUM[:, 8 * gi:8 * gi + 8]))
                    p.settle()
                    p.step(dv.tensor_tensor(gs, gs, gt, ALU.mult))
                    p.settle()
                    tmp = NTMP.rearrange("p (h e) -> p h e", h=8)
                    p.step(dv.tensor_tensor(tmp, PS[:, 6 + gi % 2, :].rearrange("p (h e) -> p h e", h=8),
                                            gs.unsqueeze(2).to_broadcast([P, 8, 64]), ALU.mult))
                    p.settle()
                    o = NO[:, t, 512 * g:512 * g + 512]
                    p.step(dv.tensor_tensor(o, o, NTMP, ALU.add), f"nsa.acc{gi}")
                    p.settle()
            for t in range(2):
                for n in range(2):
                    wait(dv, "pe", f"nsa.ytr{t}{n}")
                    p.step(dv.tensor_copy(YH[:, 4 * n:4 * n + 4, P * t:P * t + P], PS[:, 2 * t + n, :].rearrange("p (c t) -> p c t", c=4)),
                           f"nsa.yt{t}{n}")
            for n in range(2):
                for t in range(2):
                    wait(dv, "pe", f"nsa.out{n}.t{t}")
                    xr = X[:, t, 512 * n:512 * n + 512]
                    p.step(dv.tensor_tensor(xr, xr, PS[:, 4 + 2 * n + t, :], ALU.add), f"nsa.res{n}{t}")


        EA = Z[:, 0:2048].rearrange("p (t n) -> p t n", t=4)
        ECG = Z[:, 2048:4096].rearrange("p (c t) -> p c t", c=4)
        EU = Z[:, 4096:4096 + 2064].rearrange("p (c s t) -> p c s t", c=4, s=2)
        EY = Z[:, 6160:10256].rearrange("p (c t) -> p c t", c=8)
        EFX = Z[:, 10256:11280].rearrange("p (b n) -> p b n", b=2)
        RES = Z[:, 0:1024].rearrange("p (b n) -> p b n", b=2)

        def em_pe(te):
            pe, p = te.eng, te.p
            norm_pe(te, "n.mix0", range(4))
            for t in range(4):
                rows(te, "em.a", t, t, ("act", f"em.a{t}"), last=t == 3)

            def columns(nm, b0, who):
                w = te.weights(f"em.{nm}").rearrange("p (k n) -> p k n", k=8)
                for c in range(4):
                    te.take(b0 + c, who, f"em.{nm}{c}")
                    for k in range(KC):
                        m = pe.matmul(PS[:, b0 + c, :], w[:, k, P * c:P * c + P], HT[:, k, :], start=(k == 0), stop=(k == KC - 1))
                    p.step(m, f"em.{nm}{c}", *([f"em.{nm}.used"] if c == 3 else []))

            columns("c", 4, "act")
            columns("h", 0, "dve")
            columns("b", 4, "dve")
            wait(pe, "act", "em.a3")
            for n in range(9):
                if n < 8:
                    s_, g = n // 4, n % 4
                    te.take(n % 2, "act", f"em.fx{n}")
                    for t2 in range(2):
                        m = pe.matmul(PS[:, n % 2, :], EA[:, 2 * s_ + t2, P * g:P * g + P], cst(f"dft{t2}"), start=t2 == 0, stop=t2 == 1)
                    p.step(m, f"em.f{n}")
                if n >= 1:
                    v = n - 1
                    wait(pe, "act", f"em.fx{v}")
                    te.take(2 + v % 2, "dve", f"em.fy{v}")
                    pe.matmul(PS[:, 2 + v % 2, 0:256], cst("dft_cos"), EFX[:, v % 2, 0:256], start=True, stop=False)
                    p.step(pe.matmul(PS[:, 2 + v % 2, 0:256], cst("dft_nsin"), EFX[:, v % 2, 256:512], start=False, stop=True), f"em.g{v}")
            wait(pe, "dve", "em.fy7")
            wait(pe, "dve", "em.b3")
            for n in range(2):
                for t in range(4):
                    rows(te, f"em.out{n}", t, 4 * n + t, ("dve", f"em.res{n}{t}"), src=EY, last=t == 3)

        def em_act(ac, p, after):
            norm_act(ac, p, "n.mix0", range(4), after)
            for t in range(4):
                wait(ac, "pe", f"em.a.t{t}")
                p.step(ac.activation(EA[:, t, :], PS[:, t, :], ACT.Copy), f"em.a{t}")
            for c in range(4):
                wait(ac, "pe", f"em.c{c}")
                p.step(ac.activation(ECG[:, c, :], PS[:, 4 + c, :], ACT.Copy), f"em.c{c}")
            for n in range(8):
                wait(ac, "pe", f"em.f{n}")
                if n >= 2:
                    wait(ac, "pe", f"em.g{n - 2}")
                p.step(ac.activation(EFX[:, n % 2, :], PS[:, n % 2, :], ACT.Copy), f"em.fx{n}")

        def residual(dv, p, tag, who, src, t, n, gate, key, buf):
            xr = X[:, t, 512 * n:512 * n + 512]
            p.step(dv.tensor_tensor(buf, src, gate[:, 512 * n:512 * n + 512], ALU.mult))
            p.settle()
            p.step(dv.tensor_tensor(xr, xr, buf, ALU.add), key)

        def em_dve(dv, p):
            norm_dve(dv, p, "n.mix0", range(4), lambda t: MODC[:, 0, t // 2, 1, :], lambda t: MODC[:, 0, t // 2, 0, :])
            w3 = prm("conv2")
            p.step(dv.memset(EU[:, :, :, 0:1], 0.0))
            p.step(dv.memset(EU[:, :, :, 257:258], 0.0))
            for c in range(4):
                wait(dv, "pe", f"em.h{c}")
                wait(dv, "act", f"em.c{c}")
                p.step(dv.tensor_tensor(EU[:, c, :, 1:257], PS[:, c, :].rearrange("p (s t) -> p s t", s=2),
                                        ECG[:, c, :].rearrange("p (s t) -> p s t", s=2), ALU.mult), f"em.h{c}")
            for c in range(4):
                acc = EY[:, 4 + c, :].rearrange("p (s t) -> p s t", s=2)
                p.settle()
                p.step(dv.tensor_scalar(acc, EU[:, c, :, 0:256], w3[:, c:c + 1], None, ALU.mult))
                for j in range(1, 3):
                    p.settle()
                    p.step(dv.scalar_tensor_tensor(out=acc, in0=EU[:, c, :, j:j + 256], scalar=w3[:, 4 * j + c:4 * j + c + 1], in1=acc,
                                                   op0=ALU.mult, op1=ALU.add))
                p.settle()
                wait(dv, "pe", f"em.b{c}")
                p.step(dv.tensor_tensor(EY[:, 4 + c, :], EY[:, 4 + c, :], PS[:, 4 + c, :], ALU.mult), f"em.b{c}")
            for n in range(8):
                s_, g = n // 4, n % 4
                wait(dv, "pe", f"em.g{n}")
                p.step(dv.tensor_copy(EY[:, g, 256 * s_:256 * s_ + 256], PS[:, 2 + n % 2, 0:256]), f"em.fy{n}")
            dv.wait_ge(gate_loaded[0], 32)
            for n in range(2):
                for t in range(4):
                    wait(dv, "pe", f"em.out{n}.t{t}")
                    residual(dv, p, "em", "pe", PS[:, 4 * n + t, :], t, n, GB[:, t // 2, :], f"em.res{n}{t}", RES[:, t % 2, :])
                    p.settle()

        WQ = Z[:, 0:2048].rearrange("p (t n) -> p t n", t=2)
        WO = WQ
        WQT = Z[:, 2048:4096].rearrange("p (c t) -> p c t", c=8)
        WK = Z[:, 4096:6144].rearrange("p (t g u e) -> p t g u e", t=4, g=4, u=2)
        WB = Z[:, 4096:6144].rearrange("p (b n) -> p b n", b=4)
        WV = Z[:, 6144:7168].rearrange("p (t g e) -> p t g e", t=4, g=4)
        WKT = Z[:, 7168:9216].rearrange("p (g t) -> p g t", g=4)
        WSQ = Z[:, 9216:9728]
        WR = Z[:, 9728:10752].rearrange("p (j n) -> p j n", j=4)
        WPT = Z[:, 9216:10240].rearrange("p (b n) -> p b n", b=2)
        WTMP = Z[:, 10240:10752]
        WN = Z[:, 10752:11264]
        WST = Z[:, 11264:11400]
        WMX = Z[:, 11400:11432]
        WSUM = Z[:, 11432:11464]
        WNS = Z[:, 11464:11480]
        WSE = Z[:, 11480:11512]
        WUNITS = [(t, h) for t in range(2) for h in range(16)]

        def at_pe(te):
            pe, p = te.eng, te.p
            norm_pe(te, "n.mix1", range(4))
            for n in range(2):
                for t in range(2):
                    rows(te, f"at.q{n}", t, 2 * n + t, ("dve", f"at.qn{n}{t}"), last=t == 1)
            for t in range(4):
                rows(te, "at.kv", t, 4 + t, ("dve", f"at.kn{t}"), last=t == 3)
            for t in range(2):
                for n in range(2):
                    b = 2 * t + n
                    wait(pe, "dve", f"at.qr{n}{t}")
                    te.take(b, "dve", f"at.qt{n}{t}")
                    for c in range(4):
                        m = pe.transpose(PS[:, b, P * c:P * c + P], WQ[:, t, 512 * n + P * c:512 * n + P * c + P], ident)
                    p.step(m, f"at.qtr{n}{t}")
            for t in range(4):
                wait(pe, "dve", f"at.kr{t}")
                te.take(4 + t, "act", f"at.kt{t}")
                for g in range(4):
                    m = pe.transpose(PS[:, 4 + t, P * g:P * g + P], WK[:, t, g].rearrange("p u e -> p (u e)"), ident)
                p.step(m, f"at.ktr{t}")
            wait(pe, "act", "at.kt3")
            wait(pe, "dve", "at.qt11")
            n = len(WUNITS)
            for u in range(n + 4):
                if u < n:
                    t, h = WUNITS[u]
                    o = 64 * (h % 2)
                    te.take(u % 4, "dve", f"at.m{u}")
                    p.step(pe.matmul(PS[:, u % 4, :], WQT[o:o + 64, h // 2, P * t:P * t + P], WKT[o:o + 64, h // 4, :],
                                     start=True, stop=True), f"at.s{u}")
                if 3 <= u < n + 3:
                    v = u - 3
                    wait(pe, "act", f"at.e{v}")
                    te.take(4 + v % 2, *(("act" if v % 2 else "dve"), f"at.pt{v}"))
                    for c in range(4):
                        m = pe.transpose(PS[:, 4 + v % 2, P * c:P * c + P], WB[:, v % 4, P * c:P * c + P], ident)
                    p.step(m, f"at.ptr{v}")
                if u >= 4:
                    v = u - 4
                    t, h = WUNITS[v]
                    wait(pe, "act" if v % 2 else "dve", f"at.pt{v}")
                    gi = v // 8
                    if v % 8 == 0:
                        te.take(6 + gi % 2, "dve", f"at.acc{gi}")
                    for c in range(4):
                        m = pe.matmul(PS[:, 6 + gi % 2, 64 * (h % 8):64 * (h % 8) + 64], WPT[:, v % 2, P * c:P * c + P],
                                      WV[:, c, h // 4, :], start=(c == 0), stop=(c == 3))
                    p.step(m, f"at.pv{v}")
            for t in range(2):
                wait(pe, "dve", f"at.acc{2 * t + 1}")
                for n in range(2):
                    b = 2 * t + n
                    te.take(b, "dve", f"at.yt{t}{n}")
                    for c in range(4):
                        m = pe.transpose(PS[:, b, P * c:P * c + P], WO[:, t, 512 * n + P * c:512 * n + P * c + P], ident)
                    p.step(m, f"at.ytr{t}{n}")
            wait(pe, "dve", "at.yt11")
            for n in range(2):
                for t in range(2):
                    rows(te, f"at.out{n}", t, 4 + 2 * n + t, ("dve", f"at.res{n}{t}"), src=YH, last=t == 1)

        def at_act(ac, p, after):
            norm_act(ac, p, "n.mix1", range(4), after)

            def squares(bank, key, cols):
                p.settle()
                p.step(ac.activation(WSQ[:, 0:cols], PS[:, bank, 0:cols], ACT.Square), key + ".sq")
                wait(ac, "dve", key + ".inv")

            for n in range(2):
                for t in range(2):
                    wait(ac, "pe", f"at.q{n}.t{t}")
                    squares(2 * n + t, f"at.q{n}{t}", 512)
                    o = 8 * (2 * n + t)
                    p.step(ac.activation(WST[:, o:o + 8], WST[:, o:o + 8], ACT.Sqrt), f"at.q{n}{t}.rs")
            for t in range(4):
                wait(ac, "pe", f"at.kv.t{t}")
                squares(4 + t, f"at.k{t}", 256)
                o = 32 + 4 * t
                p.step(ac.activation(WST[:, o:o + 4], WST[:, o:o + 4], ACT.Sqrt), f"at.k{t}.rs")
            for t in range(4):
                wait(ac, "pe", f"at.ktr{t}")
                p.step(ac.activation(WKT[:, :, P * t:P * t + P], PS[:, 4 + t, :].rearrange("p (g t) -> p g t", g=4), ACT.Copy), f"at.kt{t}")
            for u in range(len(WUNITS) + 1):
                if u < len(WUNITS):
                    wait(ac, "dve", f"at.m{u}")
                    p.step(ac.activation(WB[:, u % 4, :], WB[:, u % 4, :], ACT.Exp, bias=WMX[:, u:u + 1],
                                         scale=-1.0, accum_out=WSUM[:, u:u + 1]), f"at.e{u}")
                    if u % 8 == 7:
                        wait(ac, "dve", f"at.sk{u // 8}")
                        p.step(ac.activation(WSE[:, u - 7:u + 1], WSE[:, u - 7:u + 1], ACT.Exp), f"at.ske{u // 8}")
                v = u - 1
                if v >= 0 and v % 2:
                    wait(ac, "pe", f"at.ptr{v}")
                    p.step(ac.activation(WPT[:, 1, :], PS[:, 5, :], ACT.Copy), f"at.pt{v}")

        def at_dve(dv, p):
            norm_dve(dv, p, "n.mix1", range(4), lambda t: MODC[:, 1, t // 2, 1, :], lambda t: MODC[:, 1, t // 2, 0, :])
            p.step(dv.tensor_scalar(WNS, prm("sink2"), -1.0, None, ALU.mult))

            def head_norm(key, src, ng, o, g, free):
                wait(dv, "act", key + ".sq")
                s = WST[:, o:o + ng]
                p.step(dv.tensor_reduce(s, WSQ[:, 0:64 * ng].rearrange("p (h e) -> p h e", h=ng), AXX, ALU.add))
                p.settle()
                p.step(dv.tensor_scalar(s, s, 1.0 / 64, EPS, ALU.mult, ALU.add))
                p.settle()
                p.step(dv.reciprocal(s, s), key + ".inv")
                wait(dv, "act", key + ".rs")
                wn = WN[:, 0:64 * ng].rearrange("p (h e) -> p h e", h=ng)
                p.step(dv.tensor_tensor(wn, src.rearrange("p (h e) -> p h e", h=ng), s.unsqueeze(2).to_broadcast([P, ng, 64]), ALU.mult),
                       *([free] if free else []))
                p.settle()
                p.step(dv.tensor_tensor(wn, wn, g.unsqueeze(1).to_broadcast([P, ng, 64]), ALU.mult))
                p.settle()

            def rotate(t, ng, dsts, key):
                x = WN[:, 0:64 * ng].rearrange("p (h a s e) -> p h a s e", h=ng, a=2, s=2)
                b = lambda c: cst(c).rearrange("p (a e) -> p a e", a=2).unsqueeze(1).to_broadcast([P, ng, 2, 16])
                cs, sn = b(f"axcos{t}"), b(f"axsin{t}")
                tm = [WR[:, j, 0:32 * ng].rearrange("p (h a e) -> p h a e", h=ng, a=2) for j in range(4)]
                p.step(dv.tensor_tensor(tm[0], x[:, :, :, 0, :], cs, ALU.mult))
                p.step(dv.tensor_tensor(tm[1], x[:, :, :, 1, :], sn, ALU.mult))
                p.step(dv.tensor_tensor(tm[2], x[:, :, :, 0, :], sn, ALU.mult))
                p.step(dv.tensor_tensor(tm[3], x[:, :, :, 1, :], cs, ALU.mult))
                p.settle()
                for i, dst in enumerate(dsts):
                    d = dst.rearrange("p h (a s e) -> p h a s e", a=2, s=2)
                    p.step(dv.tensor_tensor(d[:, :, :, 0, :], tm[0], tm[1], ALU.subtract))
                    p.step(dv.tensor_tensor(d[:, :, :, 1, :], tm[2], tm[3], ALU.add), *([key] if i == len(dsts) - 1 else []))
                p.settle()

            for n in range(2):
                for t in range(2):
                    head_norm(f"at.q{n}{t}", PS[:, 2 * n + t, :], 8, 8 * (2 * n + t), prm("qg2"), f"at.qn{n}{t}")
                    rotate(t, 8, [WQ[:, t, 512 * n:512 * n + 512].rearrange("p (h e) -> p h e", h=8)], f"at.qr{n}{t}")
            for t in range(4):
                head_norm(f"at.k{t}", PS[:, 4 + t, 0:256], 4, 32 + 4 * t, prm("kg2"), None)
                p.step(dv.tensor_copy(WV[:, t], PS[:, 4 + t, 256:512].rearrange("p (g e) -> p g e", g=4)), f"at.kn{t}")
                if t < 2:
                    rotate(t, 4, [WK[:, t, :, u, :] for u in range(2)], f"at.kr{t}")
                else:
                    for u in range(2):
                        p.step(dv.tensor_copy(WK[:, t, :, u, :], WN[:, 0:256].rearrange("p (h e) -> p h e", h=4)),
                               *([f"at.kr{t}"] if u else []))
                    p.settle()
            for t in range(2):
                for n in range(2):
                    wait(dv, "pe", f"at.qtr{n}{t}")
                    p.step(dv.tensor_scalar(WQT[:, 4 * n:4 * n + 4, P * t:P * t + P], PS[:, 2 * t + n, :].rearrange("p (c t) -> p c t", c=4),
                                            0.125, None, ALU.mult), f"at.qt{n}{t}")
            wait(dv, "pe", "at.ktr3")
            n = len(WUNITS)
            for u in range(n + 5):
                if u < n:
                    t, h = WUNITS[u]
                    wait(dv, "pe", f"at.s{u}")
                    if u >= 4:
                        wait(dv, "pe", f"at.ptr{u - 4}")
                    p.step(dv.tensor_tensor_reduce(WB[:, u % 4, :], PS[:, u % 4, :], cst(f"band{t}"), -1.0, WNS[:, h:h + 1],
                                                   ALU.add, ALU.min, WMX[:, u:u + 1]), f"at.m{u}")
                    if u % 8 == 7:
                        p.settle()
                        p.step(dv.tensor_tensor(WSE[:, u - 7:u + 1], WMX[:, u - 7:u + 1], prm("sink2")[:, h - 7:h + 1], ALU.add),
                               f"at.sk{u // 8}")
                v = u - 3
                if 0 <= v < n and v % 2 == 0:
                    wait(dv, "pe", f"at.ptr{v}")
                    if v >= 2:
                        wait(dv, "pe", f"at.pv{v - 2}")
                    p.step(dv.tensor_copy(WPT[:, 0, :], PS[:, 4, :]), f"at.pt{v}")
                v = u - 5
                if v >= 0 and v % 8 == 7:
                    gi = v // 8
                    t, h = WUNITS[v]
                    g = h // 8
                    gs = WSUM[:, 8 * gi:8 * gi + 8]
                    wait(dv, "pe", f"at.pv{v}")
                    wait(dv, "act", f"at.ske{gi}")
                    p.step(dv.tensor_tensor(gs, gs, WSE[:, 8 * gi:8 * gi + 8], ALU.add))
                    p.settle()
                    p.step(dv.reciprocal(gs, gs))
                    p.settle()
                    p.step(dv.tensor_tensor(WO[:, t, 512 * g:512 * g + 512].rearrange("p (h e) -> p h e", h=8),
                                            PS[:, 6 + gi % 2, :].rearrange("p (h e) -> p h e", h=8),
                                            gs.unsqueeze(2).to_broadcast([P, 8, 64]), ALU.mult), f"at.acc{gi}")
            for t in range(2):
                for n in range(2):
                    wait(dv, "pe", f"at.ytr{t}{n}")
                    p.step(dv.tensor_copy(YH[:, 4 * n:4 * n + 4, P * t:P * t + P], PS[:, 2 * t + n, :].rearrange("p (c t) -> p c t", c=4)),
                           f"at.yt{t}{n}")
            dv.wait_ge(gate_loaded[2], 32)
            for n in range(2):
                for t in range(2):
                    wait(dv, "pe", f"at.out{n}.t{t}")
                    residual(dv, p, "at", "pe", PS[:, 4 + 2 * n + t, :], t, n, GB[:, 0, :], f"at.res{n}{t}", RES[:, t % 2, :])
                    p.settle()


        SLOTS6 = slots + [Z[:, 8192:12288]]
        XM = Z[:, 0:4096].rearrange("p (t n) -> p t n", t=4)
        XB = Z[:, 4096:6144].rearrange("p (b n) -> p b n", b=2)
        XT = Z[:, 6144:7168].rearrange("p (b k r) -> p b k r", b=2, k=8)
        H13 = Z[:, 0:1024].rearrange("p (b n) -> p b n", b=2)
        HS = Z[:, 1024:1536].rearrange("p (b j r) -> p b j r", b=2, j=4)
        HG = Z[:, 1536:2048].rearrange("p (b j r) -> p b j r", b=2, j=4)
        YB = Z[:, 2048:3072].rearrange("p (b n) -> p b n", b=2)
        YG = Z[:, 0:4096].rearrange("p (b k n) -> p b k n", b=2, k=2)

        def ge(eng, s, v):
            if not (isinstance(v, int) and v <= 0):
                eng.wait_ge(s, v)

        class Experts:
            def __init__(self, layer, nt, before):
                self.l, self.nt, self.before = layer, nt, before
                self.J = nt * P // CAP - 1
                L = f"moe{layer}"
                self.L = L
                s = lambda n: sem(f"{L}_{n}")
                self.xb_loaded = [s(f"rows{b}_loaded") for b in range(2)]
                self.w_loaded = [s(f"weights{i}_loaded") for i in range(6)]
                self.t1, self.m1, self.t2, self.m2 = s("rows_turned"), s("hidden_ready"), s("hidden_turned"), s("block_ready")
                self.xt, self.sl, self.y = s("rows_t_copied"), s("silu_done"), s("block_copied")
                self.h, self.g = s("hidden_copied"), s("gated_done")
                self.y_stored = [s(f"block{b}_stored") for b in range(2)]
                self.scattered = s("rows_scattered")
                self.gathered = [[s(f"gathered{b}{k}") for k in range(2)] for b in range(2)]
                self.o_loaded, self.o_stored = s("over_loaded"), s("over_stored")
                self.w = [a[f"w{j}_2"][layer] for j in (1, 3, 2)]
                R = Z[:, 7168:8192]
                self.LG = R[:, 0:36 * nt].rearrange("p (t n) -> p t n", t=nt)
                self.OH = R[:, 144:144 + 64 * nt].rearrange("p (t k e) -> p t k e", t=nt, k=2)
                self.CT = R[:, 400:400 + 32 * nt].rearrange("p (t e) -> p t e", t=nt)
                self.RK = R[:, 528:528 + 32 * nt].rearrange("p (t e) -> p t e", t=nt)
                self.CNT, self.EX, self.END, self.STA = [R[:, 656 + 32 * i:688 + 32 * i] for i in range(4)]
                self.TM = SM[:, 256:256 + 64 * nt].rearrange("p (t k e) -> p t k e", t=nt, k=2)
                self.M8 = R[:, 784:784 + 8 * nt].rearrange("p (t n) -> p t n", t=nt)
                self.IF = R[:, 816:816 + 8 * nt].rearrange("p (t n) -> p t n", t=nt)
                q = lambda i, n: SM[:, 512 + 16 * i:512 + 16 * i + n]
                self.gm, self.gv, self.g0, self.tmp = [q(i, nt) for i in range(4)]
                self.GO = q(4, 4 * nt).rearrange("p (t g) -> p t g", t=nt)
                self.G2 = q(5, 4 * nt).rearrange("p (t g) -> p t g", t=nt)
                self.GW = q(6, 2 * nt).rearrange("p (t k) -> p t k", t=nt)
                self.rk, self.qq, self.st, self.sl_, self.ov = [q(i, 2 * nt).rearrange("p (t k) -> p t k", t=nt) for i in range(7, 12)]
                self.EC = SM[0:1, 256:768].rearrange("p (j e) -> p j e", j=16)
                self.EO = R[0:1, 848:868]

            def load_weights(self, sp, e, b, i, first=False):
                for j in range(3):
                    s_ = 3 * b + j
                    if first:
                        if s_ < RING:
                            if self.before_slots[s_]:
                                freed(sp, self.before_slots[s_])
                        else:
                            wait(sp, "dve", self.before)
                    else:
                        ge(sp, self.m1 if j < 2 else self.m2, i - 1)
                    view = SLOTS6[s_]
                    src = self.w[j][bass.ds(e, 1)].rearrange("a (p k) n -> p (a k n)", p=P)
                    sp.dma_start(view, src).then_inc(self.w_loaded[s_], 16)

            def load_rows(self, sp, b, i):
                ge(sp, self.t1, i - 1)
                sp.dma_start(XB[0:CAP, b, :], xb_dram[bass.ds(CAP * i, CAP), :]).then_inc(self.xb_loaded[b], 16)

            def sp(self, sp):
                self.before_slots = before_moe[self.l]
                for b in range(2):
                    self.load_weights(sp, b, b, b, first=True)
                sp.wait_ge(self.scattered, 16 * 2 * self.nt)
                for b in range(2):
                    self.load_rows(sp, b, b)
                with sp.Fori(1, NE // 2) as it:
                    for b in range(2):
                        i = 2 * it + b
                        self.load_rows(sp, b, i)
                        self.load_weights(sp, i, b, i)
                wait(sp, "dve", self.L + ".over")
                n = sp.value_load(OVF[0:1, 16:17], min_val=0, max_val=15)
                sp.wait_ge(self.m2, NE)
                with sp.If(n > 0):
                    with sp.Fori(0, n) as j:
                        sp.wait_ge(self.m2, NE + j)
                        e = sp.value_load(OVF[0:1, bass.ds(j, 1)], min_val=0, max_val=NE - 1)
                        sp.dma_start(XB[0:CAP, 0, :], xb_dram[bass.ds(CAP * NE + CAP * j, CAP), :]).then_inc(self.o_loaded, 16)
                        for k in range(3):
                            src = self.w[k][bass.ds(e, 1)].rearrange("a (p k) n -> p (a k n)", p=P)
                            sp.dma_start(SLOTS6[k], src).then_inc(self.o_loaded, 16)
                with sp.Else():
                    pass
                sp.wait_ge(self.m2, NE + n)

            def turn_rows(self, pe, b, done):
                pe.matmul(PS[:, b, 0:CAP], XB[0:CAP, b, 0:P], ident[0:CAP, 0:CAP], start=True, stop=True)
                for k in range(1, KC):
                    m = pe.transpose(PS[:, b, CAP * k:CAP * k + CAP], XB[0:CAP, b, P * k:P * k + P], ident[0:CAP, 0:CAP])
                m.then_inc(done, 1)

            def hidden(self, pe, b, done):
                w1, w3 = [SLOTS6[3 * b + j].rearrange("p (k n) -> p k n", k=8) for j in range(2)]
                for k in range(KC):
                    pe.matmul(PS[0:64, 2 + b, :], XT[:, b, k, :], w1[:, k, :], start=k == 0, stop=k == KC - 1)
                    m = pe.matmul(PS[64:128, 2 + b, :], XT[:, b, k, :], w3[:, k, :], start=k == 0, stop=k == KC - 1)
                m.then_inc(done, 1)

            def turn_hidden(self, pe, b, done):
                for j in range(4):
                    m = pe.transpose(PS[:, 4 + b, P * j:P * j + P], H13[:, b, j::4], ident)
                m.then_inc(done, 1)

            def down(self, pe, b, done):
                w2 = SLOTS6[3 * b + 2].rearrange("p (j n) -> p j n", j=4)
                for j in range(4):
                    pe.matmul(PS[0:64, 6 + b, :], HG[:, b, j, :], w2[:, j, 0:512], start=j == 0, stop=j == 3)
                    m = pe.matmul(PS[64:128, 6 + b, :], HG[:, b, j, :], w2[:, j, 512:1024], start=j == 0, stop=j == 3)
                m.then_inc(done, 1)

            def pe_rows(self, pe, it, b):
                i = 2 * it + b
                pe.wait_ge(self.xb_loaded[b], 16 * it + 16)
                ge(pe, self.xt, i - 1)
                self.turn_rows(pe, b, self.t1)

            def pe_down(self, pe, it, b):
                i = 2 * it + b
                pe.wait_ge(self.w_loaded[3 * b + 2], 16 * it + 16)
                pe.wait_ge(self.g, i + 1)
                ge(pe, self.y, i - 1)
                self.down(pe, b, self.m2)

            def pe_block(self, pe, it, b, last=False):
                i = 2 * it + b
                for j in range(2):
                    pe.wait_ge(self.w_loaded[3 * b + j], 16 * it + 16)
                pe.wait_ge(self.xt, i + 1)
                ge(pe, self.h, i - 1)
                self.hidden(pe, b, self.m1)
                if not last:
                    self.pe_rows(pe, it + b, 1 - b)
                if not (isinstance(i, int) and i == 0):
                    self.pe_down(pe, it - 1 + b, 1 - b)
                pe.wait_ge(self.h, i + 1)
                ge(pe, self.g, i - 1)
                self.turn_hidden(pe, b, self.t2)

            def pe(self, te):
                pe, p, L = te.eng, te.p, self.L
                norm_pe(te, f"n.{L}", range(self.nt))
                for t in range(self.nt):
                    for hf in range(2):
                        b = 2 * (t % 2) + hf
                        te.take(b, "act", f"{L}.xm{t}{hf}")
                        for j in range(4):
                            m = pe.transpose(PS[:, b, P * j:P * j + P], HT[:, 4 * hf + j, P * t:P * t + P], ident)
                        p.step(m, f"{L}.xmt{t}{hf}")
                for t in range(self.nt):
                    rows(te, f"{L}.r", t, 4 + t, ("dve", f"{L}.lg{t}"), n=36, last=t == self.nt - 1)
                wait(pe, "dve", f"{L}.ct")
                te.take(0, "dve", f"{L}.rk")
                for t in range(self.nt):
                    for u in range(t + 1):
                        pe.matmul(PS[:, 0, 32 * t:32 * t + 32], cst("before") if u == t else cst("ones")[:, 0:P], self.CT[:, u, :],
                                  start=u == 0, stop=u == t)
                for t in range(self.nt):
                    m = pe.matmul(PS[:, 0, 128:160], cst("ones")[:, 0:P], self.CT[:, t, :], start=t == 0, stop=t == self.nt - 1)
                p.step(m, f"{L}.rank")
                for who in te.banks.values():
                    wait(pe, *who)
                te.banks = {}
                self.pe_rows(pe, 0, 0)
                for b in range(2):
                    self.pe_block(pe, 0, b)
                with pe.Fori(1, NE // 2 - 1) as it:
                    for b in range(2):
                        self.pe_block(pe, it, b)
                for b in range(2):
                    self.pe_block(pe, NE // 2 - 1, b, last=b == 1)
                self.pe_down(pe, NE // 2 - 1, 1)
                for s in (self.xt, self.h, self.g, self.y):
                    pe.wait_ge(s, NE)
                wait(pe, "dve", L + ".over")
                n = pe.value_load(OVF[0:1, 16:17], min_val=0, max_val=15)
                with pe.If(n > 0):
                    with pe.Fori(0, n) as j:
                        pe.wait_ge(self.y, NE + j)
                        pe.wait_ge(self.o_loaded, 64 * j + 64)
                        self.turn_rows(pe, 0, self.t1)
                        pe.wait_ge(self.xt, NE + j + 1)
                        self.hidden(pe, 0, self.m1)
                        pe.wait_ge(self.h, NE + j + 1)
                        self.turn_hidden(pe, 0, self.t2)
                        pe.wait_ge(self.g, NE + j + 1)
                        self.down(pe, 0, self.m2)
                with pe.Else():
                    pass
                pe.wait_ge(self.y, NE + n)

            def copy_rows(self, ac, b, done):
                ac.activation(XT[:, b], PS[:, b, :].rearrange("p (k r) -> p k r", k=8), ACT.Copy).then_inc(done, 1)

            def silu(self, ac, b, done):
                ac.activation(HS[:, b], PS[:, 4 + b, :].rearrange("p (j r) -> p j r", j=4)[:, :, 0:64], ACT.Silu).then_inc(done, 1)

            def store(self, ac, b, row, stored):
                for hf in range(2):
                    ac.dma_start(yb_dram[bass.ds(row, CAP), 512 * hf:512 * hf + 512], YB[64 * hf:64 * hf + 64, b, :]).then_inc(stored, 16)

            def act_rows(self, ac, it, b):
                i = 2 * it + b
                ac.wait_ge(self.t1, i + 1)
                ge(ac, self.m1, i - 1)
                self.copy_rows(ac, b, self.xt)

            def act_out(self, ac, it, b):
                i = 2 * it + b
                ac.wait_ge(self.m2, i + 1)
                ge(ac, self.y_stored[b], 32 * it)
                ac.activation(YB[:, b, :], PS[:, 6 + b, :], ACT.Copy).then_inc(self.y, 1)
                ac.wait_ge(self.y, i + 1)
                self.store(ac, b, CAP * i, self.y_stored[b])

            def act_block(self, ac, it, b, last=False):
                i = 2 * it + b
                if not last:
                    self.act_rows(ac, it + b, 1 - b)
                if not (isinstance(i, int) and i == 0):
                    self.act_out(ac, it - 1 + b, 1 - b)
                ac.wait_ge(self.t2, i + 1)
                ge(ac, self.g, i - 1)
                self.silu(ac, b, self.sl)

            def act(self, ac, p, after):
                L = self.L
                norm_act(ac, p, f"n.{L}", range(self.nt), after)
                for t in range(self.nt):
                    for hf in range(2):
                        wait(ac, "pe", f"{L}.xmt{t}{hf}")
                        p.step(ac.activation(XM[:, t, 512 * hf:512 * hf + 512], PS[:, 2 * (t % 2) + hf, :], ACT.Copy), f"{L}.xm{t}{hf}")
                wait(ac, "dve", f"{L}.gsub")
                p.step(ac.activation(self.G2, self.G2, ACT.Exp), f"{L}.gexp")
                wait(ac, "dve", f"{L}.d")
                p.step(ac.activation(self.g0, self.g0, ACT.Exp), f"{L}.dexp")
                self.act_rows(ac, 0, 0)
                for b in range(2):
                    self.act_block(ac, 0, b)
                with ac.Fori(1, NE // 2 - 1) as it:
                    for b in range(2):
                        self.act_block(ac, it, b)
                for b in range(2):
                    self.act_block(ac, NE // 2 - 1, b, last=b == 1)
                self.act_out(ac, NE // 2 - 1, 1)
                for b in range(2):
                    ac.wait_ge(self.y_stored[b], 32 * (NE // 2))
                wait(ac, "dve", L + ".over")
                n = ac.value_load(OVF[0:1, 16:17], min_val=0, max_val=15)
                with ac.If(n > 0):
                    with ac.Fori(0, n) as j:
                        ac.wait_ge(self.t1, NE + j + 1)
                        self.copy_rows(ac, 0, self.xt)
                        ac.wait_ge(self.t2, NE + j + 1)
                        self.silu(ac, 0, self.sl)
                        ac.wait_ge(self.m2, NE + j + 1)
                        ac.activation(YB[:, 0, :], PS[:, 6, :], ACT.Copy).then_inc(self.y, 1)
                        ac.wait_ge(self.y, NE + j + 1)
                        self.store(ac, 0, CAP * NE + CAP * j, self.o_stored)
                        ac.wait_ge(self.o_stored, 32 * j + 32)
                with ac.Else():
                    pass
                p.step(ac.activation(SM[0:1, 830:831], cst("ones", 1)[:, 0:1], ACT.Copy), f"{L}.stored")

            def dve_block(self, dv, it, b):
                i = 2 * it + b
                dv.wait_ge(self.m1, i + 1)
                ge(dv, self.t2, i - 1)
                dv.tensor_copy(H13[:, b, :], PS[:, 2 + b, :]).then_inc(self.h, 1)
                dv.wait_ge(self.sl, i + 1)
                ge(dv, self.m2, i - 1)
                self.gate(dv, b, self.g)

            def gate(self, dv, b, done):
                dv.tensor_tensor(HG[:, b], HS[:, b], PS[:, 4 + b, :].rearrange("p (j r) -> p j r", j=4)[:, :, 64:128], ALU.mult)\
                    .then_inc(done, 1)

            def dve(self, dv, p):
                L, nt, l = self.L, self.nt, self.l
                norm_dve(dv, p, f"n.{L}", range(nt), lambda t: MODC[:, l, t // 2, 4, :], lambda t: MODC[:, l, t // 2, 3, :])
                p.settle()

                def do(instr, *key):
                    p.step(instr, *key)
                    p.settle()

                iota = cst("iota")
                bc = lambda v, n: v.unsqueeze(2).to_broadcast([P, v.shape[1], n])
                for t in range(nt):
                    wait(dv, "pe", f"{L}.r.t{t}")
                    p.step(dv.tensor_tensor(self.LG[:, t], PS[:, 4 + t, 0:36], prm(f"b_rt{l}"), ALU.add), f"{L}.lg{t}")
                p.settle()
                gl, el = self.LG[:, :, 0:4], self.LG[:, :, 4:36]
                i4 = iota[:, 0:4].unsqueeze(1).to_broadcast([P, nt, 4])
                do(dv.tensor_reduce(self.gm, gl, AXX, ALU.max))
                do(dv.tensor_tensor(self.G2, gl, bc(self.gm, 4), ALU.subtract), f"{L}.gsub")
                do(dv.tensor_tensor(self.GO, gl, bc(self.gm, 4), ALU.is_equal))
                do(dv.tensor_scalar(self.GO, self.GO, -64.0, None, ALU.mult))
                do(dv.tensor_tensor(self.GO, self.GO, i4, ALU.add))
                do(dv.tensor_reduce(self.gm, self.GO, AXX, ALU.min))
                do(dv.tensor_tensor(self.GO, self.GO, bc(self.gm, 4), ALU.is_equal))
                do(dv.tensor_scalar(self.GO, self.GO, 1e30, -1e30, ALU.mult, ALU.add))
                e4 = el.rearrange("p t (g e) -> p t g e", g=4)
                for t in range(nt):
                    do(dv.tensor_tensor(e4[:, t], e4[:, t], bc(self.GO[:, t], 8), ALU.add))
                wait(dv, "act", f"{L}.gexp")
                do(dv.tensor_reduce(self.gv, self.G2, AXX, ALU.add))
                do(dv.reciprocal(self.gv, self.gv))
                for t in range(nt):
                    do(dv.max(self.M8[:, t], el[:, t]))
                    do(dv.max_index(EIDX[:, 8 * t:8 * t + 8], self.M8[:, t], el[:, t]))
                do(dv.tensor_copy(self.IF, EIDX[:, 0:8 * nt].rearrange("p (t n) -> p t n", t=nt)))
                do(dv.tensor_tensor(self.g0.unsqueeze(2), self.M8[:, :, 1:2], self.M8[:, :, 0:1], ALU.subtract), f"{L}.d")
                i32_ = iota.unsqueeze(1).to_broadcast([P, 2, 32])
                for t in range(nt):
                    do(dv.tensor_tensor(self.OH[:, t], bc(self.IF[:, t, 0:2], 32), i32_, ALU.is_equal))
                do(dv.tensor_tensor(self.CT, self.OH[:, :, 0, :], self.OH[:, :, 1, :], ALU.add), f"{L}.ct")
                wait(dv, "act", f"{L}.dexp")
                do(dv.tensor_scalar(self.tmp, self.g0, 1.0, None, ALU.add))
                do(dv.reciprocal(self.tmp, self.tmp))
                do(dv.tensor_tensor(self.tmp, self.tmp, self.gv, ALU.mult))
                do(dv.tensor_copy(self.GW[:, :, 0:1], self.tmp.unsqueeze(2)))
                do(dv.tensor_tensor(self.GW[:, :, 1:2], self.tmp.unsqueeze(2), self.g0.unsqueeze(2), ALU.mult))
                wait(dv, "pe", f"{L}.rank")
                p.step(dv.tensor_copy(self.RK, PS[:, 0, 0:32 * nt].rearrange("p (t e) -> p t e", t=nt)))
                do(dv.tensor_copy(self.CNT, PS[:, 0, 128:160]), f"{L}.rk")
                do(dv.tensor_scalar(self.EX, self.CNT, float(CAP), None, ALU.is_gt))
                for j in range(2, self.J + 1):
                    do(dv.scalar_tensor_tensor(out=self.EX, in0=self.CNT, scalar=float(CAP * j), in1=self.EX, op0=ALU.is_gt, op1=ALU.add))
                do(dv.tensor_tensor_scan(self.END, cst("ones")[:, 0:32], self.EX, 0.0, ALU.mult, ALU.add))
                do(dv.tensor_tensor(self.STA, self.END, self.EX, ALU.subtract))

                def pick(dst, table_):
                    for t in range(nt):
                        row = table_[:, t] if len(table_.shape) == 3 else table_
                        do(dv.tensor_tensor(self.TM[:, t], self.OH[:, t], row.unsqueeze(1).to_broadcast([P, 2, 32]), ALU.mult))
                        do(dv.tensor_reduce(dst[:, t], self.TM[:, t], AXX, ALU.add))

                pick(self.rk, self.RK)
                pick(self.st, self.STA)
                do(dv.tensor_scalar(self.qq, self.rk, float(CAP), None, ALU.is_ge))
                for j in range(2, self.J + 1):
                    do(dv.scalar_tensor_tensor(out=self.qq, in0=self.rk, scalar=float(CAP * j), in1=self.qq, op0=ALU.is_ge, op1=ALU.add))
                do(dv.scalar_tensor_tensor(out=self.rk, in0=self.qq, scalar=-float(CAP), in1=self.rk, op0=ALU.mult, op1=ALU.add))
                do(dv.tensor_tensor(self.st, self.st, self.qq, ALU.add))
                do(dv.tensor_scalar(self.st, self.st, float(NE - 1), None, ALU.add))
                do(dv.tensor_tensor(self.st, self.st, self.IF[:, :, 0:2], ALU.subtract))
                do(dv.tensor_scalar(self.ov, self.qq, 1.0, None, ALU.min))
                do(dv.tensor_tensor(self.st, self.st, self.ov, ALU.mult))
                do(dv.tensor_tensor(self.st, self.st, self.IF[:, :, 0:2], ALU.add))
                do(dv.scalar_tensor_tensor(out=self.sl_, in0=self.st, scalar=float(CAP), in1=self.rk, op0=ALU.mult, op1=ALU.add))
                do(dv.tensor_copy(ROWS[:, 0:2 * nt].rearrange("p (t k) -> p t k", t=nt), self.sl_), f"{L}.rows")
                do(dv.tensor_copy(self.EO[:, 16:17], self.END[0:1, 31:32]))
                wait_gw = self.GW
                do(dv.tensor_copy(GWK[:, 0:2 * nt].rearrange("p (t k) -> p t k", t=nt), wait_gw))
                do(dv.tensor_tensor(self.EC, self.END[0:1].unsqueeze(1).to_broadcast([1, 16, 32]),
                                    iota[0:1, 0:16].unsqueeze(2).to_broadcast([1, 16, 32]), ALU.is_le))
                do(dv.tensor_reduce(self.EO[:, 0:16], self.EC, AXX, ALU.add))
                do(dv.tensor_scalar(self.EO[:, 0:16], self.EO[:, 0:16], float(NE - 1), None, ALU.min))
                do(dv.tensor_copy(OVF[0:1, 0:17], self.EO[:, 0:17]), L + ".over")
                for b in range(2):
                    self.dve_block(dv, 0, b)
                with dv.Fori(1, NE // 2) as it:
                    for b in range(2):
                        self.dve_block(dv, it, b)
                n = dv.value_load(OVF[0:1, 16:17], min_val=0, max_val=15)
                with dv.If(n > 0):
                    with dv.Fori(0, n) as j:
                        dv.wait_ge(self.m1, NE + j + 1)
                        dv.tensor_copy(H13[:, 0, :], PS[:, 2, :]).then_inc(self.h, 1)
                        dv.wait_ge(self.sl, NE + j + 1)
                        self.gate(dv, 0, self.g)
                with dv.Else():
                    pass
                dv.wait_ge(gate_loaded[1 + 2 * l], 32)
                for t in range(nt):
                    y0, y1 = YG[:, t % 2, 0, :], YG[:, t % 2, 1, :]
                    for k in range(2):
                        dv.wait_ge(self.gathered[t % 2][k], 16 * (t // 2) + 16)
                    do(dv.tensor_scalar(y0, y0, GWK[:, 2 * t:2 * t + 1], None, ALU.mult))
                    do(dv.scalar_tensor_tensor(out=y0, in0=y1, scalar=GWK[:, 2 * t + 1:2 * t + 2], in1=y0, op0=ALU.mult, op1=ALU.add))
                    do(dv.tensor_tensor(y0, y0, GB[:, t // 2, :], ALU.mult), f"{L}.comb{t}")
                    do(dv.tensor_tensor(X[:, t, :], X[:, t, :], y0, ALU.add), f"{L}.x{t}", *([L + ".end"] if t == nt - 1 else []))

            def pool(self, po):
                L = self.L
                wait(po, "dve", f"{L}.rows")
                if self.l == 0:
                    po.wait_ge(zeroed, 16 * 16)
                for t in range(self.nt):
                    wait(po, "act", f"{L}.xm{t}1")
                    for k in range(2):
                        po.indirect_dma_start(xb_dram[:, :], bass.IndirectOffsetOnAxis(ap=ROWS[:, 2 * t + k:2 * t + k + 1], axis=0),
                                              XM[:, t, :], None).then_inc(self.scattered, 16)
                wait(po, "act", f"{L}.stored")
                for t in range(self.nt):
                    if t >= 2:
                        wait(po, "dve", f"{L}.x{t - 2}")
                    for k in range(2):
                        po.indirect_dma_start(YG[:, t % 2, k, :], None, yb_dram[:, :],
                                              bass.IndirectOffsetOnAxis(ap=ROWS[:, 2 * t + k:2 * t + k + 1], axis=0))\
                            .then_inc(self.gathered[t % 2][k], 16)

        moe = [Experts(0, 4, "em.res13"), Experts(1, 2, "at.res11")] if on("moe0") else None

        def moe_zero_fill(po):
            zero = Z[:, 11600:11600 + 512]
            po.memset(zero, 0.0).then_inc(zero_set, 1)
            po.wait_ge(zero_set, 1)
            pieces = [xb_dram[256 * q:256 * q + 256] for q in range(12)] + [yb_dram[NE * CAP + 256 * q:][0:256] for q in range(4)]
            for q, rows_ in enumerate(pieces):
                wait(po, "pe", f"ffn0.u{q + 2}")
                po.dma_start(rows_.rearrange("(p n) (h c) -> p (n h) c", p=P, h=2), zero.unsqueeze(1).to_broadcast([P, 4, 512]))\
                    .then_inc(zeroed, 16)

        def gate_rows(po, j, layer, v):
            for r in range(2):
                po.dma_start(GB[:, r, :], mod_dram[layer, r:r + 1, D * v:D * v + D].to_broadcast([P, D])).then_inc(gate_loaded[j], 16)

        @block.sync
        def _(sp):
            sp.dma_start(X[:, 0:2, :], a["x"].rearrange("o (t p) d -> p (o t) d", p=P)).then_inc(x_loaded, 16)
            sp.dma_start(CST[:, 0:P], a["consts"][:, 0:P]).then_inc(ident_loaded, 16)
            sp.dma_start(PRM[:, :], a["params"]).then_inc(params_loaded, 16)
            for i_, (name, parts) in enumerate(stream[:moe_at[0]]):
                load_tile(sp, name, parts)
                if i_ == 1:
                    sp.dma_start(CST[:, P:], a["consts"][:, P:]).then_inc(consts_loaded, 16)
                if i_ == 8:
                    sp.dma_start(X[:, 2:4, :], a["ctx_2"].rearrange("o (t p) d -> p (o t) d", p=P)).then_inc(ctx_loaded, 16)
            if on("moe0"):
                moe[0].sp(sp)
            for name, parts in stream[moe_at[0]:moe_at[1]]:
                load_tile(sp, name, parts)
            if on("out"):
                moe[1].sp(sp)
            wait(sp, "dve", "end")
            sp.dma_start(out.rearrange("o (t p) d -> p (o t) d", p=P), X[:, 0:2, :]).then_inc(out_sem, 16)
            sp.wait_ge(out_sem, 16)

        @block.gpsimd
        def _(po):
            p = Progress("pool", sems["pool"], po, table)
            for i in range(2):
                po.dma_start(GB[:, i, :], a["ple_norm_g"][i:i + 1, :].to_broadcast([P, D])).then_inc(emb_sem[i], 16)
            if on("moe0"):
                moe_zero_fill(po)
            if on("mod"):
                for i in range(2):
                    mod_columns_pool(po, i)
                for i in range(2):
                    po.wait_ge(gates_written[i], 16 * 4)
                wait(po, "dve", "ple1.res")
                gate_rows(po, 0, 0, 2)
            if on("moe0"):
                wait(po, "dve", "em.res13")
                gate_rows(po, 1, 0, 5)
                moe[0].pool(po)
            if on("at"):
                wait(po, "dve", "moe0.end")
                gate_rows(po, 2, 1, 2)
            if on("out"):
                wait(po, "dve", "at.res11")
                gate_rows(po, 3, 1, 5)
                moe[1].pool(po)

        @block.scalar
        def _(ac):
            p = Progress("act", sems["act"], ac, table)
            ac.wait_ge(x_loaded, 16)
            ab_act(ac, p)
            p.step(ac.activation(CSILU[:, :].rearrange("p (r k) -> p k r", r=2), prm("cvec").rearrange("p (k r) -> p k r", k=8), ACT.Silu), "mod.silu")
            if on("ffn0"):
                ffn_act(ac, p, 0, "ab.res11")
            if on("ple0"):
                ple_act(ac, p, 0, "ffn0.res11")
            if on("nsa"):
                nsa_act(ac, p, "ple0.res")
            if on("ffn1"):
                ffn_act(ac, p, 1, "nsa.res11")
            if on("ple1"):
                ple_act(ac, p, 1, "ffn1.res11")
            if on("em"):
                ac.wait_ge(ctx_loaded, 16)
                em_act(ac, p, "ple1.res")
            if on("moe0"):
                moe[0].act(ac, p, "em.res13")
            if on("at"):
                at_act(ac, p, "moe0.end")
            if on("out"):
                moe[1].act(ac, p, "at.res11")

        @block.vector
        def _(dv):
            p = Progress("dve", sems["dve"], dv, table)
            dv.wait_ge(x_loaded, 16)
            dv.wait_ge(params_loaded, 16)
            ab_dve(dv, p)
            p.settle()
            if on("ffn0"):
                ffn_dve(dv, p, 0)
                p.settle()
            if on("ple0"):
                ple_dve(dv, p, 0)
                if on("mod"):
                    mod_columns_dve(dv, p, 0)
                p.settle()
            if on("moe0"):
                dv.wait_ge(zeroed, 16 * 16)
            if on("nsa"):
                nsa_dve(dv, p)
                p.settle()
            if on("ffn1"):
                ffn_dve(dv, p, 1)
                p.settle()
            if on("ple1"):
                ple_dve(dv, p, 1)
                if on("mod"):
                    mod_columns_dve(dv, p, 1)
                p.settle()
            if on("em"):
                dv.wait_ge(ctx_loaded, 16)
                em_dve(dv, p)
            if on("moe0"):
                moe[0].dve(dv, p)
            if on("at"):
                at_dve(dv, p)
            if on("out"):
                moe[1].dve(dv, p)
            p.step(dv.memset(SM[0:1, 822:822 + 1], 0.0), "end")

        @block.tensor
        def _(pe):
            te = Tensor(pe)
            pe.wait_ge(ident_loaded, 16)
            ab_pe(te)
            if on("ffn0"):
                ffn_pe(te, 0)
            if on("ple0"):
                ple_pe(te, 0)
            if on("nsa"):
                nsa_pe(te)
            if on("ffn1"):
                ffn_pe(te, 1)
            if on("ple1"):
                ple_pe(te, 1)
            if on("em"):
                em_pe(te)
            if on("moe0"):
                moe[0].pe(te)
            if on("at"):
                at_pe(te)
            if on("out"):
                moe[1].pe(te)


_INS = None


def kernel(**inputs):
    import concourse.bacc as _bacc
    from concourse.bass_utils import run_bass_kernel_spmd as _run

    table = {}
    params, param_at = param_table(inputs)
    for _ in range(2):
        nc = _bacc.Bacc("TRN2", target_bir_lowering=False, num_devices=1)
        arrays, aps = {}, {}
        for name, v in {**inputs, "consts": CONST, "params": params}.items():
            v = np.ascontiguousarray(v)
            arrays[f"in_{name}"] = v
            aps[name] = nc.dram_tensor(f"in_{name}", v.shape, mybir.dt.from_np(v.dtype), kind="ExternalInput").ap()
        out = nc.dram_tensor("out_0", (1, T, D), F32, kind="ExternalOutput").ap()
        build_program(nc, aps, out, table, param_at)
    r = _run(nc, [arrays], core_ids=[0])
    return r.results[0]["out_0"]
```

```python
from contextlib import ExitStack

import numpy as np
import concourse.bass as bass
from concourse import mybir

F32 = mybir.dt.float32
I32 = mybir.dt.int32
U32 = mybir.dt.uint32
ALU = mybir.AluOpType
ACT = mybir.ActivationFunctionType
AXX = mybir.AxisListType.X

P = 128
D = 1024
T = 256
KC = D // P
EPS = 1e-6
NEG = -1e30
FF = 2816
FC = FF // P
NC_CMP = (T - 32) // 16 + 1
NE = 32
FE = 512
CAP = 64
RING = 5


def constant_table():
    at, cols = {}, []

    def add(name, a):
        a = np.asarray(a, np.float64)
        full = np.zeros((P, a.shape[1]))
        full[:a.shape[0]] = a
        at[name] = (sum(c.shape[1] for c in cols), a.shape[1])
        cols.append(full)

    i = np.arange(P)
    add("ident", np.eye(P))
    add("eps", np.full((P, 1), EPS))
    add("ones", np.ones((P, T)))
    diff = i[None, :] - i[:, None]
    for h in range(4):
        lg = np.log1p(-(2.0 ** (-5.0 - h)))
        diag = np.where(diff >= 0, np.exp(np.where(diff >= 0, diff, 0) * lg), 0.0)
        add(f"decay{h}", np.concatenate([diag, np.exp((diff + P) * lg), diag], 1) / 8)
    c = (diff >= 0) / 8.0
    add("causal_mul", np.concatenate([c, np.full((P, P), 0.125), c], 1))
    add("causal_add", np.concatenate([np.zeros((P, P)), np.where(i[None, :] <= i[:, None], 0.0, NEG)], 1))
    inv = 10000.0 ** (-np.arange(32) / 32.0)
    inv16 = 10000.0 ** (-np.arange(16) / 16.0)
    t = np.arange(T)
    ang = (t[:, None].astype(np.float32) * inv.astype(np.float32)[None, :]).astype(np.float64)
    ax = np.stack([(t // 64)[:, None] * inv16, (t % 64)[:, None] * inv16], 1).reshape(T, 32)
    for j in range(2):
        r = slice(j * P, (j + 1) * P)
        add(f"cos{j}", np.cos(ang[r]))
        add(f"sin{j}", np.sin(ang[r]))
        add(f"axcos{j}", np.cos(ax[r]))
        add(f"axsin{j}", np.sin(ax[r]))
        valid = (16 * np.arange(NC_CMP) + 31)[None, :] <= t[r][:, None]
        add(f"cmp_add{j}", np.where(valid, 0.0, NEG))
        add(f"cmp_mul{j}", valid)
        band = np.where(np.abs(t[None, :] - t[r][:, None]) <= P, 0.0, NEG)
        add(f"band{j}", np.concatenate([band, np.zeros((P, T))], 1))
        w = 2 * np.pi * np.outer(t[r], t) / T
        add(f"dft{j}", np.concatenate([np.cos(w), np.sin(w)], 1) / np.sqrt(T))
    w = 2 * np.pi * np.outer(i, i) / P
    add("dft_cos", np.cos(w) / np.sqrt(P))
    add("dft_nsin", -np.sin(w) / np.sqrt(P))
    r = np.arange(8 * NC_CMP)
    add("cmp_rep", (np.arange(NC_CMP)[:, None] == r[None, :] % NC_CMP))
    add("cmp_own", (r[:, None] // NC_CMP == np.arange(8)[None, :]))
    add("before", (i[:, None] < i[None, :]))
    add("iota", np.broadcast_to(np.arange(CAP), (P, CAP)))
    for h in range(4):
        s = np.zeros((4, P))
        s[h] = 1
        add(f"head{h}", s)
    return np.concatenate(cols, 1).astype(np.float32), at


CONST, CONST_AT = constant_table()


def pk(v):
    return v.reshape(P, -1)


def kp(v):
    return v.reshape(-1, P).T


def two(v):
    return np.concatenate([v, v]).reshape(P, 1)


def column(v):
    return v.reshape(-1, 1)


def param_table(x):
    at, cols, o = {}, [], 0
    items = [("g_ab", pk(x["ab_norm_g"][0])), ("g_nsa", pk(x["nsa_norm_g"][0]))]
    items += [(f"g_ffn{i}", pk(x["ffn_norm_g"][i])) for i in range(2)]
    items += [(f"g_plg{i}", pk(x["ple_gate_norm_g"][i])) for i in range(2)]
    items += [("g_ret", kp(x["ab_ret_norm_g"][0])), ("g_m", kp(x["ab_m_norm_g"][0])),
              ("ab_cw", np.concatenate([kp(x["ab_conv_w"][0, j]) for j in range(4)], 1)),
              ("ab_cb", kp(x["ab_conv_b"][0])), ("ig_b", column(x["ab_ig_b"][0])), ("fg_b", column(x["ab_fg_b"][0]))]
    for i in range(2):
        items += [(f"f_cw{i}{j}", kp(x["ffn_conv_w"][i, j])) for j in range(3)]
        items += [(f"f_cb{i}", kp(x["ffn_conv_b"][i]))]
    items += [("nsa_qg", two(x["nsa_q_norm_g"][0]))]
    items += [(f"nsa_kg{j}", two(x["nsa_k_norm_g"][0, j])) for j in range(3)]
    items += [(f"pos{n}", x[f"nsa_cmp_pos_{n}"][0].reshape(16, P).T) for n in "kv"]
    items += [(f"g_mix2{i}", pk(x["norm_mix_g_2"][i])) for i in range(2)]
    items += [(f"g_ffn2{i}", pk(x["norm_ffn_g_2"][i])) for i in range(2)]
    items += [(f"b_mod{i}{v}", pk(x["b_mod_2"][i, D * v:D * v + D])) for i in range(2) for v in range(6)]
    items += [("cvec", np.stack([pk(x["c_2"][0]), pk(x["c_ctx_2"])], 2).reshape(P, 16))]
    items += [("conv2", np.concatenate([kp(x["conv_w_2"][0, j]) for j in range(3)], 1))]
    every = lambda v: np.broadcast_to(v.reshape(1, -1), (P, v.size))
    items += [("gate_b", every(x["nsa_gate_b"][0])), ("qg2", every(x["q_norm_g_2"][0])), ("kg2", every(x["k_norm_g_2"][0])),
              ("sink2", every(x["sink_logit_2"][0]))]
    items += [(f"b_rt{i}", every(np.concatenate([x["b_router_g_2"][i], x["b_router_e_2"][i]]))) for i in range(2)]
    for name, v in items:
        full = np.zeros((P, v.shape[1]), np.float32)
        full[:v.shape[0]] = v
        at[name] = (o, v.shape[1])
        o += v.shape[1]
        cols.append(full)
    return np.ascontiguousarray(np.concatenate(cols, 1)), at


class Progress:

    def __init__(self, name, sem, eng, table):
        self.name, self.sem, self.eng, self.table, self.n = name, sem, eng, table, 0

    def step(self, instr, *keys):
        instr.then_inc(self.sem, 1)
        self.n += 1
        for k in keys:
            assert (self.name, k) not in self.table or self.table[self.name, k] == self.n, k
            self.table[self.name, k] = self.n
        return instr

    def settle(self):
        self.eng.wait_ge(self.sem, self.n)


def build_program(nc, a, out, table, PARAM_AT, stop=None):
    ctx = ExitStack()
    with ctx:
        def sb(name, cols, dt=F32):
            return ctx.enter_context(nc.sbuf_tensor(name, [P, cols], dt))

        def sem(name):
            return ctx.enter_context(nc.semaphore(name))

        X = sb("resid", 4 * D)[:, :].rearrange("p (t d) -> p t d", t=4)
        HT = sb("normed_t", KC * 512)[:, :].rearrange("p (k t) -> p k t", k=KC)
        XS = sb("scaled", 2 * D)[:, :].rearrange("p (t d) -> p t d", t=2)
        ring = sb("ring", RING * 4096)
        CST = sb("consts", CONST.shape[1])
        Z = sb("arena", 12288)
        GB = sb("rows_bcast", 2 * D)[:, :].rearrange("p (t d) -> p t d", t=2)
        PRM = sb("params", a["params"].shape[1])
        MODC = sb("modulation", 192)[:, :].rearrange("p (l r v k) -> p l r v k", l=2, r=2, v=6)
        CSILU = sb("silu_c", 16)
        SM = sb("small", 1024)
        ZERO = sb("zeros", 64)[:, :]
        PS = ctx.enter_context(nc.psum_tensor("psum", [P, 8, 512], F32))
        slots = [ring[:, i * 4096:(i + 1) * 4096] for i in range(RING)]

        sems = {n: sem(f"{n}_done") for n in ("pe", "act", "dve", "pool")}
        ring_sem = [sem(f"slot{i}_loaded") for i in range(RING)]
        x_loaded, ident_loaded, params_loaded, consts_loaded, ctx_loaded = [
            sem(n + "_loaded") for n in ("x", "identity", "params", "consts", "context")]
        emb_sem = [sem(f"ple_norm_g{i}_loaded") for i in range(2)]
        out_sem = sem("out_written")

        def cst(name, rows=P):
            o, n = CONST_AT[name]
            return CST[0:rows, o:o + n]

        ident = cst("ident")

        def wait(eng, who, key):
            eng.wait_ge(sems[who], table.get((who, key), 1))

        def prm(name, rows=P):
            o, n = PARAM_AT[name]
            return PRM[0:rows, o:o + n]

        g_ab, g_nsa = prm("g_ab"), prm("g_nsa")
        g_ffn = [prm(f"g_ffn{i}") for i in range(2)]
        g_plg = [prm(f"g_plg{i}") for i in range(2)]
        g_ret, g_m, ab_cw, ab_cb = prm("g_ret"), prm("g_m"), prm("ab_cw"), prm("ab_cb")
        ig_b, fg_b = prm("ig_b", 4), prm("fg_b", 4)
        f_cw = [[prm(f"f_cw{i}{j}") for j in range(3)] for i in range(2)]
        f_cb = [prm(f"f_cb{i}") for i in range(2)]

        order = ["ab", "ffn0", "ple0", "nsa", "ffn1", "ple1", "mod", "em", "moe0", "at", "out"]
        on = lambda st: stop is None or order.index(st) <= order.index(stop)

        stream = []

        def wtile(name, *parts):
            stream.append((name, parts))

        def v8(n):
            return lambda s: s[:, 0:8 * n].rearrange("p (k n) -> p k n", k=8)

        def after_norm(name, w, c0, n):
            wtile(name, (v8(n), w.rearrange("(p k) n -> p k n", k=KC)[:, :, c0:c0 + n]))

        def after_heads(name, w, c0, n):
            wtile(name, (v8(n), w.rearrange("(k p) n -> p k n", p=P)[:, :, c0:c0 + n]))

        AB_TILES = [("qk", 0, 512), ("v", 512, 512), ("rg", 1024, 512), ("mqk", 1536, 512),
                    ("mv", 2048, 512), ("mo", 2560, 512), ("if", 3072, 8)]
        for nm, c0, n in AB_TILES:
            after_norm(f"ab.{nm}", a["ab_w_in"][0], c0, n)
        for n in range(2):
            after_heads(f"ab.out{n}", a["ab_w_out"][0], 512 * n, 512)

        MOD_BEHIND = {"up0": (0,), "up1": (1,), "up2": (2,), "down0": (3,), "up4": (4,), "down1": (5,),
                      "up5": (6,), "up6": (7,), "down2": (8,), "up8": (9,), "down3": (10,), "up9": (11,)}
        MOD_SUM_AFTER = {2: 0, 4: 1, 6: 2, 8: 3, 10: 4}

        def mod_tile(i, m_):
            w = a["w_mod_2"][i].rearrange("(p k) n -> p k n", k=KC)
            wtile(f"mod{i}.{m_}", (lambda s: s.rearrange("p (k n) -> p k n", k=4),
                                   w[:, 4 * (m_ % 2):4 * (m_ % 2) + 4, D * (m_ // 2):D * (m_ // 2) + D]))

        def ffn_tiles(i):
            up = a["ffn_w_up"][i].rearrange("(p k) n -> p k n", k=KC)

            def mods(behind):
                for m_ in MOD_BEHIND.get(behind, ()) if on("mod") else ():
                    mod_tile(i, m_)

            for j in range(FC // 2):
                wtile(f"ffn{i}.up{j}",
                      (lambda s: s.rearrange("p (h k n) -> p h k n", h=2, k=8)[:, 0], up[:, :, 256 * j:256 * j + 256]),
                      (lambda s: s.rearrange("p (h k n) -> p h k n", h=2, k=8)[:, 1],
                       up[:, :, FF + 256 * j:FF + 256 * j + 256]))
                mods(f"up{j}")
                for d in ([j // 2 - 1] if j >= 2 and j % 2 == 0 else []) + ([FC // 4] if j == FC // 2 - 1 else []):
                    nk = min(4, FC - 4 * d)
                    wtile(f"ffn{i}.down{d}",
                          (lambda s, nk=nk: s[:, 0:nk * D].rearrange("p (c n) -> p c n", n=D),
                           a["ffn_w_down"][i].rearrange("(c p) n -> p c n", p=P)[:, 4 * d:4 * d + nk, :]))
                    mods(f"down{d}")

        def ple_tiles(i):
            wtile(f"ple{i}.w", (lambda s: s[:, 0:2048].rearrange("p (k n) -> p k n", k=2),
                                a["ple_w"][i].rearrange("(k p) n -> p k n", p=P)),
                  (lambda s: s[:, 2048:2560].rearrange("p (t n) -> p t n", t=2),
                   a["p"][i, 0].rearrange("(t p) n -> p t n", p=P)))
            for n in range(2):
                after_norm(f"ple{i}.gate{n}", a["ple_w_gate"][i], 512 * n, 512)

        if on("ffn0"):
            ffn_tiles(0)
        if on("ple0"):
            ple_tiles(0)
        if on("nsa"):
            for nm, c0, n in [("c", 1024, 256), ("q0", 0, 512), ("q1", 512, 512), ("s", 1280, 512), ("gt", 1792, 48)]:
                after_norm(f"nsa.{nm}", a["nsa_w_in"][0], c0, n)
            for n in "kv":
                wtile(f"nsa.w1{n}", (lambda s: s.rearrange("p (c n) -> p c n", c=16),
                                     a[f"nsa_cmp_w1{n}"][0].rearrange("(c p) n -> p c n", p=P)))
            wtile("nsa.w2", *[((lambda s, j=j: s[:, P * j:P * j + P].rearrange("p (c n) -> p c n", c=2)),
                               a[f"nsa_cmp_w2{n}"][0].rearrange("(c p) n -> p c n", p=P)) for j, n in enumerate("kv")])
            for n in range(2):
                after_heads(f"nsa.out{n}", a["nsa_w_out"][0], 512 * n, 512)
        if on("ffn1"):
            ffn_tiles(1)
        if on("ple1"):
            ple_tiles(1)

        def router_tile(i):
            wtile(f"moe{i}.r", (lambda s: s[:, 0:288].rearrange("p (k n) -> p k n", k=8)[:, :, 0:4],
                                a["w_router_g_2"][i].rearrange("(p k) n -> p k n", k=KC)),
                  (lambda s: s[:, 0:288].rearrange("p (k n) -> p k n", k=8)[:, :, 4:36],
                   a["w_router_e_2"][i].rearrange("(p k) n -> p k n", k=KC)))

        if on("em"):
            for nm, c0 in [("a", 0), ("c", 1024), ("h", 1536), ("b", 512)]:
                after_norm(f"em.{nm}", a["w_in_even_2"][0], c0, 512)
            for n in range(2):
                after_heads(f"em.out{n}", a["w_out_even_2"][0], 512 * n, 512)
        if on("moe0"):
            router_tile(0)
        moe_at = {0: len(stream)}
        if on("at"):
            for nm, c0 in [("q0", 0), ("q1", 512), ("kv", 1024)]:
                after_norm(f"at.{nm}", a["w_qkv_2"][0], c0, 512)
            for n in range(2):
                after_heads(f"at.out{n}", a["w_o_2"][0], 512 * n, 512)
        if on("out"):
            router_tile(1)
        moe_at[1] = len(stream)

        owner_of, slot_of, need = {}, {}, {}
        before_moe = {}
        counts, last = [0] * RING, [None] * RING
        for n, (name, parts) in enumerate(stream):
            s = n % RING
            owner_of[name], slot_of[name] = last[s], s
            counts[s] += 16 * len(parts)
            need[name], last[s] = counts[s], name
            for i in range(2):
                if moe_at[i] == n + 1:
                    before_moe[i] = list(last)

        def W(name):
            return slots[slot_of[name]]

        mod_dram = nc.dram_tensor("mod_rows", (2, 2, 6 * D), F32, kind="Internal").ap()
        yb_dram = nc.dram_tensor("expert_outputs", (48 * CAP, D), F32, kind="Internal").ap()
        zero_set, zeroed = sem("zero_tile_set"), sem("overflow_outputs_zeroed")
        ROWS, OVF, EIDX = sb("row_of_choice", 8, I32), sb("overflow_blocks", 20, I32), sb("expert_index", 32, U32)
        GWK = sb("choice_gates", 8)
        rows_written = [sem(f"mod_rows{i}_written") for i in range(2)]
        modc_loaded = [sem(f"mod_columns{i}_loaded") for i in range(2)]
        gates_written = [sem(f"gate_rows{i}_written") for i in range(2)]
        gate_loaded = [sem(f"gate{j}_loaded") for j in range(4)]
        block = ctx.enter_context(nc.Block())

        def freed(eng, tile):
            wait(eng, "dve" if tile.startswith("mod") else "pe", tile + ".used")

        def load_tile(sp, name, parts):
            if owner_of[name]:
                freed(sp, owner_of[name])
            for view, src in parts:
                sp.dma_start(view(W(name)), src).then_inc(ring_sem[slot_of[name]], 16)

        class Tensor:

            def __init__(self, eng):
                self.eng = eng
                self.p = Progress("pe", sems["pe"], eng, table)
                self.banks = {}

            def take(self, b, who, key):
                if b in self.banks:
                    wait(self.eng, *self.banks[b])
                self.banks[b] = (who, key)

            def weights(self, name):
                self.eng.wait_ge(ring_sem[slot_of[name]], need[name])
                return W(name)

        QKR = Z[:, 0:1024].rearrange("p (t n) -> p t n", t=2)
        RT = Z[:, 1024:2048].rearrange("p (c t) -> p c t", c=4)
        V = Z[:, 2048:3072].rearrange("p (t n) -> p t n", t=2)
        SRG = Z[:, 3072:4096].rearrange("p (t n) -> p t n", t=2)
        MPAD = Z[:, 4096:4096 + 4 * 259].rearrange("p (c t) -> p c t", c=4)
        MQK = Z[:, 5136:6160].rearrange("p (c t) -> p c t", c=4)
        MV = Z[:, 6160:6160 + 1032].rearrange("p (t h e) -> p t h e", t=2, h=4)
        SMO = Z[:, 7200:8224].rearrange("p (t n) -> p t n", t=2)
        RTMP = Z[:, 8224:9248].rearrange("p (j n) -> p j n", j=4)
        PB = Z[:, 9248:9248 + 1536].rearrange("p (b n) -> p b n", b=4)
        EB = Z[:, 10784:10784 + 768].rearrange("p (b n) -> p b n", b=2)
        YH = HT[:, :, 256:512]
        YTOK = XS
        gates4 = SM[0:4, :]

        def norm_table(ac, p):
            p.step(ac.activation(SM[0:1, 824:825], cst("eps", 1), ACT.Sqrt))

        def norm_act_tile(ac, p, name, t):
            if t >= 2:
                wait(ac, "pe", f"{name}.tr{t - 2}1")
            p.step(ac.activation(XS[:, t % 2, :], X[:, t, :], ACT.Square, accum_out=SM[:, 800 + t:801 + t]))
            p.settle()
            p.step(ac.activation(SM[:, 804 + t:805 + t], SM[:, 800 + t:801 + t], ACT.Sqrt, bias=cst("eps"), scale=1.0 / D), f"{name}.rs{t}")

        def norm_act(ac, p, name, tiles, after):
            norm_table(ac, p)
            for t in tiles:
                if after and after(t):
                    wait(ac, "dve", after(t))
                norm_act_tile(ac, p, name, t)

        def norm_scale(dv, p, name, t):
            wait(dv, "act", f"{name}.rs{t}")
            p.step(dv.reciprocal(SM[:, 808 + t:809 + t], SM[:, 804 + t:805 + t]))
            p.settle()
            p.step(dv.tensor_scalar(XS[:, t % 2, :], X[:, t, :], SM[:, 808 + t:809 + t], None, ALU.mult), f"{name}.xs{t}")

        def norm_dve(dv, p, name, tiles, g, shift=None, scaled=()):
            for t in tiles:
                if t not in scaled:
                    norm_scale(dv, p, name, t)
            for t in tiles:
                for hf in range(2):
                    wait(dv, "pe", f"{name}.tr{t}{hf}")
                    dst = HT[:, 4 * hf:4 * hf + 4, P * t:P * t + P]
                    src = PS[:, 2 * (t % 2) + hf, :].rearrange("p (k t) -> p k t", k=4)
                    gb = g(t)[:, 4 * hf:4 * hf + 4].unsqueeze(2).to_broadcast([P, 4, P])
                    last = [f"{name}.ht{t}"] if hf else []
                    p.step(dv.tensor_tensor(dst, src, gb, ALU.mult), f"{name}.bank{t}{hf}", *(last if shift is None else []))
                    if shift is not None:
                        p.settle()
                        sbc = shift(t)[:, 4 * hf:4 * hf + 4].unsqueeze(2).to_broadcast([P, 4, P])
                        p.step(dv.tensor_tensor(dst, dst, sbc, ALU.add), *last)

        def norm_pe(te, name, tiles):
            for t in tiles:
                wait(te.eng, "dve", f"{name}.xs{t}")
                for hf in range(2):
                    b = 2 * (t % 2) + hf
                    te.take(b, "dve", f"{name}.bank{t}{hf}")
                    for j in range(4):
                        m = te.eng.transpose(PS[:, b, P * j:P * j + P], XS[:, t % 2, 4 * hf + j::8], ident)
                    te.p.step(m, f"{name}.tr{t}{hf}")
            te.norm = name

        def rows(te, name, t, bank, reader, n=512, c0=0, src=None, tag=None, last=False, kc=KC, k0=0):
            w = te.weights(name)[:, 0:kc * n].rearrange("p (k n) -> p k n", k=kc)
            te.take(bank, *reader)
            if src is None:
                wait(te.eng, "dve", f"{te.norm}.ht{t}")
                src = HT
            for k in range(kc):
                m = te.eng.matmul(PS[:, bank, 0:n], src[:, k0 + k, P * t:P * t + P], w[:, k, :],
                                  start=(k == 0), stop=(k == kc - 1))
            te.p.step(m, f"{name}.t{t}", *([f"{name}.used"] if last else []))

        def ab_pe(te):
            pe, p = te.eng, te.p
            norm_pe(te, "n.ab", (0, 1))
            for t in range(2):
                rows(te, "ab.qk", t, t, ("dve", f"ab.rot{t}"), last=t == 1)
            for t in range(2):
                rows(te, "ab.v", t, 2 + t, ("act", f"ab.v{t}"), last=t == 1)
            for t in range(2):
                rows(te, "ab.rg", t, 4 + t, ("act", f"ab.rg{t}"), last=t == 1)
            w = te.weights("ab.mqk").rearrange("p (k n) -> p k n", k=8)
            for c in range(4):
                b = 6 + c // 2
                if c % 2 == 0:
                    te.take(b, "act", f"ab.mpad{c + 1}")
                for k in range(KC):
                    m = pe.matmul(PS[:, b, 256 * (c % 2):256 * (c % 2) + 256], w[:, k, P * c:P * c + P], HT[:, k, 0:T],
                                  start=(k == 0), stop=(k == KC - 1))
                p.step(m, f"ab.mqk{c}", *(["ab.mqk.used"] if c == 3 else []))
            for t in range(2):
                wait(pe, "dve", f"ab.rot{t}")
                te.take(t, "act", f"ab.rt{t}")
                for c in range(4):
                    m = pe.transpose(PS[:, t, P * c:P * c + P], QKR[:, t, P * c:P * c + P], ident)
                p.step(m, f"ab.rtr{t}")
            for t in range(2):
                rows(te, "ab.mv", t, 2 + t, ("dve", f"ab.mv{t}"), last=t == 1)
            for t in range(2):
                rows(te, "ab.mo", t, 4 + t, ("act", f"ab.mo{t}"), last=t == 1)
            w = te.weights("ab.if")[:, 0:64].rearrange("p (k n) -> p k n", k=8)
            te.take(6, "act", "ab.fabs")
            for j in range(2):
                for k in range(KC):
                    m = pe.matmul(PS[0:4, 6, 256 * j:256 * j + 256], w[:, k, 4 * j:4 * j + 4], HT[:, k, 0:T],
                                  start=(k == 0), stop=(k == KC - 1))
            p.step(m, "ab.if.done", "ab.if.used")

            def scores(tag, h, src, b, reader):
                o = 64 * (h % 2)
                q, kk = src[o:o + 64, h // 2, :], src[o:o + 64, 2 + h // 2, :]
                te.take(b, *reader)
                pe.matmul(PS[:, b, 0:256], kk[:, 0:P], q, start=True, stop=True)
                p.step(pe.matmul(PS[:, b, 256:384], kk[:, P:T], q[:, P:T], start=True, stop=True), f"{tag}.s{h}")

            wait(pe, "act", "ab.rt1")
            wait(pe, "act", "ab.v1")
            for h in range(5):
                if h < 4:
                    scores("ret", h, RT, h % 2, ("dve", f"ret.p{h}"))
                if h >= 1:
                    g = h - 1
                    wait(pe, "dve", f"ret.p{g}")
                    if g == 0:
                        te.take(6 + 1, "dve", "ret.n1")
                        te.take(2, "dve", "ret.n0")
                    vv = lambda t: V[:, t, P * g:P * g + P]
                    pe.matmul(PS[:, 2, P * g:P * g + P], PB[:, g, 0:P], vv(0), start=True, stop=True)
                    pe.matmul(PS[:, 7, P * g:P * g + P], PB[:, g, P:2 * P], vv(0), start=True, stop=False)
                    m = pe.matmul(PS[:, 7, P * g:P * g + P], PB[:, g, 2 * P:3 * P], vv(1), start=False, stop=True)
                    p.step(m, f"ret.pv{g}")
            wait(pe, "dve", "ml.rows")
            pe.wait_ge(consts_loaded, 16)
            te.take(3, "dve", "ml.cols")
            for t in range(2):
                pe.transpose(PS[:, 3, 4 * t:4 * t + 4], gates4[:, 0 + P * t:P * t + P], ident[0:4, 0:4])
                m = pe.transpose(PS[:, 3, 8 + 4 * t:12 + 4 * t], gates4[:, 256 + P * t:256 + P * t + P], ident[0:4, 0:4])
            p.step(m, "ml.colt")
            wait(pe, "dve", "ml.mqk")
            for h in range(5):
                if h < 4:
                    te.take(4 + h % 2, "dve", f"ml.g{h}")
                    p.step(pe.matmul(PS[:, 4 + h % 2, 0:256], cst(f"head{h}", 4), G4, start=True, stop=True), f"ml.gb{h}")
                    scores("ml", h, MQK, h % 2, ("dve", f"ml.ps{h}"))
                if h >= 1:
                    g = h - 1
                    wait(pe, "dve", f"ml.p{g}")
                    b0, b1 = ((3, 6), (2, 7))[g // 2]
                    if g % 2 == 0:
                        te.take(b0, "dve", f"ml.o0{g // 2}")
                        te.take(b1, "dve", f"ml.o1{g // 2}")
                    o = 129 * (g % 2)
                    pe.matmul(PS[:, b0, o:o + 129], PB[:, g, 0:P], MV[:, 0, g, :], start=True, stop=True)
                    pe.matmul(PS[:, b1, o:o + 129], PB[:, g, P:2 * P], MV[:, 0, g, :], start=True, stop=False)
                    m = pe.matmul(PS[:, b1, o:o + 129], PB[:, g, 2 * P:3 * P], MV[:, 1, g, :], start=False, stop=True)
                    p.step(m, f"ml.pv{g}")
            for j in range(2):
                for t in range(2):
                    wait(pe, "dve", f"ab.y{j}{t}")
                    b = 2 * j + t
                    te.take((0, 1, 4, 5)[b], "dve", f"ab.yt{j}{t}")
                    for c in range(4):
                        m = pe.transpose(PS[:, (0, 1, 4, 5)[b], P * c:P * c + P],
                                         YTOK[:, t, 512 * j + P * c:512 * j + P * c + P], ident)
                    p.step(m, f"ab.ytr{j}{t}")
            wait(pe, "dve", "ab.yt11")
            for n in range(2):
                for t in range(2):
                    rows(te, f"ab.out{n}", t, 2 * n + t, ("dve", f"ab.res{n}{t}"), src=YH, last=t == 1)

        G4 = SM[0:4, 512:768]

        def ab_act(ac, p):
            norm_act(ac, p, "n.ab", (0, 1), None)
            for t in range(2):
                wait(ac, "pe", f"ab.v.t{t}")
                p.step(ac.activation(V[:, t, :], PS[:, 2 + t, :], ACT.Copy), f"ab.v{t}")
            for t in range(2):
                wait(ac, "pe", f"ab.rg.t{t}")
                p.step(ac.activation(SRG[:, t, :], PS[:, 4 + t, :], ACT.Silu), f"ab.rg{t}")
            for c in range(4):
                wait(ac, "pe", f"ab.mqk{c | 1}")
                p.step(ac.activation(MPAD[:, c, 3:259], PS[:, 6 + c // 2, 256 * (c % 2):256 * (c % 2) + 256], ACT.Copy),
                       f"ab.mpad{c}")
            for t in range(2):
                wait(ac, "pe", f"ab.rtr{t}")
                p.step(ac.activation(RT[:, :, P * t:P * t + P], PS[:, t, :].rearrange("p (c t) -> p c t", c=4), ACT.Copy),
                       f"ab.rt{t}")
            for t in range(2):
                wait(ac, "pe", f"ab.mo.t{t}")
                p.step(ac.activation(SMO[:, t, :], PS[:, 4 + t, :], ACT.Sigmoid), f"ab.mo{t}")
            wait(ac, "pe", "ab.if.done")
            ac.wait_ge(params_loaded, 16)
            ac.wait_ge(consts_loaded, 16)
            p.step(ac.activation(gates4[:, 0:256], PS[0:4, 6, 0:256], ACT.Identity, bias=ig_b), "ab.i")
            p.step(ac.activation(G4, PS[0:4, 6, 256:512], ACT.Identity, bias=fg_b), "ab.f")
            p.settle()
            p.step(ac.activation(gates4[:, 256:512], G4, ACT.Abs), "ab.fabs")
            p.settle()
            p.step(ac.activation(gates4[:, 256:512], gates4[:, 256:512], ACT.Exp, scale=-1.0))
            p.settle()
            p.step(ac.activation(gates4[:, 256:512], gates4[:, 256:512], ACT.Ln, bias=cst("ones", 4)[:, 0:1]), "ab.ln")
            for c in range(4):
                wait(ac, "dve", f"ml.conv{c}")
                p.step(ac.activation(MQK[:, c, :], RTMP[:, c, :], ACT.Silu), f"ml.mqk{c}")
            wait(ac, "pe", "ret.pv3")
            p.settle()
            for t in range(2):
                p.step(ac.activation(RTMP[:, 2 * t:2 * t + 2, :].rearrange("p a b -> p (a b)"), PS[:, (2, 7)[t], :], ACT.Square),
                       f"ret.sq{t}")
            wait(ac, "dve", "ml.cols")
            p.step(ac.activation(MC[:, 16:24], MC[:, 8:16], ACT.Exp, scale=-1.0), "ml.em")
            for h in range(4):
                wait(ac, "dve", f"ml.g{h}")
                if h >= 2:
                    wait(ac, "dve", f"ml.p{h - 2}")
                p.step(ac.activation(EB[:, h % 2, 0:256], EB[:, h % 2, 0:256], ACT.Exp, bias=MC[:, h:h + 1], scale=-1.0))
                p.step(ac.activation(EB[:, h % 2, 256:384], EB[:, h % 2, 256:384], ACT.Exp, bias=MC[:, 4 + h:5 + h], scale=-1.0),
                       f"ml.e{h}")
                if h == 1:
                    wait(ac, "dve", "ret.inv")
                    p.step(ac.activation(SR[:, :, 4:8], SR[:, :, 0:4], ACT.Sqrt), "ret.rs")
            norm_table(ac, p)
            wait(ac, "dve", "ml.h")
            p.settle()
            for t in range(2):
                p.step(ac.activation(RTMP[:, 2 * t:2 * t + 2, :].rearrange("p a b -> p (a b)"), HM[:, t, :], ACT.Square),
                       f"ml.sq{t}")
            wait(ac, "dve", "ml.inv")
            p.step(ac.activation(SR[:, :, 4:8], SR[:, :, 0:4], ACT.Sqrt), "ml.rs")

        SR = SM[:, 830:846].rearrange("p (t n) -> p t n", t=2)
        SR2 = SM[:, 846:862].rearrange("p (t n) -> p t n", t=2)
        MC = SM[:, 862:890]
        HM = Z[:, 0:1024].rearrange("p (t n) -> p t n", t=2)

        def bc4(col4, n=P):
            return col4.unsqueeze(2).to_broadcast([P, 4, n])

        def h4(v):
            return v.rearrange("p (h e) -> p h e", h=4)

        def head_norm_sums(dv, p, tag):
            for t in range(2):
                wait(dv, "act", f"{tag}.sq{t}")
                p.step(dv.tensor_reduce(SR2[:, t, 0:4], h4(RTMP[:, 2 * t:2 * t + 2, :].rearrange("p a b -> p (a b)")), AXX, ALU.add))
            p.settle()
            p.step(dv.tensor_scalar(SR2[:, :, 4:8], SR2[:, :, 0:4], 1.0 / P, EPS, ALU.mult, ALU.add))
            p.settle()
            p.step(dv.reciprocal(SR[:, :, 0:4], SR2[:, :, 4:8]), f"{tag}.inv")

        def head_norm_apply(dv, p, tag, src, gate, dst, key):
            wait(dv, "act", f"{tag}.rs")
            for t in range(2):
                p.step(dv.tensor_tensor(h4(dst(t)), h4(src(t)), bc4(SR[:, t, 4:8]), ALU.mult), f"{tag}.n{t}")
                p.settle()
                p.step(dv.tensor_tensor(dst(t), dst(t), gate(t), ALU.mult), f"{key}{t}")

        def ab_dve(dv, p):
            norm_dve(dv, p, "n.ab", (0, 1), lambda t: g_ab)
            dv.wait_ge(consts_loaded, 16)
            for t in range(2):
                wait(dv, "pe", f"ab.qk.t{t}")
                q = PS[:, t, :].rearrange("p (h s e) -> p h s e", h=8, s=2)
                o = QKR[:, t, :].rearrange("p (h s e) -> p h s e", h=8, s=2)
                cs = cst(f"cos{t}").unsqueeze(1).to_broadcast([P, 8, 32])
                sn = cst(f"sin{t}").unsqueeze(1).to_broadcast([P, 8, 32])
                tm = [RTMP[:, j, :].rearrange("p (h e) -> p h e", h=8) for j in range(4)]
                p.settle()
                p.step(dv.tensor_tensor(tm[0], q[:, :, 0, :], cs, ALU.mult))
                p.step(dv.tensor_tensor(tm[1], q[:, :, 1, :], sn, ALU.mult))
                p.step(dv.tensor_tensor(tm[2], q[:, :, 0, :], sn, ALU.mult))
                p.step(dv.tensor_tensor(tm[3], q[:, :, 1, :], cs, ALU.mult))
                p.settle()
                p.step(dv.tensor_tensor(o[:, :, 0, :], tm[0], tm[1], ALU.subtract))
                p.step(dv.tensor_tensor(o[:, :, 1, :], tm[2], tm[3], ALU.add), f"ab.rot{t}")
            p.step(dv.memset(MPAD[:, :, 0:3], 0.0))
            p.step(dv.memset(MV[:, :, :, 128:129], 1.0))
            for t in range(2):
                wait(dv, "pe", f"ab.mv.t{t}")
                p.step(dv.tensor_copy(MV[:, t, :, 0:128], h4(PS[:, 2 + t, :])), f"ab.mv{t}")
            for c in range(4):
                wait(dv, "act", f"ab.mpad{c}")
                p.settle()
                p.step(dv.tensor_scalar(RTMP[:, c, :], MPAD[:, c, 0:256], ab_cw[:, c:c + 1], ab_cb[:, c:c + 1], ALU.mult, ALU.add))
                for j in range(1, 4):
                    p.settle()
                    p.step(dv.scalar_tensor_tensor(out=RTMP[:, c, :], in0=MPAD[:, c, j:j + 256],
                                                   scalar=ab_cw[:, 4 * j + c:4 * j + c + 1], in1=RTMP[:, c, :],
                                                   op0=ALU.mult, op1=ALU.add), *([f"ml.conv{c}"] if j == 3 else []))
            for h in range(4):
                wait(dv, "pe", f"ret.s{h}")
                p.step(dv.tensor_tensor(PB[:, h, :], PS[:, h % 2, 0:384], cst(f"decay{h}"), ALU.mult), f"ret.p{h}")
            wait(dv, "act", "ab.ln")
            lf, LN, A4 = G4, gates4[:, 256:512], gates4[:, 0:256]
            p.step(dv.tensor_scalar(lf, lf, 0.0, None, ALU.min))
            p.settle()
            p.step(dv.tensor_tensor(lf, lf, LN, ALU.subtract))
            p.settle()
            p.step(dv.tensor_tensor_scan(LN, cst("ones", 4), lf, 0.0, ALU.mult, ALU.add))
            p.settle()
            p.step(dv.tensor_tensor(A4, A4, LN, ALU.subtract))
            p.settle()
            p.step(dv.tensor_tensor_scan(G4, A4, A4, 0.0, ALU.max, ALU.max))
            p.settle()
            p.step(dv.tensor_tensor(LN, LN, G4, ALU.add), "ml.rows")
            wait(dv, "pe", "ml.colt")
            p.step(dv.tensor_copy(MC[:, 0:16], PS[:, 3, 0:16]), "ml.cols")
            wait(dv, "act", "ml.mqk3")
            p.step(dv.memset(SM[0:1, 821:821 + 1], 0.0), "ml.mqk")
            p.settle()

            def g_max(h):
                wait(dv, "pe", f"ml.gb{h}")
                if h >= 2:
                    wait(dv, "dve", f"ml.p{h - 2}")
                gb = PS[:, 4 + h % 2, 0:256]
                p.step(dv.tensor_scalar(EB[:, h % 2, 0:256], gb, MC[:, h:h + 1], None, ALU.max))
                p.step(dv.tensor_scalar(EB[:, h % 2, 256:384], gb[:, P:T], MC[:, 4 + h:5 + h], None, ALU.max), f"ml.g{h}")

            g_max(0)
            for h in range(4):
                wait(dv, "pe", f"ml.s{h}")
                if h == 0:
                    wait(dv, "pe", "ret.pv3")
                p.step(dv.tensor_tensor(PB[:, h, :], PS[:, h % 2, 0:384], cst("causal_mul"), ALU.mult), f"ml.ps{h}")
                if h < 3:
                    g_max(h + 1)
                p.settle()
                wait(dv, "act", f"ml.e{h}")
                p.step(dv.tensor_tensor(PB[:, h, :], PB[:, h, :], EB[:, h % 2, :], ALU.mult), f"ml.p{h}")
                if h == 0:
                    head_norm_sums(dv, p, "ret")
                if h == 1:
                    head_norm_apply(dv, p, "ret", lambda t: PS[:, (2, 7)[t], :], lambda t: SRG[:, t, :], lambda t: YTOK[:, t, 0:512], "ab.y0")
            wait(dv, "pe", "ml.pv3")
            wait(dv, "act", "ml.em")

            def mixer_columns(j):
                for t in range(2):
                    wait(dv, "pe", f"ab.ytr{j}{t}")
                    p.step(dv.tensor_tensor(YH[:, 4 * j:4 * j + 4, P * t:P * t + P], h4(PS[:, (0, 1, 4, 5)[2 * j + t], :]),
                                            bc4(g_ret if j == 0 else g_m), ALU.mult), f"ab.yt{j}{t}")

            src = lambda t, j: PS[:, ((3, 6), (2, 7))[j][t], 0:258].rearrange("p (h e) -> p h e", h=2)
            den, ab = SR2[:, :, 0:4], SR2[:, :, 4:8]
            p.settle()
            for t in range(2):
                for j in range(2):
                    p.step(dv.tensor_copy(den[:, t, 2 * j:2 * j + 2].unsqueeze(2), src(t, j)[:, :, 128:129]))
            p.settle()
            p.step(dv.scalar_tensor_tensor(out=ab, in0=den, scalar=-1.0, in1=den, op0=ALU.mult, op1=ALU.max))
            p.settle()
            p.step(dv.tensor_tensor(ab, ab, MC[:, 16:24].rearrange("p (t h) -> p t h", t=2), ALU.max))
            p.settle()
            p.step(dv.reciprocal(den, ab))
            p.settle()
            for t in range(2):
                for j in range(2):
                    p.step(dv.tensor_tensor(HM[:, t, 256 * j:256 * j + 256].rearrange("p (h e) -> p h e", h=2), src(t, j)[:, :, 0:128],
                                            den[:, t, 2 * j:2 * j + 2].unsqueeze(2).to_broadcast([P, 2, P]), ALU.mult),
                           f"ml.o{t}{j}", *(["ml.h"] if (t, j) == (1, 1) else []))
            mixer_columns(0)
            head_norm_sums(dv, p, "ml")
            head_norm_apply(dv, p, "ml", lambda t: HM[:, t, :], lambda t: SMO[:, t, :], lambda t: YTOK[:, t, 512:1024], "ab.y1")
            mixer_columns(1)
            for n in range(2):
                for t in range(2):
                    wait(dv, "pe", f"ab.out{n}.t{t}")
                    xr = X[:, t, 512 * n:512 * n + 512]
                    p.step(dv.tensor_tensor(xr, xr, PS[:, 2 * n + t, :], ALU.add), f"ab.res{n}{t}")
                    if n and on("ffn0"):
                        norm_scale(dv, p, "n.ffn0", t)

        MACC = Z[:, 7168:7168 + 4096].rearrange("p (b r n) -> p b r n", b=2, r=2)

        MOD_PAIRS = [(m_, k) for m_ in range(12) for k in range(4)]

        def mod_products(dv, p, i, c):
            first, end = [-(-len(MOD_PAIRS) * x // FC) for x in (c, c + 1)]
            for m_, k in MOD_PAIRS[first:end]:
                v, b = m_ // 2, m_ // 2 % 2
                name = f"mod{i}.{m_}"
                if k == 0:
                    dv.wait_ge(ring_sem[slot_of[name]], need[name])
                    if m_ % 2 == 0 and v >= 2:
                        wait(dv, "pe", f"mod{i}.sum{v - 2}")
                w = W(name).rearrange("p (k n) -> p k n", k=4)[:, k, :]
                for r in range(2):
                    o = 8 * r + 4 * (m_ % 2) + k
                    acc, sc = MACC[:, b, r, :], CSILU[:, o:o + 1]
                    if m_ % 2 == 0 and k == 0:
                        ins = dv.tensor_scalar(acc, w, sc, None, ALU.mult)
                    else:
                        dv.wait_ge(sems["dve"], p.n - 1)
                        ins = dv.scalar_tensor_tensor(out=acc, in0=w, scalar=sc, in1=acc, op0=ALU.mult, op1=ALU.add)
                    p.step(ins, *([name + ".used"] if (k, r) == (3, 1) else []))

        MROW = Z[:, 5632:6144]

        def mod_sum(te, i, v):
            wait(te.eng, "dve", f"mod{i}.{2 * v + 1}.used")
            te.take(3, "dve", f"mod{i}.row{v}")
            for r in range(2):
                for h in range(2):
                    g = 32 * (2 * r + h)
                    m = te.eng.matmul(PS[g:g + 32, 3, :], cst("ones")[:, 0:32], MACC[:, v % 2, r, 512 * h:512 * h + 512], start=True, stop=True)
            te.p.step(m, f"mod{i}.sum{v}")

        def mod_row_dve(dv, p, i, v):
            wait(dv, "pe", f"mod{i}.sum{v}")
            if v:
                dv.wait_ge(rows_written[i], 32 * v)
            p.step(dv.tensor_copy(MROW, PS[:, 3, :]), f"mod{i}.row{v}")

        def mod_row_act(ac, i, v):
            wait(ac, "dve", f"mod{i}.row{v}")
            for r in range(2):
                ac.dma_start(mod_dram[i, r, D * v:D * v + D].rearrange("(h n) -> h n", h=2), MROW[64 * r:64 * r + 64:32, :])\
                    .then_inc(rows_written[i], 16)

        def mod_columns_pool(po, i):
            po.wait_ge(rows_written[i], 32 * 6)
            for r in range(2):
                po.dma_start(MODC[:, i, r], mod_dram[i, r].rearrange("(v p k) -> p v k", v=6, p=P)).then_inc(modc_loaded[i], 16)
            wait(po, "dve", f"mod{i}.col")
            for v in (2, 5):
                for r in range(2):
                    po.dma_start(mod_dram[i, r, D * v:D * v + D].rearrange("(p k) -> p k", p=P), MODC[:, i, r, v, :])\
                        .then_inc(gates_written[i], 16)

        def mod_columns_dve(dv, p, i):
            dv.wait_ge(modc_loaded[i], 32)
            bias = PRM[:, PARAM_AT[f"b_mod{i}0"][0]:][:, 0:48]
            p.step(dv.tensor_tensor(MODC[:, i], MODC[:, i], bias.rearrange("p (v k) -> p v k", v=6).unsqueeze(1).to_broadcast([P, 2, 6, 8]), ALU.add),
                   f"mod{i}.col")
            p.settle()
            for v, g in ((1, f"g_mix2{i}"), (4, f"g_ffn2{i}")):
                p.step(dv.scalar_tensor_tensor(out=MODC[:, i, :, v, :], in0=MODC[:, i, :, v, :], scalar=1.0,
                                               in1=prm(g).unsqueeze(1).to_broadcast([P, 2, 8]), op0=ALU.add, op1=ALU.mult))

        GT = Z[:, 0:FC * 256].rearrange("p (c t) -> p c t", c=FC)
        AC = Z[:, 6144:6144 + 1024].rearrange("p (b t) -> p b t", b=4)

        def ffn_pe(te, i):
            pe, p = te.eng, te.p
            norm_pe(te, f"n.ffn{i}", (0, 1))
            wait(pe, "dve", f"n.ffn{i}.ht1")

            def down(j):
                w = te.weights(f"ffn{i}.down{j}").rearrange("p (c n) -> p c n", n=D)
                nk = min(4, FC - 4 * j)
                for cc in range(nk):
                    c = 4 * j + cc
                    wait(pe, "dve", f"ffn{i}.g{c}")
                    for t in range(2):
                        for n in range(2):
                            if c == 0:
                                te.take(4 + 2 * n + t, "dve", f"ffn{i}.res{n}{t}")
                            m = pe.matmul(PS[:, 4 + 2 * n + t, :], GT[:, c, P * t:P * t + P], w[:, cc, 512 * n:512 * n + 512],
                                          start=(c == 0), stop=(c == FC - 1))
                p.step(m, f"ffn{i}.down{j}.used")

            for j in range(FC // 2):
                w = te.weights(f"ffn{i}.up{j}").rearrange("p (h k n) -> p h k n", h=2, k=8)
                for cc in range(2):
                    c = 2 * j + cc
                    b = c % 3
                    te.take(b, "dve", f"ffn{i}.g{c}")
                    for hf in range(2):
                        for k in range(KC):
                            m = pe.matmul(PS[:, b, 256 * hf:256 * hf + 256], w[:, hf, k, P * cc:P * cc + P], HT[:, k, 0:T],
                                          start=(k == 0), stop=(k == KC - 1))
                    p.step(m, f"ffn{i}.u{c}", *([f"ffn{i}.up{j}.used"] if cc == 1 else []))
                if on("mod") and j in MOD_SUM_AFTER:
                    mod_sum(te, i, MOD_SUM_AFTER[j])
                if j >= 2 and j % 2 == 0:
                    down(j // 2 - 1)
            if on("mod"):
                mod_sum(te, i, 5)
            down(FC // 4)

        def ffn_act(ac, p, i, after):
            norm_act(ac, p, f"n.ffn{i}", (0, 1), after)
            for c in range(FC + 1):
                if c < FC:
                    wait(ac, "pe", f"ffn{i}.u{c}")
                    if c >= 4:
                        wait(ac, "dve", f"ffn{i}.g{c - 4}")
                    p.step(ac.activation(AC[:, c % 4, :], PS[:, c % 3, 0:256], ACT.Identity, bias=f_cb[i][:, c:c + 1],
                                         scale=f_cw[i][2][:, c:c + 1]), f"ffn{i}.a{c}")
                if c >= 1:
                    wait(ac, "dve", f"ffn{i}.c{c - 1}")
                    p.step(ac.activation(AC[:, (c - 1) % 4, :], AC[:, (c - 1) % 4, :], ACT.Gelu_apprx_tanh), f"ffn{i}.gelu{c - 1}")
                if on("mod") and c % 2 == 0 and (c - 4) // 2 in MOD_SUM_AFTER:
                    mod_row_act(ac, i, MOD_SUM_AFTER[(c - 4) // 2])
            if on("mod"):
                for v in (4, 5):
                    mod_row_act(ac, i, v)

        def ffn_dve(dv, p, i):
            norm_dve(dv, p, f"n.ffn{i}", (0, 1), lambda t: g_ffn[i], scaled=(0, 1))
            wait(dv, "act", "mod.silu")
            for c in range(FC + 1):
                if c < FC:
                    wait(dv, "act", f"ffn{i}.a{c}")
                    acc, a_ = AC[:, c % 4, :], PS[:, c % 3, 0:256]
                    p.step(dv.scalar_tensor_tensor(out=acc[:, 1:256], in0=a_[:, 0:255], scalar=f_cw[i][1][:, c:c + 1],
                                                   in1=acc[:, 1:256], op0=ALU.mult, op1=ALU.add))
                    p.settle()
                    p.step(dv.scalar_tensor_tensor(out=acc[:, 2:256], in0=a_[:, 0:254], scalar=f_cw[i][0][:, c:c + 1],
                                                   in1=acc[:, 2:256], op0=ALU.mult, op1=ALU.add), f"ffn{i}.c{c}")
                if c >= 1:
                    d = c - 1
                    wait(dv, "act", f"ffn{i}.gelu{d}")
                    p.step(dv.tensor_tensor(GT[:, d, :], AC[:, d % 4, :], PS[:, d % 3, 256:512], ALU.mult), f"ffn{i}.g{d}")
                if on("mod") and c % 2 == 1 and (c - 3) // 2 in MOD_SUM_AFTER:
                    mod_row_dve(dv, p, i, MOD_SUM_AFTER[(c - 3) // 2])
                if on("mod") and c < FC:
                    mod_products(dv, p, i, c)
            if on("mod"):
                for v in (4, 5):
                    mod_row_dve(dv, p, i, v)
            wait(dv, "pe", f"ffn{i}.down{FC // 4}.used")
            for n in range(2):
                for t in range(2):
                    xr = X[:, t, 512 * n:512 * n + 512]
                    p.step(dv.tensor_tensor(xr, xr, PS[:, 4 + 2 * n + t, :], ALU.add), f"ffn{i}.res{n}{t}")
                    if n and on(f"ple{i}"):
                        norm_scale(dv, p, f"n.plg{i}", t)

        EE = Z[:, 0:2048].rearrange("p (t n) -> p t n", t=2)
        PT = Z[:, 2048:2560].rearrange("p (k t) -> p k t", k=2)
        SG = Z[:, 2560:4608].rearrange("p (t n) -> p t n", t=2)
        EJ = Z[:, 4608:5632]

        def ple_pe(te, i):
            pe, p = te.eng, te.p
            w = te.weights(f"ple{i}.w")
            ptok = w[:, 2048:2560].rearrange("p (t n) -> p t n", t=2)
            te.take(0, "act", f"ple{i}.pt")
            for t in range(2):
                for k in range(2):
                    m = pe.transpose(PS[:, 0, 256 * k + P * t:256 * k + P * t + P], ptok[:, t, P * k:P * k + P], ident)
            p.step(m, f"ple{i}.ptr")
            wait(pe, "act", f"ple{i}.pt")
            w2 = w[:, 0:2048].rearrange("p (k n) -> p k n", k=2)
            for t in range(2):
                for n in range(2):
                    te.take(4 + 2 * t + n, "dve", f"ple{i}.e{t}")
                    for k in range(2):
                        m = pe.matmul(PS[:, 4 + 2 * t + n, :], PT[:, k, P * t:P * t + P], w2[:, k, 512 * n:512 * n + 512],
                                      start=(k == 0), stop=(k == 1))
                p.step(m, f"ple{i}.e.t{t}", *([f"ple{i}.w.used"] if t == 1 else []))
            norm_pe(te, f"n.plg{i}", (0, 1))
            for n in range(2):
                for t in range(2):
                    rows(te, f"ple{i}.gate{n}", t, 2 * n + t, ("act", f"ple{i}.sg{n}{t}"), last=t == 1)

        def ple_act(ac, p, i, after):
            wait(ac, "pe", f"ple{i}.ptr")
            p.step(ac.activation(PT, PS[:, 0, :].rearrange("p (k t) -> p k t", k=2), ACT.Copy), f"ple{i}.pt")
            norm_act(ac, p, f"n.plg{i}", (0, 1), after)
            for t in range(2):
                wait(ac, "pe", f"ple{i}.e.t{t}")
                p.settle()
                p.step(ac.activation(EJ.rearrange("p (b n) -> p b n", b=2), PS[:, 4 + 2 * t:6 + 2 * t, :], ACT.Square,
                                     accum_out=SM[:, 890 + t:891 + t]), f"ple{i}.sq{t}")
                wait(ac, "dve", f"ple{i}.inv{t}")
                p.step(ac.activation(SM[:, 894 + t:895 + t], SM[:, 892 + t:893 + t], ACT.Sqrt), f"ple{i}.rs{t}")
            for n in range(2):
                for t in range(2):
                    wait(ac, "pe", f"ple{i}.gate{n}.t{t}")
                    p.step(ac.activation(SG[:, t, 512 * n:512 * n + 512], PS[:, 2 * n + t, :], ACT.Sigmoid), f"ple{i}.sg{n}{t}")

        def ple_dve(dv, p, i):
            norm_dve(dv, p, f"n.plg{i}", (0, 1), lambda t: g_plg[i], scaled=(0, 1))
            for t in range(2):
                wait(dv, "act", f"ple{i}.sq{t}")
                p.step(dv.tensor_scalar(SM[:, 896 + t:897 + t], SM[:, 890 + t:891 + t], 1.0 / D, EPS, ALU.mult, ALU.add))
                p.settle()
                p.step(dv.reciprocal(SM[:, 892 + t:893 + t], SM[:, 896 + t:897 + t]), f"ple{i}.inv{t}")
                wait(dv, "act", f"ple{i}.rs{t}")
                dv.wait_ge(emb_sem[i], 16)
                p.step(dv.scalar_tensor_tensor(out=EE[:, t, :].rearrange("p (b n) -> p b n", b=2), in0=PS[:, 4 + 2 * t:6 + 2 * t, :],
                                               scalar=SM[:, 894 + t:895 + t],
                                               in1=GB[:, i, :].rearrange("p (b n) -> p b n", b=2), op0=ALU.mult, op1=ALU.mult),
                       f"ple{i}.e{t}")
            for n in range(2):
                for t in range(2):
                    wait(dv, "act", f"ple{i}.sg{n}{t}")
                    c = slice(512 * n, 512 * n + 512)
                    p.step(dv.tensor_tensor(SG[:, t, c], SG[:, t, c], EE[:, t, c], ALU.mult))
                    p.settle()
                    p.step(dv.tensor_tensor(X[:, t, c], X[:, t, c], SG[:, t, c], ALU.add), f"ple{i}.res{n}{t}")
                    if n and on(("nsa", "em")[i]):
                        norm_scale(dv, p, ("n.nsa", "n.mix0")[i], t)


        NQ = Z[:, 0:2048].rearrange("p (t n) -> p t n", t=2)
        NO = NQ
        NQT = Z[:, 2048:4096].rearrange("p (c t) -> p c t", c=8)
        NK = Z[:, 4096:5120].rearrange("p (t a g u e) -> p t a g u e", t=2, a=2, g=2, u=2)
        NB = Z[:, 4096:5120].rearrange("p (b n) -> p b n", b=4)
        NV = Z[:, 5120:5632].rearrange("p (t a g e) -> p t a g e", t=2, a=2, g=2)
        NKT = Z[:, 5632:6656].rearrange("p (c t) -> p c t", c=4)
        NSQ = Z[:, 6656:7680].rearrange("p (b n) -> p b n", b=2)
        NPT = Z[:, 6656:7168].rearrange("p (b n) -> p b n", b=2)
        NTMP = Z[:, 7168:7680]
        BLK = Z[:, 7680:8640].rearrange("p (v l c) -> p v l c", v=2, l=16)
        HID = Z[:, 8640:9152].rearrange("p (v n) -> p v n", v=2)
        HIDT = Z[:, 9152:9272].rearrange("p (v c n) -> p v c n", v=2, c=2)
        KCN = Z[0:30, 9272:9400]
        KCT = SM[:, 256:316].rearrange("p (g u n) -> p g u n", g=2, u=2)
        VC = Z[0:NC_CMP, 9430:9558].rearrange("p (g e) -> p g e", g=2)
        VB = Z[0:120, 9558:10582].rearrange("p (g h e) -> p g h e", g=2, h=8)
        SC = Z[:, 10582:11062].rearrange("p (t h n) -> p t h n", t=2, h=16)
        PCT = Z[0:120, 11062:11574].rearrange("p (t g q) -> p t g q", t=2, g=2)
        GTS = Z[:, 11574:11670].rearrange("p (t n) -> p t n", t=2)
        NMX = Z[:, 11670:11734]
        NSUM = Z[:, 11734:11798]
        NGS = Z[:, 11798:11862]
        NST = Z[:, 11862:12102]
        UNITS = [(a_, t, h) for a_ in range(2) for t in range(2) for h in range(16)]

        def nsa_pe(te):
            pe, p = te.eng, te.p
            norm_pe(te, "n.nsa", (0, 1))
            wait(te.eng, "dve", "n.nsa.ht1")
            w = te.weights("nsa.c")[:, 0:2048].rearrange("p (k n) -> p k n", k=8)
            for v in range(2):
                te.take(6 + v, "dve", f"nsa.blk{v}")
                for g in range(2):
                    lo = P * v + 64 * g
                    for k in range(KC):
                        pe.matmul(PS[0:64, 6 + v, 256 * g:256 * g + 256], w[:, k, lo:lo + 64], HT[:, k, 0:T],
                                  start=(k == 0), stop=(k == KC - 1))
                        m = pe.matmul(PS[64:128, 6 + v, 256 * g:256 * g + 255], w[:, k, lo:lo + 64], HT[:, k, 1:T],
                                      start=(k == 0), stop=(k == KC - 1))
                p.step(m, f"nsa.c{v}", *(["nsa.c.used"] if v == 1 else []))
            for n in range(2):
                for t in range(2):
                    rows(te, f"nsa.q{n}", t, 2 * n + t, ("dve", f"nsa.qn{n}{t}"), last=t == 1)
            for t in range(2):
                rows(te, "nsa.s", t, 4 + t, ("dve", f"nsa.kn{t}"), last=t == 1)
            w = te.weights("nsa.gt")[:, 0:384].rearrange("p (k n) -> p k n", k=8)
            te.take(6, "dve", "nsa.gb")
            for t in range(2):
                for k in range(KC):
                    m = pe.matmul(PS[:, 6, 64 * t:64 * t + 48], HT[:, k, P * t:P * t + P], w[:, k, :],
                                  start=(k == 0), stop=(k == KC - 1))
            p.step(m, "nsa.gt", "nsa.gt.used")
            for t in range(2):
                for n in range(2):
                    b = 2 * t + n
                    wait(pe, "dve", f"nsa.qn{n}{t}")
                    te.take(b, "dve", f"nsa.qt{n}{t}")
                    for c in range(4):
                        m = pe.transpose(PS[:, b, P * c:P * c + P], NQ[:, t, 512 * n + P * c:512 * n + P * c + P], ident)
                    p.step(m, f"nsa.qtr{n}{t}")
                wait(pe, "dve", f"nsa.kn{t}")
                te.take(4 + t, "dve", f"nsa.kt{t}")
                for c in range(4):
                    m = pe.transpose(PS[:, 4 + t, P * c:P * c + P], NK[:, t, c // 2, c % 2].rearrange("p u e -> p (u e)"), ident)
                p.step(m, f"nsa.ktr{t}")
            for v, n in enumerate("kv"):
                w = te.weights(f"nsa.w1{n}").rearrange("p (c n) -> p c n", c=16)
                te.take((7, 0)[v], "act", f"nsa.hid{v}")
                wait(pe, "dve", f"nsa.blk{v}")
                for l in range(16):
                    m = pe.matmul(PS[0:30, (7, 0)[v], 0:256], BLK[:, v, l, :], w[:, l, :], start=(l == 0), stop=(l == 15))
                p.step(m, f"nsa.hidden{v}", f"nsa.w1{n}.used")
            te.take(7, "dve", "nsa.hidt")
            for v in range(2):
                wait(pe, "act", f"nsa.hid{v}")
                for c in range(2):
                    m = pe.transpose(PS[:, 7, 64 * v + 30 * c:64 * v + 30 * c + 30], HID[0:30, v, P * c:P * c + P], ident[0:30, 0:30])
            p.step(m, "nsa.hidtr")
            w = te.weights("nsa.w2")[:, 0:256].rearrange("p (v c n) -> p v c n", v=2, c=2)
            wait(pe, "dve", "nsa.hidt")
            te.take(7, "dve", "nsa.cmpn")
            for c in range(2):
                pe.matmul(PS[0:30, 7, 0:64], HIDT[:, 0, c, :], w[:, 0, c, :], start=(c == 0), stop=(c == 1))
            for g in range(2):
                for c in range(2):
                    m = pe.matmul(PS[0:15, 7, 64 + 64 * g:128 + 64 * g], HIDT[:, 1, c, 15 * g:15 * g + 15], w[:, 1, c, :],
                                  start=(c == 0), stop=(c == 1))
            p.step(m, "nsa.cmp", "nsa.w2.used")
            wait(pe, "dve", "nsa.cmpn")
            te.take(7, "dve", "nsa.kct")
            p.step(pe.transpose(PS[:, 7, 0:30], KCN, ident[0:30, 0:30]), "nsa.kctr")
            te.take(6, "dve", "nsa.vb")
            for g in range(2):
                m = pe.matmul(PS[0:120, 6, 64 * g:64 * g + 64], cst("cmp_rep", NC_CMP), VC[:, g, :], start=True, stop=True)
            p.step(m, "nsa.vrep")
            wait(pe, "dve", "nsa.kct")
            wait(pe, "dve", "nsa.qt11")
            for t in range(2):
                te.take(t, "dve", f"nsa.sc{t}")
                for c in range(8):
                    m = pe.matmul(PS[:, t, 30 * c:30 * c + 30], NQT[:, c, P * t:P * t + P], KCT[:, c // 4].rearrange("p u n -> p (u n)"),
                                  start=True, stop=True)
                p.step(m, f"nsa.cs{t}")
            for t in range(2):
                wait(pe, "dve", f"nsa.cp{t}")
                te.take(2 + t, "dve", f"nsa.pct{t}")
                for g in range(2):
                    m = pe.transpose(PS[0:120, 2 + t, P * g:P * g + P], SC[:, t, 8 * g:8 * g + 8, :].rearrange("p h n -> p (h n)"), ident)
                p.step(m, f"nsa.pctr{t}")
            wait(pe, "dve", "nsa.vb")
            for t in range(2):
                wait(pe, "dve", f"nsa.pct{t}")
                for g in range(2):
                    te.take(4 + g, "dve", f"nsa.oc{t}{g}")
                    p.step(pe.matmul(PS[:, 4 + g, :], PCT[:, t, g, :], VB[:, g].rearrange("p h e -> p (h e)"), start=True, stop=True),
                           f"nsa.cpv{t}{g}")
            wait(pe, "dve", "nsa.kt1")
            n = len(UNITS)
            for u in range(n + 4):
                if u < n:
                    a_, t, h = UNITS[u]
                    o, kt = 64 * (h % 2), NKT[:, 2 * a_ + h // 8, :]
                    te.take(u % 4, "dve", f"nsa.m{u}")
                    p.step(pe.matmul(PS[:, u % 4, 0:P * (t + 1)], NQT[o:o + 64, h // 2, P * t:P * t + P], kt[o:o + 64, 0:P * (t + 1)],
                                     start=True, stop=True), f"nsa.s{u}")
                if 3 <= u < n + 3:
                    v = u - 3
                    a_, t, h = UNITS[v]
                    wait(pe, "act", f"nsa.e{v}")
                    te.take(4 + v % 2, *(("act" if v % 2 else "dve"), f"nsa.pt{v}"))
                    for c in range(t + 1):
                        m = pe.transpose(PS[:, 4 + v % 2, P * c:P * c + P], NB[:, v % 4, P * c:P * c + P], ident)
                    p.step(m, f"nsa.ptr{v}")
                if u >= 4:
                    v = u - 4
                    a_, t, h = UNITS[v]
                    wait(pe, "act" if v % 2 else "dve", f"nsa.pt{v}")
                    gi = v // 8
                    if v % 8 == 0:
                        te.take(6 + gi % 2, "dve", f"nsa.acc{gi}")
                    for c in range(t + 1):
                        m = pe.matmul(PS[:, 6 + gi % 2, 64 * (h % 8):64 * (h % 8) + 64], NPT[:, v % 2, P * c:P * c + P],
                                      NV[:, c, a_, h // 8, :], start=(c == 0), stop=(c == t))
                    p.step(m, f"nsa.pv{v}")
            for t in range(2):
                wait(pe, "dve", f"nsa.acc{4 + 2 * t + 1}")
                for n in range(2):
                    b = 2 * t + n
                    te.take(b, "dve", f"nsa.yt{t}{n}")
                    for c in range(4):
                        m = pe.transpose(PS[:, b, P * c:P * c + P], NO[:, t, 512 * n + P * c:512 * n + P * c + P], ident)
                    p.step(m, f"nsa.ytr{t}{n}")
            wait(pe, "dve", "nsa.yt11")
            for n in range(2):
                for t in range(2):
                    rows(te, f"nsa.out{n}", t, 4 + 2 * n + t, ("dve", f"nsa.res{n}{t}"), src=YH, last=t == 1)

        def nsa_act(ac, p, after):
            norm_act(ac, p, "n.nsa", (0, 1), after)

            def squares(bank, key, cols=512, rows_=P):
                p.settle()
                p.step(ac.activation(NSQ[0:rows_, 0, 0:cols], PS[0:rows_, bank, 0:cols], ACT.Square), key + ".sq")

            def root(key, o, n, rows_=P):
                wait(ac, "dve", key + ".inv")
                p.step(ac.activation(NST[0:rows_, o:o + n], NST[0:rows_, o:o + n], ACT.Sqrt), key + ".rs")

            for n in range(2):
                for t in range(2):
                    wait(ac, "pe", f"nsa.q{n}.t{t}")
                    squares(2 * n + t, f"nsa.q{n}{t}")
                    root(f"nsa.q{n}{t}", 16 * (2 * n + t), 8)
            for t in range(2):
                wait(ac, "pe", f"nsa.s.t{t}")
                squares(4 + t, f"nsa.k{t}")
                root(f"nsa.k{t}", 64 + 16 * t, 8)
            wait(ac, "dve", "nsa.gb")
            p.step(ac.activation(GTS, GTS, ACT.Sigmoid), "nsa.gates")
            for v in range(2):
                wait(ac, "pe", f"nsa.hidden{v}")
                p.step(ac.activation(HID[0:30, v, :], PS[0:30, (7, 0)[v], 0:256], ACT.Gelu_apprx_tanh), f"nsa.hid{v}")
            wait(ac, "pe", "nsa.cmp")
            squares(7, "nsa.kc", 64, 30)
            root("nsa.kc", 96, 1, 30)
            for t in range(2):
                wait(ac, "dve", f"nsa.sub{t}")
                p.step(ac.activation(SC[:, t], SC[:, t], ACT.Exp), f"nsa.ce{t}")
            for u in range(len(UNITS) + 1):
                if u < len(UNITS):
                    t = UNITS[u][1]
                    wait(ac, "dve", f"nsa.m{u}")
                    p.step(ac.activation(NB[:, u % 4, 0:P * (t + 1)], NB[:, u % 4, 0:P * (t + 1)], ACT.Exp, bias=NMX[:, u:u + 1],
                                         scale=-1.0, accum_out=NSUM[:, u:u + 1]), f"nsa.e{u}")
                v = u - 1
                if v >= 0 and v % 2:
                    t = UNITS[v][1]
                    wait(ac, "pe", f"nsa.ptr{v}")
                    p.step(ac.activation(NPT[:, 1, 0:P * (t + 1)], PS[:, 5, 0:P * (t + 1)], ACT.Copy), f"nsa.pt{v}")

        def nsa_dve(dv, p):
            p.step(dv.memset(KCT, 0.0))
            norm_dve(dv, p, "n.nsa", (0, 1), lambda t: g_nsa, scaled=(0, 1))
            for v in range(2):
                wait(dv, "pe", f"nsa.c{v}")
                src = PS[:, 6 + v, :].rearrange("p (g n b c) -> p g n b c", g=2, n=16, b=8)
                for j in range(2):
                    pos = prm(f"pos{'kv'[v]}")[:, 8 * j:8 * j + 8].unsqueeze(1).to_broadcast([P, NC_CMP, 8])
                    for g in range(2):
                        p.step(dv.tensor_tensor(BLK[:, v, 8 * j:8 * j + 8, 15 * g:15 * g + 15].rearrange("p b n -> p n b"),
                                                src[:, g, j:j + NC_CMP, :, 0], pos, ALU.add),
                               *([f"nsa.blk{v}"] if (j, g) == (1, 1) else []))

            def inverse(key, src, ng, o, rows_=P):
                wait(dv, "act", key + ".sq")
                s = NST[0:rows_, o:o + ng]
                p.step(dv.tensor_reduce(s, src.rearrange("p (h e) -> p h e", h=ng), AXX, ALU.add))
                p.settle()
                p.step(dv.tensor_scalar(s, s, 1.0 / 64, EPS, ALU.mult, ALU.add))
                p.settle()
                p.step(dv.reciprocal(s, s), key + ".inv")
                wait(dv, "act", key + ".rs")
                return s

            for n in range(2):
                for t in range(2):
                    r = inverse(f"nsa.q{n}{t}", NSQ[:, 0, :], 8, 16 * (2 * n + t))
                    p.step(dv.tensor_tensor(NQ[:, t, 512 * n:512 * n + 512].rearrange("p (h e) -> p h e", h=8),
                                            PS[:, 2 * n + t, :].rearrange("p (h e) -> p h e", h=8),
                                            r.unsqueeze(2).to_broadcast([P, 8, 64]), ALU.mult), f"nsa.qn{n}{t}")
            for t in range(2):
                r = inverse(f"nsa.k{t}", NSQ[:, 0, :], 8, 64 + 16 * t).rearrange("p (a j g) -> p a j g", a=2, j=2)
                src = PS[:, 4 + t, :].rearrange("p (a j g e) -> p a j g e", a=2, j=2, g=2)
                for a_ in range(2):
                    for u in range(2):
                        p.step(dv.tensor_tensor(NK[:, t, a_, :, u, :], src[:, a_, 0], r[:, a_, 0].unsqueeze(2).to_broadcast([P, 2, 64]),
                                                ALU.mult))
                p.step(dv.tensor_copy(NV[:, t], src[:, :, 1]), f"nsa.kn{t}")
            wait(dv, "pe", "nsa.gt")
            p.step(dv.tensor_tensor(GTS, PS[:, 6, 0:128].rearrange("p (t n) -> p t n", t=2)[:, :, 0:48],
                                    prm("gate_b").unsqueeze(1).to_broadcast([P, 2, 48]), ALU.add), "nsa.gb")
            for t in range(2):
                for n in range(2):
                    wait(dv, "pe", f"nsa.qtr{n}{t}")
                    p.step(dv.tensor_scalar(NQT[:, 4 * n:4 * n + 4, P * t:P * t + P], PS[:, 2 * t + n, :].rearrange("p (c t) -> p c t", c=4),
                                            prm("nsa_qg"), 0.125, ALU.mult, ALU.mult), f"nsa.qt{n}{t}")
                wait(dv, "pe", f"nsa.ktr{t}")
                for a_ in range(2):
                    p.step(dv.tensor_scalar(NKT[:, 2 * a_:2 * a_ + 2, P * t:P * t + P],
                                            PS[:, 4 + t, 256 * a_:256 * a_ + 256].rearrange("p (c t) -> p c t", c=2),
                                            prm(f"nsa_kg{1 + a_}"), None, ALU.mult), *([f"nsa.kt{t}"] if a_ else []))
            wait(dv, "pe", "nsa.hidtr")
            p.step(dv.tensor_copy(HIDT, PS[:, 7, 0:128].rearrange("p (v n) -> p v n", v=2)[:, :, 0:60].rearrange("p v (c n) -> p v c n", c=2)),
                   "nsa.hidt")
            r = inverse("nsa.kc", NSQ[0:30, 0, 0:64], 1, 96, 30)
            p.step(dv.tensor_scalar(KCN[:, 0:64], PS[0:30, 7, 0:64], r, None, ALU.mult))
            p.step(dv.tensor_scalar(KCN[:, 64:128], PS[0:30, 7, 0:64], r, None, ALU.mult))
            p.step(dv.tensor_copy(VC, PS[0:15, 7, 64:192].rearrange("p (g e) -> p g e", g=2)), "nsa.cmpn")
            wait(dv, "pe", "nsa.kctr")
            for u in range(2):
                r = slice(64 * u, 64 * u + 64)
                p.step(dv.tensor_scalar(KCT[r, :, u, :], PS[r, 7, 0:30].rearrange("p (g n) -> p g n", g=2), prm("nsa_kg0")[r], None, ALU.mult),
                       *(["nsa.kct"] if u else []))
            wait(dv, "pe", "nsa.vrep")
            for g in range(2):
                p.step(dv.tensor_tensor(VB[:, g], PS[0:120, 6, 64 * g:64 * g + 64].unsqueeze(1).to_broadcast([120, 8, 64]),
                                        cst("cmp_own", 120).unsqueeze(2).to_broadcast([120, 8, 64]), ALU.mult),
                       *(["nsa.vb"] if g else []))
            wait(dv, "act", "nsa.gates")
            for t in range(2):
                st = NST[:, 100 + 32 * t:116 + 32 * t]
                gt = GTS[:, t, :].rearrange("p (h j) -> p h j", j=3)
                wait(dv, "pe", f"nsa.cs{t}")
                p.step(dv.tensor_tensor(SC[:, t], PS[:, t, 0:240].rearrange("p (h n) -> p h n", h=16),
                                        cst(f"cmp_add{t}").unsqueeze(1).to_broadcast([P, 16, 15]), ALU.add), f"nsa.sc{t}")
                p.settle()
                p.step(dv.tensor_reduce(st, SC[:, t], AXX, ALU.max))
                p.settle()
                p.step(dv.tensor_tensor(SC[:, t], SC[:, t], st.unsqueeze(2).to_broadcast([P, 16, 15]), ALU.subtract), f"nsa.sub{t}")
                wait(dv, "act", f"nsa.ce{t}")
                p.step(dv.tensor_reduce(st, SC[:, t], AXX, ALU.add))
                p.settle()
                p.step(dv.reciprocal(st, st))
                p.step(dv.tensor_tensor(SC[:, t], SC[:, t], cst(f"cmp_mul{t}").unsqueeze(1).to_broadcast([P, 16, 15]), ALU.mult))
                p.settle()
                p.step(dv.tensor_tensor(st.unsqueeze(2), st.unsqueeze(2), gt[:, :, 0:1], ALU.mult))
                p.settle()
                p.step(dv.tensor_tensor(SC[:, t], SC[:, t], st.unsqueeze(2).to_broadcast([P, 16, 15]), ALU.mult), f"nsa.cp{t}")
            for t in range(2):
                wait(dv, "pe", f"nsa.pctr{t}")
                p.step(dv.tensor_copy(PCT[:, t], PS[0:120, 2 + t, 0:256].rearrange("p (g q) -> p g q", g=2)), f"nsa.pct{t}")
            for t in range(2):
                for g in range(2):
                    wait(dv, "pe", f"nsa.cpv{t}{g}")
                    p.step(dv.tensor_copy(NO[:, t, 512 * g:512 * g + 512], PS[:, 4 + g, :]), f"nsa.oc{t}{g}")
            p.settle()
            n = len(UNITS)
            for u in range(n + 5):
                if u < n:
                    t = UNITS[u][1]
                    wait(dv, "pe", f"nsa.s{u}")
                    if u >= 4:
                        wait(dv, "pe", f"nsa.ptr{u - 4}")
                    p.step(dv.tensor_tensor_reduce(NB[:, u % 4, 0:P * (t + 1)], PS[:, u % 4, 0:P * (t + 1)],
                                                   cst("causal_add")[:, P * (1 - t):256], -1.0, 3e38, ALU.add, ALU.min, NMX[:, u:u + 1]),
                           f"nsa.m{u}")
                v = u - 3
                if 0 <= v < n and v % 2 == 0:
                    t = UNITS[v][1]
                    wait(dv, "pe", f"nsa.ptr{v}")
                    if v >= 2:
                        wait(dv, "pe", f"nsa.pv{v - 2}")
                    p.step(dv.tensor_copy(NPT[:, 0, 0:P * (t + 1)], PS[:, 4, 0:P * (t + 1)]), f"nsa.pt{v}")
                v = u - 5
                if v >= 0 and v % 8 == 7:
                    gi = v // 8
                    a_, t, h = UNITS[v]
                    g = h // 8
                    gs = NGS[:, 8 * (gi % 2):8 * (gi % 2) + 8]
                    gt = GTS[:, t, :].rearrange("p (h j) -> p h j", j=3)[:, 8 * g:8 * g + 8, 1 + a_]
                    wait(dv, "pe", f"nsa.pv{v}")
                    p.step(dv.reciprocal(gs, NSUM[:, 8 * gi:8 * gi + 8]))
                    p.settle()
                    p.step(dv.tensor_tensor(gs, gs, gt, ALU.mult))
                    p.settle()
                    tmp = NTMP.rearrange("p (h e) -> p h e", h=8)
                    p.step(dv.tensor_tensor(tmp, PS[:, 6 + gi % 2, :].rearrange("p (h e) -> p h e", h=8),
                                            gs.unsqueeze(2).to_broadcast([P, 8, 64]), ALU.mult))
                    p.settle()
                    o = NO[:, t, 512 * g:512 * g + 512]
                    p.step(dv.tensor_tensor(o, o, NTMP, ALU.add), f"nsa.acc{gi}")
                    p.settle()
            for t in range(2):
                for n in range(2):
                    wait(dv, "pe", f"nsa.ytr{t}{n}")
                    p.step(dv.tensor_copy(YH[:, 4 * n:4 * n + 4, P * t:P * t + P], PS[:, 2 * t + n, :].rearrange("p (c t) -> p c t", c=4)),
                           f"nsa.yt{t}{n}")
            for n in range(2):
                for t in range(2):
                    wait(dv, "pe", f"nsa.out{n}.t{t}")
                    xr = X[:, t, 512 * n:512 * n + 512]
                    p.step(dv.tensor_tensor(xr, xr, PS[:, 4 + 2 * n + t, :], ALU.add), f"nsa.res{n}{t}")
                    if n and on("ffn1"):
                        norm_scale(dv, p, "n.ffn1", t)


        EA = Z[:, 0:2048].rearrange("p (t n) -> p t n", t=4)
        ECG = Z[:, 2048:4096].rearrange("p (c t) -> p c t", c=4)
        EU = Z[:, 4096:4096 + 2064].rearrange("p (c s t) -> p c s t", c=4, s=2)
        EY = Z[:, 6160:10256].rearrange("p (c t) -> p c t", c=8)
        EFX = Z[:, 10256:11280].rearrange("p (b n) -> p b n", b=2)
        RES = Z[:, 0:1024].rearrange("p (b n) -> p b n", b=2)

        def em_pe(te):
            pe, p = te.eng, te.p
            norm_pe(te, "n.mix0", range(4))
            for t in range(4):
                rows(te, "em.a", t, t, ("act", f"em.a{t}"), last=t == 3)

            def columns(nm, b0, who):
                w = te.weights(f"em.{nm}").rearrange("p (k n) -> p k n", k=8)
                for c in range(4):
                    te.take(b0 + c, who, f"em.{nm}{c}")
                    for k in range(KC):
                        m = pe.matmul(PS[:, b0 + c, :], w[:, k, P * c:P * c + P], HT[:, k, :], start=(k == 0), stop=(k == KC - 1))
                    p.step(m, f"em.{nm}{c}", *([f"em.{nm}.used"] if c == 3 else []))

            columns("c", 4, "act")
            columns("h", 0, "dve")
            columns("b", 4, "dve")
            wait(pe, "act", "em.a3")
            for n in range(9):
                if n < 8:
                    s_, g = n // 4, n % 4
                    te.take(n % 2, "act", f"em.fx{n}")
                    for t2 in range(2):
                        m = pe.matmul(PS[:, n % 2, :], EA[:, 2 * s_ + t2, P * g:P * g + P], cst(f"dft{t2}"), start=t2 == 0, stop=t2 == 1)
                    p.step(m, f"em.f{n}")
                if n >= 1:
                    v = n - 1
                    wait(pe, "act", f"em.fx{v}")
                    te.take(2 + v % 2, "dve", f"em.fy{v}")
                    pe.matmul(PS[:, 2 + v % 2, 0:256], cst("dft_cos"), EFX[:, v % 2, 0:256], start=True, stop=False)
                    p.step(pe.matmul(PS[:, 2 + v % 2, 0:256], cst("dft_nsin"), EFX[:, v % 2, 256:512], start=False, stop=True), f"em.g{v}")
            wait(pe, "dve", "em.fy7")
            wait(pe, "dve", "em.b3")
            for n in range(2):
                for t in range(4):
                    rows(te, f"em.out{n}", t, 4 * n + t, ("dve", f"em.res{n}{t}"), src=EY, last=t == 3)

        def em_act(ac, p, after):
            norm_act(ac, p, "n.mix0", range(4), after)
            for t in range(4):
                wait(ac, "pe", f"em.a.t{t}")
                p.step(ac.activation(EA[:, t, :], PS[:, t, :], ACT.Copy), f"em.a{t}")
            for c in range(4):
                wait(ac, "pe", f"em.c{c}")
                p.step(ac.activation(ECG[:, c, :], PS[:, 4 + c, :], ACT.Copy), f"em.c{c}")
            for n in range(8):
                wait(ac, "pe", f"em.f{n}")
                if n >= 2:
                    wait(ac, "pe", f"em.g{n - 2}")
                p.step(ac.activation(EFX[:, n % 2, :], PS[:, n % 2, :], ACT.Copy), f"em.fx{n}")

        def residual(dv, p, tag, who, src, t, n, gate, key, buf):
            xr = X[:, t, 512 * n:512 * n + 512]
            p.step(dv.tensor_tensor(buf, src, gate[:, 512 * n:512 * n + 512], ALU.mult))
            p.settle()
            p.step(dv.tensor_tensor(xr, xr, buf, ALU.add), key)

        def em_dve(dv, p):
            norm_dve(dv, p, "n.mix0", range(4), lambda t: MODC[:, 0, t // 2, 1, :], lambda t: MODC[:, 0, t // 2, 0, :], scaled=(0, 1))
            w3 = prm("conv2")
            p.step(dv.memset(EU[:, :, :, 0:1], 0.0))
            p.step(dv.memset(EU[:, :, :, 257:258], 0.0))
            for c in range(4):
                wait(dv, "pe", f"em.h{c}")
                wait(dv, "act", f"em.c{c}")
                p.step(dv.tensor_tensor(EU[:, c, :, 1:257], PS[:, c, :].rearrange("p (s t) -> p s t", s=2),
                                        ECG[:, c, :].rearrange("p (s t) -> p s t", s=2), ALU.mult), f"em.h{c}")
            for c in range(4):
                acc = EY[:, 4 + c, :].rearrange("p (s t) -> p s t", s=2)
                p.settle()
                p.step(dv.tensor_scalar(acc, EU[:, c, :, 0:256], w3[:, c:c + 1], None, ALU.mult))
                for j in range(1, 3):
                    p.settle()
                    p.step(dv.scalar_tensor_tensor(out=acc, in0=EU[:, c, :, j:j + 256], scalar=w3[:, 4 * j + c:4 * j + c + 1], in1=acc,
                                                   op0=ALU.mult, op1=ALU.add))
                p.settle()
                wait(dv, "pe", f"em.b{c}")
                p.step(dv.tensor_tensor(EY[:, 4 + c, :], EY[:, 4 + c, :], PS[:, 4 + c, :], ALU.mult), f"em.b{c}")
            for n in range(8):
                s_, g = n // 4, n % 4
                wait(dv, "pe", f"em.g{n}")
                p.step(dv.tensor_copy(EY[:, g, 256 * s_:256 * s_ + 256], PS[:, 2 + n % 2, 0:256]), f"em.fy{n}")
            dv.wait_ge(gate_loaded[0], 32)
            for n in range(2):
                for t in range(4):
                    wait(dv, "pe", f"em.out{n}.t{t}")
                    residual(dv, p, "em", "pe", PS[:, 4 * n + t, :], t, n, GB[:, t // 2, :], f"em.res{n}{t}", RES[:, t % 2, :])
                    if n and t < 2 and on("moe0"):
                        norm_scale(dv, p, "n.moe0", t)
                    p.settle()

        WQ = Z[:, 0:2048].rearrange("p (t n) -> p t n", t=2)
        WO = WQ
        WQT = Z[:, 2048:4096].rearrange("p (c t) -> p c t", c=8)
        WK = Z[:, 4096:6144].rearrange("p (t g u e) -> p t g u e", t=4, g=4, u=2)
        WB = Z[:, 4096:6144].rearrange("p (b n) -> p b n", b=4)
        WV = Z[:, 6144:7168].rearrange("p (t g e) -> p t g e", t=4, g=4)
        WKT = Z[:, 7168:9216].rearrange("p (g t) -> p g t", g=4)
        WSQ = Z[:, 9216:9728]
        WR = Z[:, 9728:10752].rearrange("p (j n) -> p j n", j=4)
        WPT = Z[:, 9216:10240].rearrange("p (b n) -> p b n", b=2)
        WTMP = Z[:, 10240:10752]
        WN = Z[:, 10752:11264]
        WST = Z[:, 11264:11400]
        WMX = Z[:, 11400:11432]
        WSUM = Z[:, 11432:11464]
        WNS = Z[:, 11464:11480]
        WSE = Z[:, 11480:11512]
        WUNITS = [(t, h) for t in range(2) for h in range(16)]

        def at_pe(te):
            pe, p = te.eng, te.p
            norm_pe(te, "n.mix1", range(4))
            for n in range(2):
                for t in range(2):
                    rows(te, f"at.q{n}", t, 2 * n + t, ("dve", f"at.qn{n}{t}"), last=t == 1)
            for t in range(4):
                rows(te, "at.kv", t, 4 + t, ("dve", f"at.kn{t}"), last=t == 3)
            for t in range(2):
                for n in range(2):
                    b = 2 * t + n
                    wait(pe, "dve", f"at.qr{n}{t}")
                    te.take(b, "dve", f"at.qt{n}{t}")
                    for c in range(4):
                        m = pe.transpose(PS[:, b, P * c:P * c + P], WQ[:, t, 512 * n + P * c:512 * n + P * c + P], ident)
                    p.step(m, f"at.qtr{n}{t}")
            for t in range(4):
                wait(pe, "dve", f"at.kr{t}")
                te.take(4 + t, "act", f"at.kt{t}")
                for g in range(4):
                    m = pe.transpose(PS[:, 4 + t, P * g:P * g + P], WK[:, t, g].rearrange("p u e -> p (u e)"), ident)
                p.step(m, f"at.ktr{t}")
            wait(pe, "act", "at.kt3")
            wait(pe, "dve", "at.qt11")
            n = len(WUNITS)
            for u in range(n + 4):
                if u < n:
                    t, h = WUNITS[u]
                    o = 64 * (h % 2)
                    te.take(u % 4, "dve", f"at.m{u}")
                    p.step(pe.matmul(PS[:, u % 4, :], WQT[o:o + 64, h // 2, P * t:P * t + P], WKT[o:o + 64, h // 4, :],
                                     start=True, stop=True), f"at.s{u}")
                if 3 <= u < n + 3:
                    v = u - 3
                    wait(pe, "act", f"at.e{v}")
                    te.take(4 + v % 2, *(("act" if v % 2 else "dve"), f"at.pt{v}"))
                    for c in range(4):
                        m = pe.transpose(PS[:, 4 + v % 2, P * c:P * c + P], WB[:, v % 4, P * c:P * c + P], ident)
                    p.step(m, f"at.ptr{v}")
                if u >= 4:
                    v = u - 4
                    t, h = WUNITS[v]
                    wait(pe, "act" if v % 2 else "dve", f"at.pt{v}")
                    gi = v // 8
                    if v % 8 == 0:
                        te.take(6 + gi % 2, "dve", f"at.acc{gi}")
                    for c in range(4):
                        m = pe.matmul(PS[:, 6 + gi % 2, 64 * (h % 8):64 * (h % 8) + 64], WPT[:, v % 2, P * c:P * c + P],
                                      WV[:, c, h // 4, :], start=(c == 0), stop=(c == 3))
                    p.step(m, f"at.pv{v}")
            for t in range(2):
                wait(pe, "dve", f"at.acc{2 * t + 1}")
                for n in range(2):
                    b = 2 * t + n
                    te.take(b, "dve", f"at.yt{t}{n}")
                    for c in range(4):
                        m = pe.transpose(PS[:, b, P * c:P * c + P], WO[:, t, 512 * n + P * c:512 * n + P * c + P], ident)
                    p.step(m, f"at.ytr{t}{n}")
            wait(pe, "dve", "at.yt11")
            for n in range(2):
                for t in range(2):
                    rows(te, f"at.out{n}", t, 4 + 2 * n + t, ("dve", f"at.res{n}{t}"), src=YH, last=t == 1)

        def at_act(ac, p):

            def squares(bank, key, cols):
                p.settle()
                p.step(ac.activation(WSQ[:, 0:cols], PS[:, bank, 0:cols], ACT.Square), key + ".sq")
                wait(ac, "dve", key + ".inv")

            for n in range(2):
                for t in range(2):
                    wait(ac, "pe", f"at.q{n}.t{t}")
                    squares(2 * n + t, f"at.q{n}{t}", 512)
                    o = 8 * (2 * n + t)
                    p.step(ac.activation(WST[:, o:o + 8], WST[:, o:o + 8], ACT.Sqrt), f"at.q{n}{t}.rs")
            for t in range(4):
                wait(ac, "pe", f"at.kv.t{t}")
                squares(4 + t, f"at.k{t}", 256)
                o = 32 + 4 * t
                p.step(ac.activation(WST[:, o:o + 4], WST[:, o:o + 4], ACT.Sqrt), f"at.k{t}.rs")
            for t in range(4):
                wait(ac, "pe", f"at.ktr{t}")
                p.step(ac.activation(WKT[:, :, P * t:P * t + P], PS[:, 4 + t, :].rearrange("p (g t) -> p g t", g=4), ACT.Copy), f"at.kt{t}")
            for u in range(len(WUNITS) + 1):
                if u < len(WUNITS):
                    wait(ac, "dve", f"at.m{u}")
                    p.step(ac.activation(WB[:, u % 4, :], WB[:, u % 4, :], ACT.Exp, bias=WMX[:, u:u + 1],
                                         scale=-1.0, accum_out=WSUM[:, u:u + 1]), f"at.e{u}")
                    if u % 8 == 7:
                        wait(ac, "dve", f"at.sk{u // 8}")
                        p.step(ac.activation(WSE[:, u - 7:u + 1], WSE[:, u - 7:u + 1], ACT.Exp), f"at.ske{u // 8}")
                v = u - 1
                if v >= 0 and v % 2:
                    wait(ac, "pe", f"at.ptr{v}")
                    p.step(ac.activation(WPT[:, 1, :], PS[:, 5, :], ACT.Copy), f"at.pt{v}")

        def at_dve(dv, p):
            norm_dve(dv, p, "n.mix1", range(4), lambda t: MODC[:, 1, t // 2, 1, :], lambda t: MODC[:, 1, t // 2, 0, :], scaled=range(4))
            p.step(dv.tensor_scalar(WNS, prm("sink2"), -1.0, None, ALU.mult))

            def head_norm(key, src, ng, o, g, free):
                wait(dv, "act", key + ".sq")
                s = WST[:, o:o + ng]
                p.step(dv.tensor_reduce(s, WSQ[:, 0:64 * ng].rearrange("p (h e) -> p h e", h=ng), AXX, ALU.add))
                p.settle()
                p.step(dv.tensor_scalar(s, s, 1.0 / 64, EPS, ALU.mult, ALU.add))
                p.settle()
                p.step(dv.reciprocal(s, s), key + ".inv")
                wait(dv, "act", key + ".rs")
                wn = WN[:, 0:64 * ng].rearrange("p (h e) -> p h e", h=ng)
                p.step(dv.tensor_tensor(wn, src.rearrange("p (h e) -> p h e", h=ng), s.unsqueeze(2).to_broadcast([P, ng, 64]), ALU.mult),
                       *([free] if free else []))
                p.settle()
                p.step(dv.tensor_tensor(wn, wn, g.unsqueeze(1).to_broadcast([P, ng, 64]), ALU.mult))
                p.settle()

            def rotate(t, ng, dsts, key):
                x = WN[:, 0:64 * ng].rearrange("p (h a s e) -> p h a s e", h=ng, a=2, s=2)
                b = lambda c: cst(c).rearrange("p (a e) -> p a e", a=2).unsqueeze(1).to_broadcast([P, ng, 2, 16])
                cs, sn = b(f"axcos{t}"), b(f"axsin{t}")
                tm = [WR[:, j, 0:32 * ng].rearrange("p (h a e) -> p h a e", h=ng, a=2) for j in range(4)]
                p.step(dv.tensor_tensor(tm[0], x[:, :, :, 0, :], cs, ALU.mult))
                p.step(dv.tensor_tensor(tm[1], x[:, :, :, 1, :], sn, ALU.mult))
                p.step(dv.tensor_tensor(tm[2], x[:, :, :, 0, :], sn, ALU.mult))
                p.step(dv.tensor_tensor(tm[3], x[:, :, :, 1, :], cs, ALU.mult))
                p.settle()
                for i, dst in enumerate(dsts):
                    d = dst.rearrange("p h (a s e) -> p h a s e", a=2, s=2)
                    p.step(dv.tensor_tensor(d[:, :, :, 0, :], tm[0], tm[1], ALU.subtract))
                    p.step(dv.tensor_tensor(d[:, :, :, 1, :], tm[2], tm[3], ALU.add), *([key] if i == len(dsts) - 1 else []))
                p.settle()

            for n in range(2):
                for t in range(2):
                    head_norm(f"at.q{n}{t}", PS[:, 2 * n + t, :], 8, 8 * (2 * n + t), prm("qg2"), f"at.qn{n}{t}")
                    rotate(t, 8, [WQ[:, t, 512 * n:512 * n + 512].rearrange("p (h e) -> p h e", h=8)], f"at.qr{n}{t}")
            for t in range(4):
                head_norm(f"at.k{t}", PS[:, 4 + t, 0:256], 4, 32 + 4 * t, prm("kg2"), None)
                p.step(dv.tensor_copy(WV[:, t], PS[:, 4 + t, 256:512].rearrange("p (g e) -> p g e", g=4)), f"at.kn{t}")
                if t < 2:
                    rotate(t, 4, [WK[:, t, :, u, :] for u in range(2)], f"at.kr{t}")
                else:
                    for u in range(2):
                        p.step(dv.tensor_copy(WK[:, t, :, u, :], WN[:, 0:256].rearrange("p (h e) -> p h e", h=4)),
                               *([f"at.kr{t}"] if u else []))
                    p.settle()
            for t in range(2):
                for n in range(2):
                    wait(dv, "pe", f"at.qtr{n}{t}")
                    p.step(dv.tensor_scalar(WQT[:, 4 * n:4 * n + 4, P * t:P * t + P], PS[:, 2 * t + n, :].rearrange("p (c t) -> p c t", c=4),
                                            0.125, None, ALU.mult), f"at.qt{n}{t}")
            wait(dv, "pe", "at.ktr3")
            n = len(WUNITS)
            for u in range(n + 5):
                if u < n:
                    t, h = WUNITS[u]
                    wait(dv, "pe", f"at.s{u}")
                    if u >= 4:
                        wait(dv, "pe", f"at.ptr{u - 4}")
                    p.step(dv.tensor_tensor_reduce(WB[:, u % 4, :], PS[:, u % 4, :], cst(f"band{t}"), -1.0, WNS[:, h:h + 1],
                                                   ALU.add, ALU.min, WMX[:, u:u + 1]), f"at.m{u}")
                    if u % 8 == 7:
                        p.settle()
                        p.step(dv.tensor_tensor(WSE[:, u - 7:u + 1], WMX[:, u - 7:u + 1], prm("sink2")[:, h - 7:h + 1], ALU.add),
                               f"at.sk{u // 8}")
                v = u - 3
                if 0 <= v < n and v % 2 == 0:
                    wait(dv, "pe", f"at.ptr{v}")
                    if v >= 2:
                        wait(dv, "pe", f"at.pv{v - 2}")
                    p.step(dv.tensor_copy(WPT[:, 0, :], PS[:, 4, :]), f"at.pt{v}")
                v = u - 5
                if v >= 0 and v % 8 == 7:
                    gi = v // 8
                    t, h = WUNITS[v]
                    g = h // 8
                    gs = WSUM[:, 8 * gi:8 * gi + 8]
                    wait(dv, "pe", f"at.pv{v}")
                    wait(dv, "act", f"at.ske{gi}")
                    p.step(dv.tensor_tensor(gs, gs, WSE[:, 8 * gi:8 * gi + 8], ALU.add))
                    p.settle()
                    p.step(dv.reciprocal(gs, gs))
                    p.settle()
                    p.step(dv.tensor_tensor(WO[:, t, 512 * g:512 * g + 512].rearrange("p (h e) -> p h e", h=8),
                                            PS[:, 6 + gi % 2, :].rearrange("p (h e) -> p h e", h=8),
                                            gs.unsqueeze(2).to_broadcast([P, 8, 64]), ALU.mult), f"at.acc{gi}")
            for t in range(2):
                for n in range(2):
                    wait(dv, "pe", f"at.ytr{t}{n}")
                    p.step(dv.tensor_copy(YH[:, 4 * n:4 * n + 4, P * t:P * t + P], PS[:, 2 * t + n, :].rearrange("p (c t) -> p c t", c=4)),
                           f"at.yt{t}{n}")
            dv.wait_ge(gate_loaded[2], 32)
            for n in range(2):
                for t in range(2):
                    wait(dv, "pe", f"at.out{n}.t{t}")
                    residual(dv, p, "at", "pe", PS[:, 4 + 2 * n + t, :], t, n, GB[:, 0, :], f"at.res{n}{t}", RES[:, t % 2, :])
                    if n and on("out"):
                        norm_scale(dv, p, "n.moe1", t)
                    p.settle()


        ARENA_SLOT = Z[:, 8192:12288]
        XM = Z[:, 0:4096].rearrange("p (t n) -> p t n", t=4)
        H13 = Z[:, 4096:5120].rearrange("p (b n) -> p b n", b=2)
        HS = Z[:, 5120:5632].rearrange("p (b j r) -> p b j r", b=2, j=4)
        HG = Z[:, 5632:6144].rearrange("p (b j r) -> p b j r", b=2, j=4)
        XT = Z[:, 6144:7168].rearrange("p (b k r) -> p b k r", b=2, k=8)
        YB = Z[:, 7168:8192].rearrange("p (b n) -> p b n", b=2)
        XSF = XS.rearrange("p t d -> p (t d)")
        RB = SM[:, 900:908]
        YG = Z[:, 0:8192].rearrange("p (t k n) -> p t k n", t=4, k=2)

        def ge(eng, s, v):
            if not (isinstance(v, int) and v <= 0):
                eng.wait_ge(s, v)

        class Experts:
            def __init__(self, layer, nt, before, following):
                self.l, self.nt, self.before, self.following = layer, nt, before, following
                L = f"moe{layer}"
                self.L = L
                s = lambda n: sem(f"{L}_{n}")
                self.selected = s("selection_steps")
                self.picked, self.xa = s("rows_picked"), s("rows_copied")
                self.w_loaded = [s(f"weights{i}_loaded") for i in range(6)]
                self.t1, self.m1, self.t2, self.m2 = s("rows_turned"), s("hidden_ready"), s("hidden_turned"), s("block_ready")
                self.xt, self.sl, self.y = s("rows_t_copied"), s("silu_done"), s("block_copied")
                self.h, self.g = s("hidden_copied"), s("gated_done")
                self.y_stored = [s(f"block{b}_stored") for b in range(2)]
                self.gathered = [[s(f"gathered{t}{k}") for k in range(2)] for t in range(nt)]
                self.o_loaded, self.o_stored = s("over_loaded"), s("over_stored")
                self.w = [a[f"w{j}_2"][layer] for j in (1, 3, 2)]
                self.S = XSF[:, 0:2 * CAP * nt].rearrange("p (b t r) -> p b t r", b=2, t=nt)
                self.hit = XSF[:, 512:512 + 2 * CAP * nt].rearrange("p (t k r) -> p t k r", t=nt, k=2)
                self.rb = RB[:, 0:2 * nt].rearrange("p (t k) -> p t k", t=nt)
                self.XA = XSF[:, 1024:1536]
                self.owners = sorted((n for n in before_moe[layer]), key=[n for n, _ in stream].index)
                self.owners.insert(4, None)
                self.slots = [slots[slot_of[n]] if n else ARENA_SLOT for n in self.owners]
                R = Z[:, 7168:8192]
                self.LG = R[:, 0:36 * nt].rearrange("p (t n) -> p t n", t=nt)
                self.OH = R[:, 144:144 + 64 * nt].rearrange("p (t k e) -> p t k e", t=nt, k=2)
                self.CT = R[:, 400:400 + 32 * nt].rearrange("p (t e) -> p t e", t=nt)
                self.RK = R[:, 528:528 + 32 * nt].rearrange("p (t e) -> p t e", t=nt)
                self.CNT, self.EX, self.END, self.STA = [R[:, 656 + 32 * i:688 + 32 * i] for i in range(4)]
                self.TM = SM[:, 256:256 + 64 * nt].rearrange("p (t k e) -> p t k e", t=nt, k=2)
                self.M8 = R[:, 784:784 + 8 * nt].rearrange("p (t n) -> p t n", t=nt)
                self.IF = R[:, 816:816 + 8 * nt].rearrange("p (t n) -> p t n", t=nt)
                q = lambda i, n: SM[:, 512 + 16 * i:512 + 16 * i + n]
                self.gm, self.gv, self.g0, self.tmp = [q(i, nt) for i in range(4)]
                self.GO = q(4, 4 * nt).rearrange("p (t g) -> p t g", t=nt)
                self.G2 = q(5, 4 * nt).rearrange("p (t g) -> p t g", t=nt)
                self.GW = q(6, 2 * nt).rearrange("p (t k) -> p t k", t=nt)
                self.rk, self.qq, self.st, self.sl_, self.ov = [q(i, 2 * nt).rearrange("p (t k) -> p t k", t=nt) for i in range(7, 12)]
                self.EC = SM[0:1, 256:768].rearrange("p (j e) -> p j e", j=16)
                self.EO = R[0:1, 848:868]

            def load_weights(self, sp, e, b, i, first=False):
                for j in range(3):
                    s_ = 3 * b + j
                    if first:
                        if self.owners[s_]:
                            freed(sp, self.owners[s_])
                        else:
                            wait(sp, "dve", self.before)
                    else:
                        ge(sp, self.m1 if j < 2 else self.m2, i - 1)
                    src = self.w[j][bass.ds(e, 1)].rearrange("a (p k) n -> p (a k n)", p=P)
                    sp.dma_start(self.slots[s_], src).then_inc(self.w_loaded[s_], 16)

            def sp(self, sp, tiles):
                for b in range(2):
                    self.load_weights(sp, b, b, b, first=True)
                with sp.Fori(1, NE // 2) as it:
                    for b in range(2):
                        self.load_weights(sp, 2 * it + b, b, 2 * it + b)
                sp.wait_ge(self.m1, NE - 1)
                for name, parts in tiles[:1]:
                    load_tile(sp, name, parts)
                wait(sp, "dve", self.L + ".over")
                n = sp.value_load(OVF[0:1, 16:17], min_val=0, max_val=15)
                sp.wait_ge(self.m2, NE)
                with sp.If(n > 0):
                    with sp.Fori(0, n) as j:
                        sp.wait_ge(self.m2, NE + j)
                        e = sp.value_load(OVF[0:1, bass.ds(j, 1)], min_val=0, max_val=NE - 1)
                        for k in range(3):
                            src = self.w[k][bass.ds(e, 1)].rearrange("a (p k) n -> p (a k n)", p=P)
                            sp.dma_start(self.slots[3 + k], src).then_inc(self.o_loaded, 16)
                with sp.Else():
                    pass
                sp.wait_ge(self.m2, NE + n)
                for g in self.gathered:
                    for k in range(2):
                        sp.wait_ge(g[k], 16)
                for name, parts in tiles[1:]:
                    load_tile(sp, name, parts)

            def pick_rows(self, pe, b, done):
                for t in range(self.nt):
                    for h in range(2):
                        m = pe.matmul(PS[64 * h:64 * h + 64, 0, :], self.S[:, b, t, :], XM[:, t, 512 * h:512 * h + 512],
                                      start=t == 0, stop=t == self.nt - 1)
                m.then_inc(done, 1)

            def turn_rows(self, pe, done):
                for j in range(4):
                    m = pe.transpose(PS[:, 1, P * j:P * j + P], self.XA[:, P * j:P * j + P], ident)
                m.then_inc(done, 1)

            def hidden(self, pe, b, done, s0=None):
                s0 = 3 * b if s0 is None else s0
                w1, w3 = [self.slots[s0 + j].rearrange("p (k n) -> p k n", k=8) for j in range(2)]
                for k in range(KC):
                    pe.matmul(PS[0:64, 2 + b, :], XT[:, b, k, :], w1[:, k, :], start=k == 0, stop=k == KC - 1)
                    m = pe.matmul(PS[64:128, 2 + b, :], XT[:, b, k, :], w3[:, k, :], start=k == 0, stop=k == KC - 1)
                m.then_inc(done, 1)

            def turn_hidden(self, pe, b, done):
                for j in range(4):
                    m = pe.transpose(PS[:, 4 + b, P * j:P * j + P], H13[:, b, j::4], ident)
                m.then_inc(done, 1)

            def down(self, pe, b, done, s0=None):
                w2 = self.slots[(3 * b if s0 is None else s0) + 2].rearrange("p (j n) -> p j n", j=4)
                for j in range(4):
                    pe.matmul(PS[0:64, 6 + b, :], HG[:, b, j, :], w2[:, j, 0:512], start=j == 0, stop=j == 3)
                    m = pe.matmul(PS[64:128, 6 + b, :], HG[:, b, j, :], w2[:, j, 512:1024], start=j == 0, stop=j == 3)
                m.then_inc(done, 1)

            def pe_pick(self, pe, b, i):
                pe.wait_ge(self.selected, 3 * i + 3)
                ge(pe, self.xa, i)
                self.pick_rows(pe, b, self.picked)

            def pe_rows(self, pe, i):
                pe.wait_ge(self.xa, i + 1)
                ge(pe, self.xt, i)
                self.turn_rows(pe, self.t1)

            def pe_down(self, pe, it, b):
                i = 2 * it + b
                pe.wait_ge(self.w_loaded[3 * b + 2], 16 * it + 16)
                pe.wait_ge(self.g, i + 1)
                ge(pe, self.y, i - 1)
                self.down(pe, b, self.m2)

            def pe_block(self, pe, it, b, left=2):
                i = 2 * it + b
                for j in range(2):
                    pe.wait_ge(self.w_loaded[3 * b + j], 16 * it + 16)
                pe.wait_ge(self.xt, i + 1)
                ge(pe, self.h, i - 1)
                self.hidden(pe, b, self.m1)
                if left > 0:
                    self.pe_rows(pe, i + 1)
                if not (isinstance(i, int) and i == 0):
                    self.pe_down(pe, it - 1 + b, 1 - b)
                pe.wait_ge(self.h, i + 1)
                ge(pe, self.g, i - 1)
                self.turn_hidden(pe, b, self.t2)
                if left > 1:
                    self.pe_pick(pe, b, i + 2)

            def pe(self, te):
                pe, p, L = te.eng, te.p, self.L
                norm_pe(te, f"n.{L}", range(self.nt))
                for t in range(self.nt):
                    wait(pe, "dve", f"n.{L}.ht{t}")
                    for hf in range(2):
                        b = 2 * (t % 2) + hf
                        te.take(b, "act", f"{L}.xm{t}{hf}")
                        for j in range(4):
                            m = pe.transpose(PS[:, b, P * j:P * j + P], HT[:, 4 * hf + j, P * t:P * t + P], ident)
                        p.step(m, f"{L}.xmt{t}{hf}")
                for t in range(self.nt):
                    rows(te, f"{L}.r", t, 4 + t, ("dve", f"{L}.lg{t}"), n=36, last=t == self.nt - 1)
                wait(pe, "dve", f"{L}.ct")
                te.take(0, "dve", f"{L}.rk")
                for t in range(self.nt):
                    for u in range(t + 1):
                        pe.matmul(PS[:, 0, 32 * t:32 * t + 32], cst("before") if u == t else cst("ones")[:, 0:P], self.CT[:, u, :],
                                  start=u == 0, stop=u == t)
                for t in range(self.nt):
                    m = pe.matmul(PS[:, 0, 128:160], cst("ones")[:, 0:P], self.CT[:, t, :], start=t == 0, stop=t == self.nt - 1)
                p.step(m, f"{L}.rank")
                for who in te.banks.values():
                    wait(pe, *who)
                te.banks = {}
                self.pe_pick(pe, 0, 0)
                self.pe_rows(pe, 0)
                self.pe_pick(pe, 1, 1)
                for b in range(2):
                    self.pe_block(pe, 0, b)
                with pe.Fori(1, NE // 2 - 1) as it:
                    for b in range(2):
                        self.pe_block(pe, it, b)
                for b in range(2):
                    self.pe_block(pe, NE // 2 - 1, b, left=1 - b)
                self.pe_down(pe, NE // 2 - 1, 1)
                for s in (self.xt, self.h, self.g, self.y):
                    pe.wait_ge(s, NE)
                wait(pe, "dve", L + ".over")
                n = pe.value_load(OVF[0:1, 16:17], min_val=0, max_val=15)
                with pe.If(n > 0):
                    with pe.Fori(0, n) as j:
                        pe.wait_ge(self.y, NE + j)
                        pe.wait_ge(self.selected, 3 * NE + 3 * j + 3)
                        self.pick_rows(pe, 0, self.picked)
                        pe.wait_ge(self.xa, NE + j + 1)
                        self.turn_rows(pe, self.t1)
                        pe.wait_ge(self.o_loaded, 48 * j + 48)
                        pe.wait_ge(self.xt, NE + j + 1)
                        self.hidden(pe, 0, self.m1, s0=3)
                        pe.wait_ge(self.h, NE + j + 1)
                        self.turn_hidden(pe, 0, self.t2)
                        pe.wait_ge(self.g, NE + j + 1)
                        self.down(pe, 0, self.m2, s0=3)
                with pe.Else():
                    pass
                pe.wait_ge(self.y, NE + n)

            def copy_rows(self, ac, b, done):
                ac.activation(XT[:, b].rearrange("p (h j) r -> p j h r", h=2), PS[:, 1, :].rearrange("p (j h r) -> p j h r", j=4, h=2),
                              ACT.Copy).then_inc(done, 1)

            def silu(self, ac, b, done):
                ac.activation(HS[:, b], PS[:, 4 + b, :].rearrange("p (j r) -> p j r", j=4)[:, :, 0:64], ACT.Silu).then_inc(done, 1)

            def store(self, ac, b, row, stored):
                for hf in range(2):
                    ac.dma_start(yb_dram[bass.ds(row, CAP), 512 * hf:512 * hf + 512], YB[64 * hf:64 * hf + 64, b, :]).then_inc(stored, 16)

            def act_picked(self, ac, i):
                ac.wait_ge(self.picked, i + 1)
                ge(ac, self.t1, i)
                ac.activation(self.XA, PS[:, 0, :], ACT.Copy).then_inc(self.xa, 1)

            def act_rows(self, ac, b, i):
                ac.wait_ge(self.t1, i + 1)
                ge(ac, self.m1, i - 1)
                self.copy_rows(ac, b, self.xt)

            def act_out(self, ac, it, b):
                i = 2 * it + b
                ac.wait_ge(self.m2, i + 1)
                ge(ac, self.y_stored[b], 32 * it)
                ac.activation(YB[:, b, :], PS[:, 6 + b, :], ACT.Copy).then_inc(self.y, 1)
                ac.wait_ge(self.y, i + 1)
                self.store(ac, b, CAP * i, self.y_stored[b])

            def act_block(self, ac, it, b, left=2):
                i = 2 * it + b
                if left > 0:
                    self.act_rows(ac, 1 - b, i + 1)
                if not (isinstance(i, int) and i == 0):
                    self.act_out(ac, it - 1 + b, 1 - b)
                ac.wait_ge(self.t2, i + 1)
                ge(ac, self.g, i - 1)
                self.silu(ac, b, self.sl)
                if left > 1:
                    self.act_picked(ac, i + 2)

            def act(self, ac, p, after):
                L = self.L
                norm_act(ac, p, f"n.{L}", range(self.nt), after)
                for t in range(self.nt):
                    for hf in range(2):
                        wait(ac, "pe", f"{L}.xmt{t}{hf}")
                        p.step(ac.activation(XM[:, t, 512 * hf:512 * hf + 512], PS[:, 2 * (t % 2) + hf, :], ACT.Copy), f"{L}.xm{t}{hf}")
                wait(ac, "dve", f"{L}.gsub")
                p.step(ac.activation(self.G2, self.G2, ACT.Exp), f"{L}.gexp")
                wait(ac, "dve", f"{L}.d")
                p.step(ac.activation(self.g0, self.g0, ACT.Exp), f"{L}.dexp")
                self.act_picked(ac, 0)
                self.act_rows(ac, 0, 0)
                self.act_picked(ac, 1)
                for b in range(2):
                    self.act_block(ac, 0, b)
                with ac.Fori(1, NE // 2 - 1) as it:
                    for b in range(2):
                        self.act_block(ac, it, b)
                for b in range(2):
                    self.act_block(ac, NE // 2 - 1, b, left=1 - b)
                self.act_out(ac, NE // 2 - 1, 1)
                for b in range(2):
                    ac.wait_ge(self.y_stored[b], 32 * (NE // 2))
                wait(ac, "dve", L + ".over")
                n = ac.value_load(OVF[0:1, 16:17], min_val=0, max_val=15)
                with ac.If(n > 0):
                    with ac.Fori(0, n) as j:
                        self.act_picked(ac, NE + j)
                        ac.wait_ge(self.t1, NE + j + 1)
                        self.copy_rows(ac, 0, self.xt)
                        ac.wait_ge(self.t2, NE + j + 1)
                        self.silu(ac, 0, self.sl)
                        ac.wait_ge(self.m2, NE + j + 1)
                        ac.activation(YB[:, 0, :], PS[:, 6, :], ACT.Copy).then_inc(self.y, 1)
                        ac.wait_ge(self.y, NE + j + 1)
                        self.store(ac, 0, CAP * NE + CAP * j, self.o_stored)
                        ac.wait_ge(self.o_stored, 32 * j + 32)
                with ac.Else():
                    pass
                p.step(ac.activation(SM[0:1, 830:831], cst("ones", 1)[:, 0:1], ACT.Copy), f"{L}.stored")
                norm_table(ac, p)
                for t in range(self.nt + 1):
                    if t < self.nt:
                        ac.wait_ge(self.gathered[t][0], 16)
                        y0 = YG[:, t, 0, :]
                        p.step(ac.activation(y0, y0, ACT.Copy, scale=GWK[:, 2 * t:2 * t + 1]), f"{L}.y0{t}")
                    if t >= 1 and self.following:
                        wait(ac, "dve", f"{L}.x{t - 1}")
                        norm_act_tile(ac, p, self.following, t - 1)

            def select(self, dv, b, i, free):
                if not (isinstance(i, int) and i == 0):
                    dv.wait_ge(self.selected, 3 * i)
                ge(dv, self.picked, free)
                ids = cst("iota").unsqueeze(1).unsqueeze(1).to_broadcast([P, self.nt, 2, CAP])
                dv.tensor_tensor(self.hit, self.rb.unsqueeze(3).to_broadcast([P, self.nt, 2, CAP]), ids, ALU.is_equal)\
                    .then_inc(self.selected, 1)
                dv.wait_ge(self.selected, 3 * i + 1)
                dv.tensor_tensor(self.S[:, b], self.hit[:, :, 0, :], self.hit[:, :, 1, :], ALU.add).then_inc(self.selected, 1)
                dv.tensor_scalar(self.rb, self.rb, -float(CAP), None, ALU.add).then_inc(self.selected, 1)

            def dve_block(self, dv, it, b, last=False):
                i = 2 * it + b
                if not last:
                    self.select(dv, b, i + 2, i + 1)
                dv.wait_ge(self.m1, i + 1)
                ge(dv, self.t2, i - 1)
                dv.tensor_copy(H13[:, b, :], PS[:, 2 + b, :]).then_inc(self.h, 1)
                dv.wait_ge(self.sl, i + 1)
                ge(dv, self.m2, i - 1)
                self.gate(dv, b, self.g)

            def gate(self, dv, b, done):
                dv.tensor_tensor(HG[:, b], HS[:, b], PS[:, 4 + b, :].rearrange("p (j r) -> p j r", j=4)[:, :, 64:128], ALU.mult)\
                    .then_inc(done, 1)

            def dve(self, dv, p):
                L, nt, l = self.L, self.nt, self.l
                norm_dve(dv, p, f"n.{L}", range(nt), lambda t: MODC[:, l, t // 2, 4, :], lambda t: MODC[:, l, t // 2, 3, :], scaled=(0, 1))
                p.settle()

                def do(instr, *key):
                    p.step(instr, *key)
                    p.settle()

                iota = cst("iota")[:, 0:NE]
                bc = lambda v, n: v.unsqueeze(2).to_broadcast([P, v.shape[1], n])
                for t in range(nt):
                    wait(dv, "pe", f"{L}.r.t{t}")
                    p.step(dv.tensor_tensor(self.LG[:, t], PS[:, 4 + t, 0:36], prm(f"b_rt{l}"), ALU.add), f"{L}.lg{t}")
                p.settle()
                gl, el = self.LG[:, :, 0:4], self.LG[:, :, 4:36]
                i4 = iota[:, 0:4].unsqueeze(1).to_broadcast([P, nt, 4])
                do(dv.tensor_reduce(self.gm, gl, AXX, ALU.max))
                do(dv.tensor_tensor(self.G2, gl, bc(self.gm, 4), ALU.subtract), f"{L}.gsub")
                do(dv.tensor_tensor(self.GO, gl, bc(self.gm, 4), ALU.is_equal))
                do(dv.tensor_scalar(self.GO, self.GO, -64.0, None, ALU.mult))
                do(dv.tensor_tensor(self.GO, self.GO, i4, ALU.add))
                do(dv.tensor_reduce(self.gm, self.GO, AXX, ALU.min))
                do(dv.tensor_tensor(self.GO, self.GO, bc(self.gm, 4), ALU.is_equal))
                do(dv.tensor_scalar(self.GO, self.GO, 1e30, -1e30, ALU.mult, ALU.add))
                e4 = el.rearrange("p t (g e) -> p t g e", g=4)
                do(dv.tensor_tensor(e4, e4, self.GO.unsqueeze(3).to_broadcast([P, nt, 4, 8]), ALU.add))
                for t in range(nt):
                    p.step(dv.max(self.M8[:, t], el[:, t]))
                p.settle()
                for t in range(nt):
                    p.step(dv.max_index(EIDX[:, 8 * t:8 * t + 8], self.M8[:, t], el[:, t]))
                p.settle()
                p.step(dv.tensor_copy(self.IF, EIDX[:, 0:8 * nt].rearrange("p (t n) -> p t n", t=nt)))
                do(dv.tensor_tensor(self.g0.unsqueeze(2), self.M8[:, :, 1:2], self.M8[:, :, 0:1], ALU.subtract), f"{L}.d")
                do(dv.tensor_tensor(self.OH, self.IF[:, :, 0:2].unsqueeze(3).to_broadcast([P, nt, 2, NE]),
                                    iota.unsqueeze(1).unsqueeze(1).to_broadcast([P, nt, 2, NE]), ALU.is_equal))
                do(dv.tensor_tensor(self.CT, self.OH[:, :, 0, :], self.OH[:, :, 1, :], ALU.add), f"{L}.ct")
                wait(dv, "act", f"{L}.gexp")
                do(dv.tensor_reduce(self.gv, self.G2, AXX, ALU.add))
                do(dv.reciprocal(self.gv, self.gv))
                wait(dv, "act", f"{L}.dexp")
                do(dv.tensor_scalar(self.tmp, self.g0, 1.0, None, ALU.add))
                do(dv.reciprocal(self.tmp, self.tmp))
                do(dv.tensor_tensor(self.tmp, self.tmp, self.gv, ALU.mult))
                do(dv.tensor_copy(self.GW[:, :, 0:1], self.tmp.unsqueeze(2)))
                do(dv.tensor_tensor(self.GW[:, :, 1:2], self.tmp.unsqueeze(2), self.g0.unsqueeze(2), ALU.mult))
                wait(dv, "pe", f"{L}.rank")
                p.step(dv.tensor_copy(self.RK, PS[:, 0, 0:32 * nt].rearrange("p (t e) -> p t e", t=nt)))
                do(dv.tensor_copy(self.CNT, PS[:, 0, 128:160]), f"{L}.rk")
                BIG = 1.5 * 2 ** 23
                c_if = self.IF[:, :, 0:2]
                per_choice = lambda table_: table_.to_broadcast([P, nt, 2, NE])
                p.step(dv.tensor_scalar(self.EX, self.CNT, -1.0 - (CAP - 1) / 2, 1.0 / CAP, ALU.add, ALU.mult))
                do(dv.tensor_tensor(self.TM, self.OH, per_choice(self.RK.unsqueeze(2)), ALU.mult))
                p.step(dv.tensor_scalar(self.EX, self.EX, BIG, None, ALU.add))
                do(dv.tensor_reduce(self.rk, self.TM, AXX, ALU.add))
                p.step(dv.tensor_scalar(self.EX, self.EX, -BIG, 0.0, ALU.add, ALU.max))
                do(dv.tensor_scalar(self.qq, self.rk, -(CAP - 1) / 2, 1.0 / CAP, ALU.add, ALU.mult))
                p.step(dv.tensor_tensor_scan(self.END, cst("ones")[:, 0:32], self.EX, 0.0, ALU.mult, ALU.add))
                do(dv.tensor_scalar(self.qq, self.qq, BIG, None, ALU.add))
                p.step(dv.tensor_tensor(self.STA, self.END, self.EX, ALU.subtract))
                do(dv.tensor_scalar(self.qq, self.qq, -BIG, None, ALU.add))
                p.step(dv.tensor_tensor(self.TM, self.OH, per_choice(self.STA.unsqueeze(1).unsqueeze(1)), ALU.mult))
                p.step(dv.scalar_tensor_tensor(out=self.rk, in0=self.qq, scalar=-float(CAP), in1=self.rk, op0=ALU.mult, op1=ALU.add))
                p.step(dv.scalar_tensor_tensor(out=self.sl_, in0=self.qq, scalar=float(NE - 1), in1=c_if, op0=ALU.add, op1=ALU.subtract))
                do(dv.tensor_scalar(self.ov, self.qq, 1.0, None, ALU.min))
                do(dv.tensor_reduce(self.st, self.TM, AXX, ALU.add))
                do(dv.tensor_tensor(self.st, self.st, self.sl_, ALU.add))
                do(dv.tensor_tensor(self.st, self.st, self.ov, ALU.mult))
                do(dv.tensor_tensor(self.st, self.st, c_if, ALU.add))
                p.step(dv.scalar_tensor_tensor(out=self.rb, in0=self.st, scalar=float(CAP), in1=self.rk, op0=ALU.mult, op1=ALU.add))
                do(dv.scalar_tensor_tensor(out=self.sl_, in0=self.st, scalar=float(CAP), in1=self.rk, op0=ALU.mult, op1=ALU.add))
                for b in range(2):
                    self.select(dv, b, b, 0)
                do(dv.tensor_copy(ROWS[:, 0:2 * nt].rearrange("p (t k) -> p t k", t=nt), self.sl_), f"{L}.rows")
                do(dv.tensor_copy(self.EO[:, 16:17], self.END[0:1, 31:32]))
                do(dv.tensor_copy(GWK[:, 0:2 * nt].rearrange("p (t k) -> p t k", t=nt), self.GW))
                do(dv.tensor_tensor(self.EC, self.END[0:1].unsqueeze(1).to_broadcast([1, 16, 32]),
                                    iota[0:1, 0:16].unsqueeze(2).to_broadcast([1, 16, 32]), ALU.is_le))
                do(dv.tensor_reduce(self.EO[:, 0:16], self.EC, AXX, ALU.add))
                do(dv.tensor_scalar(self.EO[:, 0:16], self.EO[:, 0:16], float(NE - 1), None, ALU.min))
                do(dv.tensor_copy(OVF[0:1, 0:17], self.EO[:, 0:17]), L + ".over")
                for b in range(2):
                    self.dve_block(dv, 0, b)
                with dv.Fori(1, NE // 2 - 1) as it:
                    for b in range(2):
                        self.dve_block(dv, it, b)
                for b in range(2):
                    self.dve_block(dv, NE // 2 - 1, b, last=True)
                n = dv.value_load(OVF[0:1, 16:17], min_val=0, max_val=15)
                with dv.If(n > 0):
                    with dv.Fori(0, n) as j:
                        self.select(dv, 0, NE + j, NE + j)
                        dv.wait_ge(self.m1, NE + j + 1)
                        dv.tensor_copy(H13[:, 0, :], PS[:, 2, :]).then_inc(self.h, 1)
                        dv.wait_ge(self.sl, NE + j + 1)
                        self.gate(dv, 0, self.g)
                with dv.Else():
                    pass
                dv.wait_ge(gate_loaded[1 + 2 * l], 32)
                for t in range(nt + 1):
                    if t < nt:
                        y0, y1 = YG[:, t, 0, :], YG[:, t, 1, :]
                        dv.wait_ge(self.gathered[t][1], 16)
                        wait(dv, "act", f"{L}.y0{t}")
                        do(dv.scalar_tensor_tensor(out=y0, in0=y1, scalar=GWK[:, 2 * t + 1:2 * t + 2], in1=y0, op0=ALU.mult, op1=ALU.add))
                        do(dv.tensor_tensor(y0, y0, GB[:, t // 2, :], ALU.mult))
                        p.step(dv.tensor_tensor(X[:, t, :], X[:, t, :], y0, ALU.add), f"{L}.x{t}", *([L + ".end"] if t == nt - 1 else []))
                    if t >= 1 and self.following:
                        norm_scale(dv, p, self.following, t - 1)

            def pool(self, po):
                L = self.L
                wait(po, "dve", f"{L}.rows")
                if self.l == 0:
                    po.wait_ge(zeroed, 16 * 4)
                wait(po, "act", f"{L}.stored")
                for t in range(self.nt):
                    for k in range(2):
                        po.indirect_dma_start(YG[:, t, k, :], None, yb_dram[:, :],
                                              bass.IndirectOffsetOnAxis(ap=ROWS[:, 2 * t + k:2 * t + k + 1], axis=0))\
                            .then_inc(self.gathered[t][k], 16)

        moe = [Experts(0, 4, "em.res13", "n.mix1" if on("at") else None), Experts(1, 2, "at.res11", None)] if on("moe0") else None

        def moe_zero_fill(po):
            po.memset(ZERO, 0.0).then_inc(zero_set, 1)
            po.wait_ge(zero_set, 1)
            pieces = [yb_dram[NE * CAP + 256 * q:][0:256] for q in range(4)]
            for q, rows_ in enumerate(pieces):
                wait(po, "pe", f"nsa.s{8 * q}")
                po.dma_start(rows_.rearrange("(p n) (h c) -> p (n h) c", p=P, h=16), ZERO.unsqueeze(1).to_broadcast([P, 32, 64]))\
                    .then_inc(zeroed, 16)

        def gate_rows(po, j, layer, v):
            for r in range(2):
                po.dma_start(GB[:, r, :], mod_dram[layer, r:r + 1, D * v:D * v + D].to_broadcast([P, D])).then_inc(gate_loaded[j], 16)

        @block.sync
        def _(sp):
            sp.dma_start(X[:, 0:2, :], a["x"].rearrange("o (t p) d -> p (o t) d", p=P)).then_inc(x_loaded, 16)
            sp.dma_start(CST[:, 0:P + 1], a["consts"][:, 0:P + 1]).then_inc(ident_loaded, 16)
            sp.dma_start(PRM[:, :], a["params"]).then_inc(params_loaded, 16)
            for i_, (name, parts) in enumerate(stream[:moe_at[0]]):
                load_tile(sp, name, parts)
                if i_ == 1:
                    sp.dma_start(CST[:, P + 1:], a["consts"][:, P + 1:]).then_inc(consts_loaded, 16)
                if i_ == 8:
                    sp.dma_start(X[:, 2:4, :], a["ctx_2"].rearrange("o (t p) d -> p (o t) d", p=P)).then_inc(ctx_loaded, 16)
            if on("moe0"):
                moe[0].sp(sp, stream[moe_at[0]:moe_at[1]])
            if on("out"):
                moe[1].sp(sp, [])
            for t in range(2):
                wait(sp, "dve", f"moe1.x{t}" if on("out") else "end")
                sp.dma_start(out[0, P * t:P * t + P, :], X[:, t, :]).then_inc(out_sem, 16)
            sp.wait_ge(out_sem, 32)

        @block.gpsimd
        def _(po):
            p = Progress("pool", sems["pool"], po, table)
            for i in range(2):
                po.dma_start(GB[:, i, :], a["ple_norm_g"][i:i + 1, :].to_broadcast([P, D])).then_inc(emb_sem[i], 16)
            if on("mod"):
                mod_columns_pool(po, 0)
                if on("moe0"):
                    moe_zero_fill(po)
                mod_columns_pool(po, 1)
                for i in range(2):
                    po.wait_ge(gates_written[i], 16 * 4)
                wait(po, "dve", "ple1.res11")
                gate_rows(po, 0, 0, 2)
            if on("moe0"):
                wait(po, "dve", "em.res13")
                gate_rows(po, 1, 0, 5)
                moe[0].pool(po)
            if on("at"):
                wait(po, "dve", "moe0.end")
                gate_rows(po, 2, 1, 2)
            if on("out"):
                wait(po, "dve", "at.res11")
                gate_rows(po, 3, 1, 5)
                moe[1].pool(po)

        @block.scalar
        def _(ac):
            p = Progress("act", sems["act"], ac, table)
            ac.wait_ge(x_loaded, 16)
            ac.wait_ge(ident_loaded, 16)
            ab_act(ac, p)
            p.step(ac.activation(CSILU[:, :].rearrange("p (r k) -> p k r", r=2), prm("cvec").rearrange("p (k r) -> p k r", k=8), ACT.Silu), "mod.silu")
            if on("ffn0"):
                ffn_act(ac, p, 0, lambda t: f"ab.res1{t}")
            if on("ple0"):
                ple_act(ac, p, 0, lambda t: f"ffn0.res1{t}")
            if on("nsa"):
                nsa_act(ac, p, lambda t: f"ple0.res1{t}")
            if on("ffn1"):
                ffn_act(ac, p, 1, lambda t: f"nsa.res1{t}")
            if on("ple1"):
                ple_act(ac, p, 1, lambda t: f"ffn1.res1{t}")
            if on("em"):
                ac.wait_ge(ctx_loaded, 16)
                em_act(ac, p, lambda t: f"ple1.res1{t}" if t < 2 else None)
            if on("moe0"):
                moe[0].act(ac, p, lambda t: f"em.res1{t}")
            if on("at"):
                at_act(ac, p)
            if on("out"):
                moe[1].act(ac, p, lambda t: f"at.res1{t}")

        @block.vector
        def _(dv):
            p = Progress("dve", sems["dve"], dv, table)
            dv.wait_ge(x_loaded, 16)
            dv.wait_ge(params_loaded, 16)
            ab_dve(dv, p)
            p.settle()
            if on("ffn0"):
                ffn_dve(dv, p, 0)
                p.settle()
            if on("ple0"):
                ple_dve(dv, p, 0)
                if on("mod"):
                    mod_columns_dve(dv, p, 0)
                p.settle()
            if on("nsa"):
                nsa_dve(dv, p)
                p.settle()
            if on("ffn1"):
                ffn_dve(dv, p, 1)
                p.settle()
            if on("ple1"):
                ple_dve(dv, p, 1)
                if on("mod"):
                    mod_columns_dve(dv, p, 1)
                p.settle()
            if on("em"):
                dv.wait_ge(ctx_loaded, 16)
                em_dve(dv, p)
            if on("moe0"):
                moe[0].dve(dv, p)
            if on("at"):
                at_dve(dv, p)
            if on("out"):
                moe[1].dve(dv, p)
            p.step(dv.memset(SM[0:1, 822:822 + 1], 0.0), "end")

        @block.tensor
        def _(pe):
            te = Tensor(pe)
            pe.wait_ge(ident_loaded, 16)
            ab_pe(te)
            if on("ffn0"):
                ffn_pe(te, 0)
            if on("ple0"):
                ple_pe(te, 0)
            if on("nsa"):
                nsa_pe(te)
            if on("ffn1"):
                ffn_pe(te, 1)
            if on("ple1"):
                ple_pe(te, 1)
            if on("em"):
                em_pe(te)
            if on("moe0"):
                moe[0].pe(te)
            if on("at"):
                at_pe(te)
            if on("out"):
                moe[1].pe(te)


_INS = None


def kernel(**inputs):
    import concourse.bacc as _bacc
    from concourse.bass_utils import run_bass_kernel_spmd as _run

    table = {}
    params, param_at = param_table(inputs)
    for _ in range(2):
        nc = _bacc.Bacc("TRN2", target_bir_lowering=False, num_devices=1)
        arrays, aps = {}, {}
        for name, v in {**inputs, "consts": CONST, "params": params}.items():
            v = np.ascontiguousarray(v)
            arrays[f"in_{name}"] = v
            aps[name] = nc.dram_tensor(f"in_{name}", v.shape, mybir.dt.from_np(v.dtype), kind="ExternalInput").ap()
        out = nc.dram_tensor("out_0", (1, T, D), F32, kind="ExternalOutput").ap()
        build_program(nc, aps, out, table, param_at)
    r = _run(nc, [arrays], core_ids=[0])
    return r.results[0]["out_0"]
```
